# Optimizing a Trainium2 kernel written in Bass

```python
import jax
import jax.numpy as jnp
from jax import lax
import numpy as np

D_MODEL = 1024
BATCH = 1
SEQ = 256
DEPTH = 2

GRID_W = 64
CTX_LEN = 256
HEAD_DIM = 64
N_NA_HEADS = 8
N_HG_HEADS = 8
NA_WIDTH = N_NA_HEADS * HEAD_DIM
HG_WIDTH = N_HG_HEADS * HEAD_DIM
N_EVEN_PARTS = 8
EVEN_IN_WIDTH = 3 * NA_WIDTH + 5 * HG_WIDTH
MIX_WIDTH = NA_WIDTH + HG_WIDTH
NA_WIN_ROWS = 8
NA_WIN_COLS = 16
HG_CHUNK = 64
FORGET_FLOOR = 1e-30
LRU_WIDTH = D_MODEL
LRU_BLOCKS = 16
LRU_BLOCK_DIM = LRU_WIDTH // LRU_BLOCKS
LRU_C = 8.0
CONV_W = 4
CONV_PAD_LEFT = 2
N_EXPERTS = 64
TOP_K = 6
EXPERT_HIDDEN = 256
SHARED_HIDDEN = 256
ROUTED_SCALE = 2.5
MOE_BLOCK = 128
N_EVEN = (DEPTH + 1) // 2
N_ODD = DEPTH // 2
DEEPNORM_ALPHA = (2 * DEPTH) ** 0.25
DEEPNORM_BETA = (8 * DEPTH) ** -0.25
LN_EPS = 1e-5
RMS_EPS = 1e-6

kernel_name = 'hybrid_na_hgrn2_rglru_moe_diffusion_trunk'

def layer_norm(x, g, b):
    x32 = x.astype(jnp.float32)
    mu = jnp.mean(x32, axis=-1, keepdims=True)
    var = jnp.mean(jnp.square(x32 - mu), axis=-1, keepdims=True)
    y = (x32 - mu) * lax.rsqrt(var + LN_EPS)
    return (y * g.astype(jnp.float32) + b.astype(jnp.float32)).astype(x.dtype)

def to_heads(t):
    b, n, _ = t.shape
    return t.reshape(b, n, -1, HEAD_DIM).transpose(0, 2, 1, 3)

def from_heads(t):
    b, h, n, d = t.shape
    return t.transpose(0, 2, 1, 3).reshape(b, n, h * d)

def neighbourhood_attention(q, k, v, k_ctx, v_ctx, rpb):
    b, h, n, dh = q.shape
    rows = n // GRID_W
    kr = min(NA_WIN_ROWS, rows)
    kc = NA_WIN_COLS
    q = q.reshape(b, h, rows, GRID_W, dh)
    k = k.reshape(b, h, rows, GRID_W, dh)
    v = v.reshape(b, h, rows, GRID_W, dh)
    col = jnp.arange(GRID_W)
    col_idx = jnp.clip(col - kc // 2, 0, GRID_W - kc)[:, None] + jnp.arange(kc)[None, :]
    col_bias_idx = col_idx - col[:, None] + (NA_WIN_COLS - 1)

    def one_row(r):
        r0 = jnp.clip(r - kr // 2, 0, rows - kr)
        k_band = lax.dynamic_slice_in_dim(k, r0, kr, axis=2)
        v_band = lax.dynamic_slice_in_dim(v, r0, kr, axis=2)
        k_win = k_band[:, :, :, col_idx, :]
        v_win = v_band[:, :, :, col_idx, :]
        q_r = lax.dynamic_index_in_dim(q, r, axis=2, keepdims=False)
        row_bias_idx = r0 + jnp.arange(kr) - r + (NA_WIN_ROWS - 1)
        bias = rpb[:, row_bias_idx[None, :, None], col_bias_idx[:, None, :]]
        s_loc = jnp.einsum('bhwd,bhrwkd->bhwrk', q_r, k_win) + bias[None]
        s_loc = s_loc.reshape(b, h, GRID_W, kr * kc)
        s_ctx = jnp.einsum('bhwd,bhcd->bhwc', q_r, k_ctx)
        p = jax.nn.softmax(jnp.concatenate([s_loc, s_ctx], axis=-1).astype(jnp.float32), axis=-1).astype(v.dtype)
        p_loc = p[..., :kr * kc].reshape(b, h, GRID_W, kr, kc)
        p_ctx = p[..., kr * kc:]
        return (jnp.einsum('bhwrk,bhrwkd->bhwd', p_loc, v_win)
                + jnp.einsum('bhwc,bhcd->bhwd', p_ctx, v_ctx))

    o = lax.map(one_row, jnp.arange(rows))
    return o.transpose(1, 2, 0, 3, 4).reshape(b, h, n, dh)

def context_attention(q, k, v):
    s = jnp.einsum('bhqd,bhkd->bhqk', q, k).astype(jnp.float32)
    p = jax.nn.softmax(s, axis=-1).astype(v.dtype)
    return jnp.einsum('bhqk,bhkd->bhqd', p, v)

def log_forget(z, lb):
    f = lb.astype(jnp.float32) + (1.0 - lb.astype(jnp.float32)) * jax.nn.sigmoid(z.astype(jnp.float32))
    return jnp.log(jnp.maximum(f, FORGET_FLOOR))

def hgrn2_chunk_scan(q, k, v, g, s0):
    b, h, n, dk = q.shape
    dv = v.shape[-1]
    nc = n // HG_CHUNK

    def chunks(t):
        return jnp.moveaxis(t.reshape(b, h, nc, HG_CHUNK, t.shape[-1]), 2, 0)

    causal = jnp.tril(jnp.ones((HG_CHUNK, HG_CHUNK), dtype=bool))[:, :, None]

    def step(state, blk):
        qb, kb, vb, gb = blk
        qb = qb.astype(jnp.float32)
        kb = kb.astype(jnp.float32)
        vb = vb.astype(jnp.float32)
        cum = jnp.cumsum(gb.astype(jnp.float32), axis=2)
        rel = cum[:, :, :, None, :] - cum[:, :, None, :, :]
        decay = jnp.where(causal, jnp.exp(jnp.minimum(rel, 0.0)), 0.0)
        scores = jnp.einsum('bhtk,bhsk,bhtsk->bhts', qb, kb, decay)
        out = (jnp.einsum('bhts,bhsv->bhtv', scores, vb)
               + jnp.einsum('bhtk,bhkv->bhtv', qb * jnp.exp(cum), state))
        tail = cum[:, :, -1:, :]
        new_state = (jnp.exp(tail[:, :, 0, :])[..., None] * state
                     + jnp.einsum('bhsk,bhsv->bhkv', kb * jnp.exp(tail - cum), vb))
        return new_state, out

    s_final, o = lax.scan(step, s0, (chunks(q), chunks(k), chunks(v), chunks(g)))
    o = jnp.moveaxis(o, 0, 2).reshape(b, h, n, dv)
    return o.astype(v.dtype), s_final

def hgrn2_direction(q, k, v, g, s0, reverse):
    if reverse:
        q, k, v, g = [jnp.flip(t, axis=2) for t in (q, k, v, g)]
    o, s = hgrn2_chunk_scan(q, k, v, g, s0)
    if reverse:
        o = jnp.flip(o, axis=2)
    return o, s

def hgrn2_readout(o, gate, norm_g):
    o32 = o.astype(jnp.float32)
    o32 = o32 * lax.rsqrt(jnp.mean(jnp.square(o32), axis=-1, keepdims=True) + RMS_EPS) * norm_g.astype(jnp.float32)
    return from_heads((o32 * jax.nn.silu(gate.astype(jnp.float32))).astype(gate.dtype))

def even_mixer(hx, hc, w_in, w_out, rpb, lb, norm_g, need_ctx):
    bsz = hx.shape[0]
    scale = HEAD_DIM ** -0.5
    qx, kx, vx, hq_x, ff_x, fb_x, hi_x, hg_x = [to_heads(t) for t in jnp.split(hx @ w_in, N_EVEN_PARTS, axis=-1)]
    qc, kc, vc, hq_c, ff_c, fb_c, hi_c, hg_c = [to_heads(t) for t in jnp.split(hc @ w_in, N_EVEN_PARTS, axis=-1)]
    na_x = neighbourhood_attention(qx * scale, kx, vx, kc, vc, rpb)
    hqx = jax.nn.silu(hq_x) * scale
    hqc = jax.nn.silu(hq_c) * scale
    o_x = 0.0
    o_c = 0.0
    for d, (fz_x, fz_c) in enumerate(((ff_x, ff_c), (fb_x, fb_c))):
        lb_d = lb[d].reshape(N_HG_HEADS, 1, HEAD_DIM)
        g_c = log_forget(fz_c, lb_d)
        g_x = log_forget(fz_x, lb_d)
        s0 = jnp.zeros((bsz, N_HG_HEADS, HEAD_DIM, HEAD_DIM), jnp.float32)
        oc_d, s_ctx = hgrn2_direction(hqc, -jnp.expm1(g_c), hi_c, g_c, s0, d == 1)
        ox_d, _ = hgrn2_direction(hqx, -jnp.expm1(g_x), hi_x, g_x, s_ctx, d == 1)
        o_x = o_x + ox_d
        o_c = o_c + oc_d
    out_x = jnp.concatenate([from_heads(na_x), hgrn2_readout(o_x, hg_x, norm_g)], axis=-1) @ w_out
    if not need_ctx:
        return out_x, None
    na_c = context_attention(qc * scale, kc, vc)
    out_c = jnp.concatenate([from_heads(na_c), hgrn2_readout(o_c, hg_c, norm_g)], axis=-1) @ w_out
    return out_x, out_c

def depthwise_conv(u, w, b):
    y = lax.conv_general_dilated(
        u, w[:, None, :].astype(u.dtype), window_strides=(1,),
        padding=[(CONV_PAD_LEFT, CONV_W - 1 - CONV_PAD_LEFT)],
        dimension_numbers=('NWC', 'WIO', 'NWC'), feature_group_count=u.shape[-1])
    return y + b

def linear_combine(e1, e2):
    a1, b1 = e1
    a2, b2 = e2
    return a1 * a2, a2 * b1 + b2

def rglru_scan(u, w_a, b_a, w_x, b_x, lam, h0, reverse):
    bsz, n, w = u.shape
    ub = u.reshape(bsz, n, LRU_BLOCKS, LRU_BLOCK_DIM)
    r = jax.nn.sigmoid((jnp.einsum('bnkd,kde->bnke', ub, w_a).reshape(bsz, n, w) + b_a).astype(jnp.float32))
    i = jax.nn.sigmoid((jnp.einsum('bnkd,kde->bnke', ub, w_x).reshape(bsz, n, w) + b_x).astype(jnp.float32))
    log_a = -LRU_C * r * jax.nn.softplus(-lam.astype(jnp.float32))
    a = jnp.exp(log_a)
    x_in = jnp.sqrt(-jnp.expm1(2.0 * log_a)) * i * u.astype(jnp.float32)
    first = n - 1 if reverse else 0
    last = 0 if reverse else n - 1
    x_in = x_in.at[:, first].add(a[:, first] * h0)
    _, hs = lax.associative_scan(linear_combine, (a, x_in), axis=1, reverse=reverse)
    return hs, hs[:, last]

def rglru_mixer(hx, hc, w_in, conv_w, conv_b, w_a, b_a, w_x, b_x, lam, w_out, need_ctx):
    y_x, u_x = jnp.split(hx @ w_in, 2, axis=-1)
    y_c, u_c = jnp.split(hc @ w_in, 2, axis=-1)
    u_x = depthwise_conv(u_x, conv_w, conv_b)
    u_c = depthwise_conv(u_c, conv_w, conv_b)
    h0 = jnp.zeros((hc.shape[0], LRU_WIDTH), jnp.float32)
    hs_x = 0.0
    hs_c = 0.0
    for d in range(2):
        h_c, h_c_final = rglru_scan(u_c, w_a[d], b_a[d], w_x[d], b_x[d], lam[d], h0, d == 1)
        h_x, _ = rglru_scan(u_x, w_a[d], b_a[d], w_x[d], b_x[d], lam[d], h_c_final, d == 1)
        hs_x = hs_x + h_x
        hs_c = hs_c + h_c
    out_x = (hs_x * jax.nn.gelu(y_x.astype(jnp.float32))).astype(hx.dtype) @ w_out
    if not need_ctx:
        return out_x, None
    out_c = (hs_c * jax.nn.gelu(y_c.astype(jnp.float32))).astype(hc.dtype) @ w_out
    return out_x, out_c

def moe(h, router_w, router_bias, w_gate, w_up, w_down, s_gate, s_up, s_down):
    t_count, d = h.shape
    scores = jax.nn.sigmoid((h @ router_w).astype(jnp.float32))
    _, idx = lax.top_k(scores + router_bias.astype(jnp.float32), TOP_K)
    sel = jnp.take_along_axis(scores, idx, axis=1)
    wts = sel / jnp.sum(sel, axis=-1, keepdims=True) * ROUTED_SCALE
    tk = t_count * TOP_K
    flat_e = idx.reshape(-1)
    flat_t = jnp.repeat(jnp.arange(t_count, dtype=jnp.int32), TOP_K)
    flat_w = wts.reshape(-1)
    order = jnp.argsort(flat_e)
    se = flat_e[order]
    counts = jnp.bincount(flat_e, length=N_EXPERTS)
    padded = (counts + MOE_BLOCK - 1) // MOE_BLOCK * MOE_BLOCK
    starts = jnp.cumsum(counts) - counts
    pends = jnp.cumsum(padded)
    pstarts = pends - padded
    dest = pstarts[se] + jnp.arange(tk) - starts[se]
    n_blocks = -(-tk // MOE_BLOCK) + N_EXPERTS
    n_slots = n_blocks * MOE_BLOCK
    slot_tok = jnp.full((n_slots,), t_count, jnp.int32).at[dest].set(flat_t[order])
    slot_w = jnp.zeros((n_slots,), jnp.float32).at[dest].set(flat_w[order])
    block_exp = jnp.clip(jnp.searchsorted(pends, jnp.arange(n_blocks) * MOE_BLOCK, side='right'), 0, N_EXPERTS - 1)
    h_pad = jnp.concatenate([h, jnp.zeros((1, d), h.dtype)], axis=0)

    def run_block(args):
        toks, e = args
        xb = h_pad[toks]
        return (jax.nn.silu(xb @ w_gate[e]) * (xb @ w_up[e])) @ w_down[e]

    out = lax.map(run_block, (slot_tok.reshape(n_blocks, MOE_BLOCK), block_exp))
    out = out.reshape(n_slots, d) * slot_w[:, None]
    routed = jax.ops.segment_sum(out, slot_tok, num_segments=t_count + 1)[:t_count]
    shared = (jax.nn.silu(h @ s_gate) * (h @ s_up)) @ s_down
    return (routed + shared).astype(h.dtype)

def setup_inputs(seed: int = 0) -> dict:
    key = jax.random.key(seed)
    ks = jax.random.split(key, 32)
    f32 = jnp.float32
    D = D_MODEL

    def nrm(k, shape, std):
        return jax.random.normal(k, shape, f32) * std

    u = jax.random.uniform(ks[20], (N_ODD, 2, LRU_WIDTH), f32, minval=0.9, maxval=0.999)
    a0 = u ** (1.0 / LRU_C)
    return {
        'x': nrm(ks[0], (BATCH, SEQ, D), 1.0),
        'c': nrm(ks[1], (BATCH, D), 1.0),
        'ctx': nrm(ks[2], (BATCH, CTX_LEN, D), 1.0),
        'c_ctx': nrm(ks[3], (D,), 1.0),
        'ada_w': nrm(ks[4], (DEPTH, D, 6 * D), 0.5 * D ** -0.5),
        'ada_b': nrm(ks[5], (DEPTH, 6 * D), 0.01),
        'ln_g': 1.0 + nrm(ks[6], (DEPTH, 2, D), 0.01),
        'ln_b': nrm(ks[7], (DEPTH, 2, D), 0.01),
        'ev_w_in': nrm(ks[8], (N_EVEN, D, EVEN_IN_WIDTH), D ** -0.5),
        'ev_w_out': nrm(ks[9], (N_EVEN, MIX_WIDTH, D), DEEPNORM_BETA * MIX_WIDTH ** -0.5),
        'na_rpb': nrm(ks[10], (N_EVEN, N_NA_HEADS, 2 * NA_WIN_ROWS - 1, 2 * NA_WIN_COLS - 1), 0.1),
        'hg_lb_raw': nrm(ks[11], (2, N_EVEN, HG_WIDTH), 0.5),
        'hg_norm_g': 1.0 + nrm(ks[12], (N_EVEN, HEAD_DIM), 0.01),
        'od_w_in': nrm(ks[13], (N_ODD, D, 2 * LRU_WIDTH), D ** -0.5),
        'od_conv_w': nrm(ks[14], (N_ODD, CONV_W, LRU_WIDTH), CONV_W ** -0.5),
        'od_conv_b': nrm(ks[15], (N_ODD, LRU_WIDTH), 0.01),
        'lru_w_a': nrm(ks[16], (N_ODD, 2, LRU_BLOCKS, LRU_BLOCK_DIM, LRU_BLOCK_DIM), LRU_BLOCK_DIM ** -0.5),
        'lru_b_a': nrm(ks[17], (N_ODD, 2, LRU_WIDTH), 0.01),
        'lru_w_x': nrm(ks[18], (N_ODD, 2, LRU_BLOCKS, LRU_BLOCK_DIM, LRU_BLOCK_DIM), LRU_BLOCK_DIM ** -0.5),
        'lru_b_x': nrm(ks[19], (N_ODD, 2, LRU_WIDTH), 0.01),
        'lru_lam': jnp.log(a0) - jnp.log1p(-a0),
        'od_w_out': nrm(ks[21], (N_ODD, LRU_WIDTH, D), DEEPNORM_BETA * LRU_WIDTH ** -0.5),
        'router_w': nrm(ks[22], (DEPTH, D, N_EXPERTS), D ** -0.5),
        'router_bias': nrm(ks[23], (DEPTH, N_EXPERTS), 0.01),
        'exp_w_gate': nrm(ks[24], (DEPTH, N_EXPERTS, D, EXPERT_HIDDEN), D ** -0.5),
        'exp_w_up': nrm(ks[25], (DEPTH, N_EXPERTS, D, EXPERT_HIDDEN), D ** -0.5),
        'exp_w_down': nrm(ks[26], (DEPTH, N_EXPERTS, EXPERT_HIDDEN, D), DEEPNORM_BETA * EXPERT_HIDDEN ** -0.5),
        'sh_w_gate': nrm(ks[27], (DEPTH, D, SHARED_HIDDEN), D ** -0.5),
        'sh_w_up': nrm(ks[28], (DEPTH, D, SHARED_HIDDEN), D ** -0.5),
        'sh_w_down': nrm(ks[29], (DEPTH, SHARED_HIDDEN, D), DEEPNORM_BETA * SHARED_HIDDEN ** -0.5),
    }

def reference(x, c, ctx, c_ctx, ada_w, ada_b, ln_g, ln_b, ev_w_in, ev_w_out, na_rpb, hg_lb_raw, hg_norm_g,
              od_w_in, od_conv_w, od_conv_b, lru_w_a, lru_b_a, lru_w_x, lru_b_x, lru_lam, od_w_out,
              router_w, router_bias, exp_w_gate, exp_w_up, exp_w_down, sh_w_gate, sh_w_up, sh_w_down):
    bsz, n, d = x.shape
    n_ctx_tok = ctx.shape[0] * ctx.shape[1]
    p_lb = jax.nn.softmax(hg_lb_raw.astype(jnp.float32), axis=1)
    hg_lb = jnp.cumsum(p_lb, axis=1) - p_lb[:, :1]
    silu_c = jax.nn.silu(c)
    silu_cc = jax.nn.silu(c_ctx)
    x_lat = x
    x_ctx = ctx
    for l in range(DEPTH):
        last = l == DEPTH - 1
        j = l // 2
        mod_x = jnp.split((silu_c @ ada_w[l] + ada_b[l])[:, None, :], 6, axis=-1)
        mod_c = jnp.split(silu_cc @ ada_w[l] + ada_b[l], 6, axis=-1)
        hx = x_lat * (1.0 + mod_x[1]) + mod_x[0]
        hc = x_ctx * (1.0 + mod_c[1]) + mod_c[0]
        if l % 2 == 0:
            ox, oc = even_mixer(hx, hc, ev_w_in[j], ev_w_out[j], na_rpb[j], hg_lb[:, j], hg_norm_g[j], not last)
        else:
            ox, oc = rglru_mixer(hx, hc, od_w_in[j], od_conv_w[j], od_conv_b[j], lru_w_a[j], lru_b_a[j],
                                 lru_w_x[j], lru_b_x[j], lru_lam[j], od_w_out[j], not last)
        x_lat = layer_norm(DEEPNORM_ALPHA * x_lat + mod_x[2] * ox, ln_g[l, 0], ln_b[l, 0])
        hx = x_lat * (1.0 + mod_x[4]) + mod_x[3]
        if last:
            y = moe(hx.reshape(-1, d), router_w[l], router_bias[l], exp_w_gate[l], exp_w_up[l], exp_w_down[l],
                    sh_w_gate[l], sh_w_up[l], sh_w_down[l])
        else:
            x_ctx = layer_norm(DEEPNORM_ALPHA * x_ctx + mod_c[2] * oc, ln_g[l, 0], ln_b[l, 0])
            hc = x_ctx * (1.0 + mod_c[4]) + mod_c[3]
            y_all = moe(jnp.concatenate([hc.reshape(-1, d), hx.reshape(-1, d)], axis=0), router_w[l],
                        router_bias[l], exp_w_gate[l], exp_w_up[l], exp_w_down[l],
                        sh_w_gate[l], sh_w_up[l], sh_w_down[l])
            x_ctx = layer_norm(DEEPNORM_ALPHA * x_ctx + mod_c[5] * y_all[:n_ctx_tok].reshape(x_ctx.shape),
                               ln_g[l, 1], ln_b[l, 1])
            y = y_all[n_ctx_tok:]
        x_lat = layer_norm(DEEPNORM_ALPHA * x_lat + mod_x[5] * y.reshape(bsz, n, d), ln_g[l, 1], ln_b[l, 1])
    return x_lat


_drawn_inputs = setup_inputs


def setup_inputs(seed=0):
    import zlib

    import numpy as np

    out = dict(_drawn_inputs(seed))
    spreads = {}
    factors = {'ada_b': 2.961,
     'na_rpb': 44.726,
     'hg_norm_g': 63.617,
     'od_conv_b': 5.309,
     'lru_b_a': 64.0,
     'lru_b_x': 56.654}
    for name, (base, spread) in spreads.items():
        noise = np.random.default_rng([zlib.crc32(name.encode()), seed]).standard_normal(out[name].shape)
        drawn = base * np.exp(spread * noise) if base else spread * noise
        out[name] = jnp.asarray(drawn.astype(out[name].dtype))
    for name, factor in factors.items():
        out[name] = (out[name] * factor).astype(out[name].dtype)
    return out
```

```python
from contextlib import ExitStack

import numpy as np

import concourse.bass as bass
from concourse import mybir

F32 = mybir.dt.float32
U32 = mybir.dt.uint32
ALU = mybir.AluOpType
ACT = mybir.ActivationFunctionType
AX_X = mybir.AxisListType.X

P = 128
D = 1024
KD = D // P
T = 512
HALF = 256
NT = T // P
CH = 64
NC = T // CH
HD = 64
PAIRS = 4
LEVELS = (64, 32, 16, 8, 4, 2)
NL = len(LEVELS) + 1
E = 64
HID = 256
TOPK = 6
ROUTED_SCALE = 2.5
ALPHA = 4 ** 0.25
LN_EPS = 1e-5
RMS_EPS = 1e-6
FLOOR = 1e-30
LRU_C = 8.0
SLOT = KD * 512
SLOTS = 3
EXPERT = KD * 512 + 2 * D


class Chain:

    def __init__(self, eng, sem):
        self.eng, self.sem, self.n = eng, sem, 0

    def then(self, ins):
        self.n += 1
        ins.then_inc(self.sem, 1)

    def settle(self):
        self.eng.wait_ge(self.sem, self.n)

    def link(self, ins):
        self.then(ins)
        self.settle()


def trunk(nc, a, out, debug=()):
    ctx = ExitStack()
    with ctx:
        def sb(name, words):
            return ctx.enter_context(nc.sbuf_tensor(name, [P, words], F32))

        def sem(name):
            return ctx.enter_context(nc.semaphore(name))

        W = sb("W", 18432)
        X = sb("X", NT * D)
        MOD = sb("MOD", 6 * D)
        HT = sb("HT", KD * T)
        A = sb("A", 16128)
        ident = sb("ident", P)
        ones64 = sb("ones64", P)
        levmask = sb("levmask", 2 * NL * CH)
        restart = sb("restart", T)
        iota = sb("iota", E)
        CR = sb("CR", KD * P)
        small = sb("small", 256)
        gates = sb("gates", NT * E)
        PS = [ctx.enter_context(nc.psum_tensor(f"PS{i}", [P, 512], F32)) for i in range(8)]

        def cut(t, at, *dims):
            n = 1
            for d in dims:
                n *= d
            v = t[:, at:at + n]
            if len(dims) == 2:
                return v.rearrange("p (a b) -> p a b", b=dims[1])
            if len(dims) == 3:
                return v.rearrange("p (a b c) -> p a b c", b=dims[1], c=dims[2])
            return v

        Xt = cut(X, 0, NT, D)
        HTt = cut(HT, 0, KD, T)
        eps = small[:, 0:1]
        rmseps = small[:, 1:2]
        cT = small[:, 8:24]
        lbr = small[:, 128:136]
        normg = small[:, 136:137]
        convw = small[:, 137:169]
        convb = small[:, 169:177]
        gbias = small[:, 177:209]
        lam = small[:, 209:225]
        lb = small[:, 32:40]
        omlb = small[:, 40:48]
        stats = small[:, 64:64 + 12]
        mv = small[:, 80:82]
        rstd = small[:, 82:84]
        chain = {n: sem("chain_" + n) for n in ("dve", "act", "pool")}
        DV = Chain(nc.vector, chain["dve"])
        AC = Chain(nc.scalar, chain["act"])
        GP = Chain(nc.gpsimd, chain["pool"])

        chunks = []

        def chunk(*parts):
            chunks.append(parts)
            return len(chunks) - 1

        rows = lambda w: w.rearrange("(p k) n -> p k n", k=KD)
        ada_chunk = lambda l, n: chunk(rows(a["ada_w"][l])[:, :, 512 * n:512 * n + 512])
        ada = [[ada_chunk(0, n) for n in range(12)], []]
        ev = rows(a["ev_w_in"][0])
        col = lambda part, p: ev[:, :, 512 * part + P * p:512 * part + P * p + P]
        na_w, hz_w, hv_w = [], [], []
        for p in range(PAIRS):
            na_w.append(chunk(col(0, p), col(1, p), col(2, p)))
            hz_w.append(chunk(col(3, p), col(4, p), col(5, p)))
            hv_w.append(chunk(col(6, p), col(7, p)))
        nat = lambda w: w.rearrange("(k p) n -> p k n", p=P)
        evo = [chunk(nat(a["ev_w_out"][0])[:, :, 512 * n:512 * n + 512]) for n in range(2)]
        moe0_at = len(chunks)
        ada[1] += [ada_chunk(1, n) for n in range(4)]
        odi = [chunk(rows(a["od_w_in"][0])[:, :, 512 * n:512 * n + 512]) for n in range(4)]
        ada[1] += [ada_chunk(1, n) for n in range(4, 12)]
        odo = [chunk(nat(a["od_w_out"][0])[:, :, 512 * n:512 * n + 512]) for n in range(2)]
        moe1_at = len(chunks)

        slot_sem = [sem(f"slot{i}") for i in range(SLOTS)]
        chunk_used = sem("chunk_used")
        landed, count = [], [0] * SLOTS
        for i, parts in enumerate(chunks):
            count[i % SLOTS] += 16 * len(parts)
            landed.append(count[i % SLOTS])
        sent, limit = [0], [moe0_at]

        def view(i, part=0):
            at = SLOT * (i % SLOTS)
            for q in chunks[i][:part]:
                at += q.shape[1] * q.shape[2]
            return cut(W, at, *chunks[i][part].shape[1:])

        def send(sp, upto):
            while sent[0] < min(upto, limit[0]):
                i = sent[0]
                if i >= SLOTS:
                    sp.wait_ge(chunk_used, i - SLOTS + 1)
                for j, q in enumerate(chunks[i]):
                    sp.dma_start(view(i, j), q).then_inc(slot_sem[i % SLOTS], 16)
                sent[0] += 1

        def arrived(eng, i):
            eng.wait_ge(slot_sem[i % SLOTS], landed[i])

        with nc.Block() as block:
            const = sem("const")
            cond = sem("cond")

            @block.sync
            def _(sp):
                sp.dma_start(cut(small, 8, 8), a["c_ctx"].rearrange("(p k) -> p k", k=KD)).then_inc(const, 16)
                sp.dma_start(cut(small, 16, 8), a["c"][0].rearrange("(p k) -> p k", k=KD)).then_inc(const, 16)
                send(sp, 3)
                for t, name in ((ident, "k_ident"), (ones64, "k_ones64"), (levmask, "k_levmask"),
                                (restart, "k_restart"), (iota, "k_iota")):
                    sp.dma_start(t[:], a[name]).then_inc(const, 16)
                for s, name in enumerate(("ctx", "x")):
                    sp.dma_start(Xt[64 * s:64 * s + 64], a[name][0].rearrange("(i n) d -> n i d", n=CH)).then_inc(const, 16)
                sp.dma_start(small[:, 128:225], a["vectors"]).then_inc(const, 16)
                sp.wait_ge(const, 16 * 10)

            @block.gpsimd
            def _(pool):
                pool.memset(A[:], 0.0)
                pool.memset(small[:, 0:1], LN_EPS)
                pool.memset(small[:, 1:2], RMS_EPS)

            @block.scalar
            def _(act):
                act.wait_ge(const, 16 * 10)
                act.activation(cT, cT, ACT.Silu).then_inc(cond, 1)

        def replicate(tag, split):
            with nc.Block() as block:
                @block.vector
                def _(dve):
                    cr = cut(CR, 0, KD, P)
                    if split:
                        dve.tensor_copy(cr[:, :, 0:64], cT[:, 0:8].unsqueeze(2).broadcast_to([P, KD, 64]))
                    else:
                        dve.tensor_copy(cr[:, :, 0:64], cT[:, 8:16].unsqueeze(2).broadcast_to([P, KD, 64]))
                    dve.tensor_copy(cr[:, :, 64:128], cT[:, 8:16].unsqueeze(2).broadcast_to([P, KD, 64]))

        with nc.Block() as block:
            lbs = sem("lbs")

            @block.vector
            def _(dve):
                DV.link(dve.tensor_tensor(lb, lbr, lbr, ALU.subtract))
                dve.wait_ge(cond, 1)
                dve.nop().then_inc(lbs, 1)
                dve.wait_ge(lbs, 2)
                DV.link(dve.reciprocal(omlb, lb))
                DV.link(dve.tensor_tensor(lb, lb, omlb, ALU.mult))
                DV.link(dve.tensor_tensor(lb, lb, lb, ALU.subtract))
                DV.link(dve.tensor_scalar(omlb, lb, -1.0, 1.0, ALU.mult, ALU.add))

            @block.scalar
            def _(act):
                act.wait_ge(lbs, 1)
                act.activation(lb, lb, ACT.Exp).then_inc(lbs, 1)

        def modulation(l, ns):
            bias_in, prod, added = sem(f"bias_in{l}{ns[0]}"), sem(f"mod_prod{l}{ns[0]}"), sem(f"mod_added{l}{ns[0]}")
            cr = cut(CR, 0, KD, P)
            lo, hi = 512 * ns[0], 512 * ns[-1] + 512
            with nc.Block() as block:
                @block.sync
                def _(sp):
                    sp.dma_start(MOD[:, lo:hi], a["ada_b"][l:l + 1, lo:hi].broadcast_to([P, hi - lo])).then_inc(bias_in, 16)
                    send(sp, ada[l][ns[-1]] + 1 + SLOTS)

                @block.tensor
                def _(pe):
                    for j, n in enumerate(ns):
                        i = ada[l][n]
                        arrived(pe, i)
                        if j >= 4:
                            pe.wait_ge(added, j - 3)
                        for k in range(KD):
                            mm = pe.matmul(PS[j % 4][:], cr[:, k, :], view(i)[:, k, :], start=(k == 0), stop=(k == KD - 1))
                        mm.then_inc(chunk_used, 1)

                @block.vector
                def _(dve):
                    dve.wait_ge(bias_in, 16)
                    for j, n in enumerate(ns):
                        dve.wait_ge(chunk_used, ada[l][n] + 1)
                        m = MOD[:, 512 * n:512 * n + 512]
                        dve.tensor_tensor(m, PS[j % 4][:], m, ALU.add).then_inc(added, 1)

        H = cut(A, 0, NT, D)

        def modulate(tag, shift, scale, nt, mixed, upto):
            h_ready, turned, copied = sem("h_ready" + tag), sem("turned" + tag), sem("copied" + tag)
            if mixed:
                cols = HT[:].rearrange("p (k s i n) -> p k s i n", k=KD, s=2, i=NT)
            with nc.Block() as block:
                @block.sync
                def _(sp):
                    send(sp, upto)

                @block.vector
                def _(dve):
                    for i in range(nt):
                        DV.link(dve.scalar_tensor_tensor(H[:, i, :], MOD[:, D * scale:D * scale + D], 1.0, Xt[:, i, :], ALU.add, ALU.mult))
                        dve.tensor_tensor(H[:, i, :], H[:, i, :], MOD[:, D * shift:D * shift + D], ALU.add).then_inc(h_ready, 1)

                @block.tensor
                def _(pe):
                    for i in range(nt):
                        pe.wait_ge(h_ready, i + 1)
                        h = H[:, i, :].rearrange("t (p k) -> t k p", k=KD)
                        for g in range(2):
                            b = (2 * i + g) % 4
                            if 2 * i + g >= 4:
                                pe.wait_ge(copied, 2 * i + g - 3)
                            for k in range(4):
                                tr = pe.transpose(PS[b][:, P * k:P * k + P], h[:, 4 * g + k, :], ident[:])
                            tr.then_inc(turned, 1)

                @block.scalar
                def _(act):
                    for i in range(nt):
                        for g in range(2):
                            act.wait_ge(turned, 2 * i + g + 1)
                            src = PS[(2 * i + g) % 4]
                            if mixed:
                                for s in range(2):
                                    ins = act.activation(cols[:, 4 * g:4 * g + 4, s, i, :],
                                                         src[:].rearrange("p (k s n) -> p k s n", s=2, n=CH)[:, :, s, :], ACT.Copy)
                            else:
                                ins = act.activation(HTt[:, 4 * g:4 * g + 4, P * i:P * i + P],
                                                     src[:].rearrange("p (k n) -> p k n", n=P), ACT.Copy)
                            ins.then_inc(copied, 1)

        LNG, LNB = cut(A, 8192, D), cut(A, 8192 + D, D)

        def project_out(tag, cks, srcT, gate, nt, lhs, upto):
            done, freed = sem("out_done" + tag), sem("out_freed" + tag)
            with nc.Block() as block:
                @block.sync
                def _(sp):
                    send(sp, upto)

                @block.tensor
                def _(pe):
                    for n in range(2):
                        arrived(pe, cks[n])
                        for i in range(nt):
                            j = nt * n + i
                            if j >= 4:
                                pe.wait_ge(freed, j - 3)
                            for k in range(KD):
                                mm = pe.matmul(PS[j % 4][:], lhs(srcT, k, i), view(cks[n])[:, k, :], start=(k == 0), stop=(k == KD - 1))
                            if i == nt - 1:
                                mm.then_inc(chunk_used, 1)
                            else:
                                mm.then_inc(done, 1)

                @block.vector
                def _(dve):
                    for n in range(2):
                        for i in range(nt):
                            if i == nt - 1:
                                dve.wait_ge(chunk_used, cks[n] + 1)
                            else:
                                dve.wait_ge(done, (nt - 1) * n + i + 1)
                            dve.tensor_tensor(H[:, i, 512 * n:512 * n + 512], PS[(nt * n + i) % 4][:],
                                              MOD[:, D * gate + 512 * n:D * gate + 512 * n + 512], ALU.mult).then_inc(freed, 1)

        def residual_norm(tag, l, which, nt, src, gate, upto):
            ln_in, var, root, normed = sem("ln_in" + tag), sem("ln_var" + tag), sem("ln_root" + tag), sem("ln_normed" + tag)
            with nc.Block() as block:
                @block.sync
                def _(sp):
                    sp.dma_start(LNG, a["ln_g"][l, which:which + 1, :].broadcast_to([P, D])).then_inc(ln_in, 16)
                    sp.dma_start(LNB, a["ln_b"][l, which:which + 1, :].broadcast_to([P, D])).then_inc(ln_in, 16)
                    send(sp, upto)

                @block.vector
                def _(dve):
                    for i in range(nt):
                        x = Xt[:, i, :]
                        if gate is not None:
                            DV.link(dve.tensor_tensor(src[:, i, :], src[:, i, :], MOD[:, D * gate:D * gate + D], ALU.mult))
                        DV.link(dve.scalar_tensor_tensor(x, x, ALPHA, src[:, i, :], ALU.mult, ALU.add))
                        for s in range(2):
                            DV.then(dve.bn_stats(stats[:, 6 * s:6 * s + 6], x[:, 512 * s:512 * s + 512]))
                        DV.settle()
                        dve.bn_aggr(mv, stats).then_inc(var, 1)
                        dve.wait_ge(root, i + 1)
                        DV.link(dve.reciprocal(rstd[:, 1:2], rstd[:, 0:1]))
                        dve.tensor_scalar(x, x, mv[:, 0:1], rstd[:, 1:2], ALU.subtract, ALU.mult).then_inc(normed, 1)

                @block.scalar
                def _(act):
                    for i in range(nt):
                        act.wait_ge(var, i + 1)
                        act.activation(rstd[:, 0:1], mv[:, 1:2], ACT.Sqrt, bias=eps).then_inc(root, 1)

                @block.gpsimd
                def _(pool):
                    pool.wait_ge(ln_in, 32)
                    for i in range(nt):
                        x = Xt[:, i, :]
                        pool.wait_ge(normed, i + 1)
                        GP.link(pool.tensor_tensor(x, x, LNG, ALU.mult))
                        pool.tensor_tensor(x, x, LNB, ALU.add)

        pass
        plain_cols = lambda t, k, i: t[:, T * k + P * i:T * k + P * i + P]

        mixT = cut(A, 12032, 2 * PAIRS, T)
        by_tile = lambda v: v.rearrange("p (i s n) -> p s i n", s=2, n=CH)
        TAIL = SLOTS * SLOT

        def tail(at, *dims):
            return cut(W, TAIL + at, *dims)

        qT, kT, vT = tail(0, T), tail(512, T), tail(1024, NT, P)
        BT = tail(1536, 2, 6, CH)
        Sb = [tail(2304 + 512 * i, 512) for i in range(2)]
        Pr = [tail(3328 + 512 * i, 512) for i in range(2)]
        PT = [tail(4352 + 512 * i, 512) for i in range(2)]
        window = cut(MOD, 448, CH)
        na = {n: sem("na_" + n) for n in ("proj", "evac", "bias_in", "bias", "score", "biased", "negmax", "exp", "prob", "turn",
                                          "turned", "pv", "win")}
        UNITS = [(t, h) for t in range(NT) for h in range(2)]
        NU = len(UNITS)

        def attention(p):
            i = na_w[p]
            with nc.Block() as block:
                @block.sync
                def _(sp):
                    if p == 0:
                        sp.dma_start(window, a["k_window"]).then_inc(na["win"], 16)
                    sp.dma_start(BT, a["rpb_band"][:, 2 * p:2 * p + 2]).then_inc(na["bias_in"], 16)
                    send(sp, i + 1 + SLOTS)

                @block.tensor
                def _(pe):
                    arrived(pe, i)
                    for part in range(2):
                        for k in range(KD):
                            mm = pe.matmul(PS[part][:], view(i, part)[:, k, :], HTt[:, k, :], start=(k == 0), stop=(k == KD - 1))
                        mm.then_inc(na["proj"], 1)
                    for t in range(NT):
                        for k in range(KD):
                            mm = pe.matmul(PS[2][:, P * t:P * t + P], HTt[:, k, P * t:P * t + P], view(i, 2)[:, k, :],
                                           start=(k == 0), stop=(k == KD - 1))
                    mm.then_inc(chunk_used, 1)
                    pe.wait_ge(na["evac"], 3 * p + 3)

                    def scores(u):
                        t, h = UNITS[u]
                        if u >= 2:
                            pe.wait_ge(na["exp"], NU * p + u - 1)
                        n = T if t >= 2 else HALF
                        pe.matmul(PS[3 + h][:, 0:n], qT[64 * h:64 * h + 64, P * t:P * t + P], kT[64 * h:64 * h + 64, 0:n],
                                  start=True, stop=True).then_inc(na["score"], 1)

                    scores(0)
                    for u, (t, h) in enumerate(UNITS):
                        if u + 1 < NU:
                            scores(u + 1)
                        kt = 4 if t >= 2 else 2
                        pe.wait_ge(na["prob"], NU * p + u + 1)
                        if u >= 2:
                            pe.wait_ge(na["turned"], NU * p + u - 1)
                        for j in range(kt):
                            tr = pe.transpose(PS[5 + u % 2][:, P * j:P * j + P], Pr[u % 2][:, P * j:P * j + P], ident[:])
                        tr.then_inc(na["turn"], 1)
                        pe.wait_ge(na["turned"], NU * p + u + 1)
                        for j in range(kt):
                            mm = pe.matmul(PS[7][64 * h:64 * h + 64, P * t:P * t + P], vT[:, j, 64 * h:64 * h + 64],
                                           PT[u % 2][:, P * j:P * j + P], start=(j == 0), stop=(j == kt - 1))
                        mm.then_inc(na["pv"], 1)

                @block.scalar
                def _(act):
                    act.wait_ge(na["proj"], 2 * p + 1)
                    act.activation(qT, PS[0][:], ACT.Copy, scale=HD ** -0.5).then_inc(na["evac"], 1)
                    act.wait_ge(na["proj"], 2 * p + 2)
                    act.activation(kT, PS[1][:], ACT.Copy).then_inc(na["evac"], 1)
                    act.wait_ge(chunk_used, i + 1)
                    act.activation(vT, PS[2][:].rearrange("p (t n) -> p t n", n=P), ACT.Copy).then_inc(na["evac"], 1)

                    def turned(u):
                        t, h = UNITS[u]
                        n = T if t >= 2 else HALF
                        act.wait_ge(na["turn"], NU * p + u + 1)
                        if u >= 2:
                            act.wait_ge(na["pv"], NU * p + u - 1)
                        act.activation(PT[u % 2][:, 0:n], PS[5 + u % 2][:, 0:n], ACT.Copy).then_inc(na["turned"], 1)

                    for u, (t, h) in enumerate(UNITS):
                        act.wait_ge(na["negmax"], NU * p + u + 1)
                        if u >= 2:
                            act.wait_ge(na["turn"], NU * p + u - 1)
                        if t >= 2:
                            src, n = Sb[u % 2], T
                        else:
                            src, n = PS[3 + h][:, 0:HALF], HALF
                        act.activation(Pr[u % 2][:, 0:n], src, ACT.Exp, bias=small[:, 88 + u % 2:89 + u % 2],
                                       accum_out=small[:, 90 + u % 2:91 + u % 2]).then_inc(na["exp"], 1)
                        if u >= 1:
                            turned(u - 1)
                    turned(NU - 1)
                    act.wait_ge(na["pv"], NU * (p + 1))
                    act.activation(by_tile(mixT[:, p, :]), PS[7][:].rearrange("p (s i n) -> p s i n", s=2, n=CH), ACT.Copy)

                @block.vector
                def _(dve):
                    if p == 0:
                        dve.wait_ge(na["win"], 16)
                    dve.wait_ge(na["bias_in"], 16 * (p + 1))
                    bt = BT.rearrange("p h o w -> p (h o) w") if len(BT.shape) == 4 else BT
                    DV.link(dve.tensor_tensor(bt, bt, window.unsqueeze(1).broadcast_to([P, 12, CH]), ALU.add))
                    band = tail(1536, 2, 6 * CH)

                    def norm(u):
                        t, h = UNITS[u]
                        n = T if t >= 2 else HALF
                        dve.wait_ge(na["exp"], NU * p + u + 1)
                        r = small[:, 92 + u % 2:93 + u % 2]
                        DV.link(dve.reciprocal(r, small[:, 90 + u % 2:91 + u % 2]))
                        dve.tensor_scalar(Pr[u % 2][:, 0:n], Pr[u % 2][:, 0:n], r, None, ALU.mult).then_inc(na["prob"], 1)

                    for u, (t, h) in enumerate(UNITS):
                        dve.wait_ge(na["score"], NU * p + u + 1)
                        ps = PS[3 + h]
                        if t >= 2:
                            if u >= 2:
                                dve.wait_ge(na["exp"], NU * p + u - 1)
                            DV.then(dve.tensor_copy(Sb[u % 2][:, 0:HALF], ps[:, 0:HALF]))
                            at = CH * (2 - 2 * (t - 2))
                            DV.link(dve.tensor_tensor(Sb[u % 2][:, HALF:T], ps[:, HALF:T], band[:, h, at:at + HALF], ALU.add))
                            src = Sb[u % 2]
                        else:
                            src = ps[:, 0:HALF]
                        dve.tensor_reduce(small[:, 88 + u % 2:89 + u % 2], src, AX_X, ALU.max, negate=True).then_inc(na["negmax"], 1)
                        if u >= 1:
                            norm(u - 1)
                    norm(NU - 1)

        HQ, SG, F, KK, CUM, QS, KS = (tail(512 * n, T) for n in range(7))
        KST = tail(3584, NT, P)
        DD = [tail(4096 + HALF * n, HALF) for n in range(2)]
        EE = [tail(4608 + HALF * n, HALF) for n in range(2)]
        OS, SQ = tail(5120, T), tail(5632, T)
        NCH = NC // 2
        KB = [cut(A, 3584 * n, NL * NCH, P) for n in range(2)]
        QB = [cut(A, 7168 + 1536 * n, NL - 1, HALF) for n in range(2)]
        VB = cut(A, 10240, NC, P)
        MK = [cut(A, 11264, NL, CH), cut(MOD, 0, NL, CH)]
        SM = [cut(A, 11712 + CH * n, CH) for n in range(2)]
        ST = cut(MOD, 1024, NC, P)
        V = cut(MOD, 512, NT, P)
        TL, ET = small[:, 96:104], small[:, 104:112]
        lm = cut(levmask, 0, 2 * NL, CH)
        hg = {n: sem("hg_" + n) for n in (
            "proj", "query", "values", "gate", "sig", "forget", "log", "cum", "factor", "inter", "kturn", "kturned",
            "update", "state", "diff", "exp", "level", "diag", "score", "masked", "summed", "out", "out1", "osum", "square",
            "mean", "root", "clean")}
        ORDER = [list(range(NC)), [3, 2, 1, 0, 7, 6, 5, 4]]

        def hgrn(p):
            iz, iv = hz_w[p], hv_w[p]
            U = [(d, hf) for d in range(2) for hf in range(2)]
            with nc.Block() as block:
                @block.sync
                def _(sp):
                    send(sp, iv + 1 + SLOTS)

                @block.tensor
                def _(pe):
                    arrived(pe, iz)
                    for part in range(3):
                        for k in range(KD):
                            mm = pe.matmul(PS[part][:], view(iz, part)[:, k, :], HTt[:, k, :], start=(k == 0), stop=(k == KD - 1))
                        mm.then_inc(chunk_used if part == 2 else hg["proj"], 1)
                    arrived(pe, iv)
                    for t in range(NT):
                        for k in range(KD):
                            mm = pe.matmul(PS[3][:, P * t:P * t + P], HTt[:, k, P * t:P * t + P], view(iv, 0)[:, k, :],
                                           start=(k == 0), stop=(k == KD - 1))
                    mm.then_inc(hg["proj"], 1)
                    for k in range(KD):
                        mm = pe.matmul(PS[4][:], view(iv, 1)[:, k, :], HTt[:, k, :], start=(k == 0), stop=(k == KD - 1))
                    mm.then_inc(chunk_used, 1)

                    def turn_keys(d):
                        pe.wait_ge(hg["inter"], 2 * p + d + 1)
                        if d:
                            pe.wait_ge(hg["kturned"], 2 * p + d)
                        for t in range(NT):
                            tr = pe.transpose(PS[6][:, P * t:P * t + P], KS[:, P * t:P * t + P], ident[:])
                        tr.then_inc(hg["kturn"], 1)

                    def updates(d):
                        pe.wait_ge(hg["kturned"], 2 * p + d + 1)
                        pe.wait_ge(hg["values"], p + 1)
                        if d:
                            pe.wait_ge(hg["state"], 2 * p + d)
                        for t in range(NT):
                            for j in range(2):
                                mm = pe.matmul(PS[3 + 2 * j][:, P * t:P * t + P], KST[64 * j:64 * j + 64, t, :],
                                               V[64 * j:64 * j + 64, t, :], start=True, stop=True)
                        mm.then_inc(hg["update"], 1)

                    def level_scores(n, c):
                        d, hf = U[n]
                        s = NCH * n + c
                        if s >= 2:
                            pe.wait_ge(hg["masked"], 16 * p + s - 1)
                        for l in range(NL):
                            rhs = QB[n % 2][:, l, CH * c:CH * c + CH] if l < NL - 1 else HQ[:, HALF * hf + CH * c:HALF * hf + CH * c + CH]
                            mm = pe.matmul(PS[4 * (s % 2)][:, CH * l:CH * l + CH], KB[n % 2][:, NCH * l + c, :], rhs, start=True, stop=True)
                        mm.then_inc(hg["score"], 1)

                    def outputs(n, c):
                        d, hf = U[n]
                        s = NCH * n + c
                        g = NCH * hf + c
                        o = PS[(7, 1)[d]][:, CH * g:CH * g + CH]
                        pe.wait_ge(hg["summed"], 16 * p + s + 1)
                        pe.matmul(o, VB[:, g, :], SM[s % 2], start=True, stop=False)
                        pe.matmul(o, ST[:, g, :], QS[:, CH * g:CH * g + CH], start=False, stop=True).then_inc(hg["out"], 1)

                    for n, (d, hf) in enumerate(U):
                        if hf == 0:
                            turn_keys(d)
                            updates(d)
                        if n == 0:
                            pe.wait_ge(hg["query"], p + 1)
                            pe.wait_ge(hg["gate"], p + 1)
                        pe.wait_ge(hg["level"], 6 * (4 * p + n + 1))
                        pe.wait_ge(hg["diag"], 4 * p + n + 1)
                        level_scores(n, 0)
                        if hf == 0:
                            pe.wait_ge(hg["state"], 2 * p + d + 1)
                        for c in range(NCH):
                            if c + 1 < NCH:
                                level_scores(n, c + 1)
                            outputs(n, c)
                    pe.wait_ge(hg["square"], p + 1)
                    pe.matmul(PS[3][:], ones64[:], SQ, start=True, stop=True).then_inc(hg["mean"], 1)

                @block.scalar
                def _(act):
                    def sigmoids(d):
                        z = PS[1 + d]
                        act.activation(F, z[:], ACT.Sigmoid)
                        act.activation(KK, z[:], ACT.Sigmoid, scale=-1.0).then_inc(hg["sig"], 1)

                    act.wait_ge(hg["proj"], 3 * p + 1)
                    act.activation(HQ, PS[0][:], ACT.Silu).then_inc(hg["query"], 1)
                    act.wait_ge(hg["proj"], 3 * p + 2)
                    sigmoids(0)
                    act.wait_ge(hg["proj"], 3 * p + 3)
                    src = PS[3][:].rearrange("p (t n) -> p t n", n=P)
                    act.activation(V, src, ACT.Copy)
                    for j in range(2):
                        for h in range(2):
                            ins = act.activation(VB[64 * h:64 * h + 64, j::2, 64 * h:64 * h + 64],
                                                 src[64 * j:64 * j + 64, :, 64 * h:64 * h + 64], ACT.Copy)
                    ins.then_inc(hg["values"], 1)
                    act.wait_ge(chunk_used, iv + 1)
                    act.activation(SG, PS[4][:], ACT.Silu).then_inc(hg["gate"], 1)
                    for n, (d, hf) in enumerate(U):
                        if hf == 0:
                            if d:
                                act.wait_ge(hg["level"], 24 * p + 12)
                                act.wait_ge(hg["diag"], 4 * p + 2)
                                sigmoids(1)
                            act.wait_ge(hg["forget"], 2 * p + d + 1)
                            act.activation(F, F, ACT.Ln).then_inc(hg["log"], 1)
                            act.wait_ge(hg["cum"], 2 * p + d + 1)
                            if d:
                                act.wait_ge(hg["out"], 16 * p + 8)
                                act.wait_ge(hg["kturn"], 2 * p + 1)
                            act.activation(ET, TL, ACT.Exp)
                            act.activation((QS, KS)[d], CUM, ACT.Exp)
                            act.activation((KS, QS)[d], F, ACT.Exp).then_inc(hg["factor"], 1)
                            act.wait_ge(hg["kturn"], 2 * p + d + 1)
                            if d:
                                act.wait_ge(hg["update"], 2 * p + d)
                            act.activation(KST, PS[6][:].rearrange("p (t n) -> p t n", n=P), ACT.Copy).then_inc(hg["kturned"], 1)
                        for l in range(NL - 1):
                            s = 24 * p + 6 * n + l
                            act.wait_ge(hg["diff"], s + 1)
                            if s % 24 >= 2:
                                act.wait_ge(hg["level"], s - 1)
                            act.activation(EE[l % 2], DD[l % 2], ACT.Exp).then_inc(hg["exp"], 1)
                    act.wait_ge(hg["out"], 16 * p + 16)
                    act.activation(OS, PS[1][:], ACT.Copy).then_inc(hg["out1"], 1)
                    act.wait_ge(hg["osum"], p + 1)
                    act.activation(SQ, OS, ACT.Square).then_inc(hg["square"], 1)
                    act.wait_ge(hg["mean"], p + 1)
                    act.activation(SQ, PS[3][:], ACT.Sqrt, bias=rmseps).then_inc(hg["root"], 1)

                @block.gpsimd
                def _(pool):
                    pool.memset(ST, 0.0).then_inc(hg["clean"], 1)
                    pool.wait_ge(hg["clean"], p + 1)
                    for n, (d, hf) in enumerate(U):
                        pool.wait_ge(hg["cum"], 2 * p + d + 1)
                        if n:
                            pool.wait_ge(hg["diff"], 24 * p + 6 * n)
                        if n >= 2:
                            pool.wait_ge(hg["score"], 16 * p + NCH * (n - 1))
                        for h in range(2):
                            r = slice(64 * h, 64 * h + 64)
                            ins = pool.tensor_copy(KB[n % 2][r, NCH * (NL - 1):, r],
                                                   KK[r, HALF * hf:HALF * hf + HALF].rearrange("p (c s) -> p c s", s=CH))
                        ins.then_inc(hg["diag"], 1)
                        pool.wait_ge(hg["diag"], 4 * p + n + 1)
                        for l, b in enumerate(LEVELS):
                            s = 24 * p + 6 * n + l
                            if s % 24 >= 2:
                                pool.wait_ge(hg["exp"], s - 1)
                            m = b // 2 - 1 + d
                            v = CUM[:, HALF * hf:HALF * hf + HALF].rearrange("p (n b) -> p n b", b=b)
                            o = DD[l % 2].rearrange("p (n b) -> p n b", b=b)
                            ref = v[:, :, m:m + 1].broadcast_to([P, HALF // b, b // 2])
                            pool.tensor_tensor(o[:, :, 0:b // 2], ref, v[:, :, 0:b // 2], ALU.subtract)
                            pool.tensor_tensor(o[:, :, b // 2:], v[:, :, b // 2:], ref, ALU.subtract).then_inc(hg["diff"], 1)

                @block.vector
                def _(dve):
                    dve.wait_ge(hg["query"], p + 1)
                    DV.link(dve.tensor_scalar(HQ, HQ, HD ** -0.5, None, ALU.mult))
                    for n, (d, hf) in enumerate(U):
                        if hf == 0:
                            j = PAIRS * d + p
                            dve.wait_ge(hg["sig"], 2 * p + d + 1)
                            DV.then(dve.tensor_scalar(F, F, omlb[:, j:j + 1], lb[:, j:j + 1], ALU.mult, ALU.add))
                            DV.then(dve.tensor_scalar(KK, KK, omlb[:, j:j + 1], None, ALU.mult))
                            DV.settle()
                            dve.tensor_scalar(F, F, FLOOR, None, ALU.max).then_inc(hg["forget"], 1)
                            dve.wait_ge(hg["log"], 2 * p + d + 1)
                            if d:
                                dve.wait_ge(hg["diff"], 24 * p + 12)
                            DV.link(dve.tensor_tensor_scan(CUM, restart[:], F, 0.0, ALU.mult, ALU.add))
                            c3 = CUM.rearrange("p (c s) -> p c s", s=CH)
                            DV.link(dve.tensor_copy(TL, c3[:, :, CH - 1]))
                            if d:
                                DV.link(dve.tensor_tensor(CUM, CUM, F, ALU.subtract))
                            dve.tensor_tensor(F.rearrange("p (c s) -> p c s", s=CH), TL.unsqueeze(2).broadcast_to([P, NC, CH]),
                                              c3, ALU.subtract).then_inc(hg["cum"], 1)
                            dve.wait_ge(hg["factor"], 2 * p + d + 1)
                            DV.link(dve.tensor_tensor(QS, QS, HQ, ALU.mult))
                            dve.tensor_tensor(KS, KS, KK, ALU.mult).then_inc(hg["inter"], 1)
                        if n >= 2:
                            dve.wait_ge(hg["score"], 16 * p + NCH * (n - 1))
                        for l, b in enumerate(LEVELS):
                            dve.wait_ge(hg["exp"], 24 * p + 6 * n + l + 1)
                            ksl = slice(0, b // 2) if d == 0 else slice(b // 2, b)
                            qsl = slice(b // 2, b) if d == 0 else slice(0, b // 2)
                            blk = lambda v: v.rearrange("p (n b) -> p n b", b=b)
                            dve.tensor_tensor(blk(QB[n % 2][:, l, :])[:, :, qsl], blk(EE[l % 2])[:, :, qsl],
                                              blk(HQ[:, HALF * hf:HALF * hf + HALF])[:, :, qsl], ALU.mult)
                            four = lambda v: v.rearrange("p c (n b) -> p c n b", b=b)
                            for h in range(2):
                                r = slice(64 * h, 64 * h + 64)
                                e3 = EE[l % 2][r, :].rearrange("p (c s) -> p c s", s=CH)
                                k3 = KK[r, HALF * hf:HALF * hf + HALF].rearrange("p (c s) -> p c s", s=CH)
                                ins = dve.tensor_tensor(four(KB[n % 2][r, NCH * l:NCH * l + NCH, r])[:, :, :, ksl],
                                                        four(e3)[:, :, :, ksl], four(k3)[:, :, :, ksl], ALU.mult)
                            ins.then_inc(hg["level"], 1)
                        if hf == 0:
                            dve.wait_ge(hg["update"], 2 * p + d + 1)
                            dve.wait_ge(hg["clean"], p + 1)
                            if d:
                                dve.wait_ge(hg["out"], 16 * p + 8)
                            o = ORDER[d]
                            for h in range(2):
                                DV.then(dve.memset(ST[64 * h:64 * h + 64, o[0], 64 * h:64 * h + 64], 0.0))
                            DV.settle()
                            for q in range(NC - 1):
                                for h in range(2):
                                    r = slice(64 * h, 64 * h + 64)
                                    upd = PS[3 + 2 * (o[q] % 2)][r, P * (o[q] // 2) + 64 * h:P * (o[q] // 2) + 64 * h + 64]
                                    ins = dve.scalar_tensor_tensor(ST[r, o[q + 1], r], ST[r, o[q], r], ET[r, o[q]:o[q] + 1], upd,
                                                                   ALU.mult, ALU.add)
                                    if q < NC - 2 or h == 0:
                                        DV.then(ins)
                                    else:
                                        ins.then_inc(hg["state"], 1)
                                if q < NC - 2:
                                    DV.settle()
                        for c in range(NCH):
                            s = NCH * n + c
                            dve.wait_ge(hg["score"], 16 * p + s + 1)
                            dve.tensor_tensor(MK[s % 2], PS[4 * (s % 2)][:, 0:NL * CH].rearrange("p (l t) -> p l t", t=CH),
                                              lm[:, NL * d:NL * d + NL, :], ALU.mult).then_inc(hg["masked"], 1)
                            dve.wait_ge(hg["masked"], 16 * p + s + 1)
                            if s >= 2:
                                dve.wait_ge(hg["out"], 16 * p + s - 1)
                            dve.tensor_reduce(SM[s % 2], MK[s % 2].rearrange("p l t -> p t l"), AX_X, ALU.add).then_inc(hg["summed"], 1)
                    dve.wait_ge(hg["out1"], p + 1)
                    dve.tensor_tensor(OS, PS[7][:], OS, ALU.add).then_inc(hg["osum"], 1)
                    dve.wait_ge(hg["root"], p + 1)
                    DV.link(dve.reciprocal(SQ, SQ))
                    DV.link(dve.tensor_tensor(OS, OS, SQ, ALU.mult))
                    for s in range(2):
                        tokens = lambda v: v[:, HALF * s:HALF * s + HALF].rearrange("p (i n) -> p i n", n=CH)
                        dve.scalar_tensor_tensor(by_tile(mixT[:, PAIRS + p, :])[:, s], tokens(OS), normg, tokens(SG), ALU.mult, ALU.mult)

        def clean_levels():
            with nc.Block() as block:
                @block.gpsimd
                def _(pool):
                    pool.memset(A[:, 0:11264], 0.0)

        EB = [cut(W, 0, EXPERT), cut(W, EXPERT, EXPERT)]

        def expert_view(b):
            return (cut(W, EXPERT * b, KD, HID), cut(W, EXPERT * b + KD * HID, KD, HID), cut(W, EXPERT * b + 2 * KD * HID, 2, D))

        Y = cut(A, 4096, NT, D)
        HS = [cut(A, 8192 + 1024 * i, 2, 512) for i in range(2)]
        HB = [cut(A, 10240 + 1024 * i, 2, 512) for i in range(2)]
        RW, RB = cut(A, 12288, KD, E), cut(A, 12800, E)
        SC, BI, HOT, IDX = cut(A, 12864, E), cut(A, 12928, E), cut(A, 12992, E), cut(A, 13056, 8)
        TOP = cut(A, 13064, 8)
        IDF = cut(A, 13072, 8)

        def moe(tag, l, nt, lhs, n_tok):
            r_in, rprod, sig = sem("r_in" + tag), sem("r_prod" + tag), sem("r_sig" + tag)
            picked = sem("r_picked" + tag)
            w_in = [sem(f"expert_in{b}" + tag) for b in range(2)]
            up, act_done, mul, down, added = (sem(n + tag) for n in ("moe_up", "moe_silu", "moe_mul", "moe_down", "moe_added"))
            G = cut(gates, 0, NT, E)
            sources = lambda e: (rows(a["exp_w_gate"][l][e]), rows(a["exp_w_up"][l][e]), nat(a["exp_w_down"][l][e]))
            with nc.Block() as block:
                @block.sync
                def _(sp):
                    sp.dma_start(RW, rows(a["router_w"][l])).then_inc(r_in, 16)
                    sp.dma_start(RB, a["router_bias"][l:l + 1, :].broadcast_to([P, E])).then_inc(r_in, 16)
                    for v, w in zip(expert_view(0), (rows(a["sh_w_gate"][l]), rows(a["sh_w_up"][l]), nat(a["sh_w_down"][l]))):
                        sp.dma_start(v, w).then_inc(w_in[0], 16)
                    for v, w in zip(expert_view(1), (rows(a["exp_w_gate"][l, 0]), rows(a["exp_w_up"][l, 0]), nat(a["exp_w_down"][l, 0]))):
                        sp.dma_start(v, w).then_inc(w_in[1], 16)

                @block.tensor
                def _(pe):
                    pe.wait_ge(r_in, 32)
                    for i in range(nt):
                        for k in range(KD):
                            mm = pe.matmul(PS[i][:, 0:E], lhs(HT[:], k, i), RW[:, k, :], start=(k == 0), stop=(k == KD - 1))
                        mm.then_inc(rprod, 1)

                @block.scalar
                def _(act):
                    for i in range(nt):
                        act.wait_ge(rprod, i + 1)
                        act.activation(G[:, i, :], PS[i][:, 0:E], ACT.Sigmoid).then_inc(sig, 1)

                @block.vector
                def _(dve):
                    dve.wait_ge(r_in, 32)
                    for i in range(nt):
                        dve.wait_ge(sig, i + 1)
                        DV.link(dve.tensor_tensor(BI, G[:, i, :], RB, ALU.add))
                        DV.link(dve.max(TOP, BI))
                        DV.link(dve.max_index(IDX.bitcast(U32), TOP, BI))
                        DV.link(dve.tensor_copy(IDF, IDX.bitcast(U32)))
                        for j in range(TOPK):
                            if j == 0:
                                DV.link(dve.tensor_scalar(HOT, iota[:], IDF[:, 0:1], None, ALU.is_equal))
                            else:
                                DV.link(dve.scalar_tensor_tensor(HOT, iota[:], IDF[:, j:j + 1], HOT, ALU.is_equal, ALU.add))
                        DV.link(dve.tensor_tensor(SC, G[:, i, :], HOT, ALU.mult))
                        DV.link(dve.tensor_reduce(stats[:, 0:1], SC, AX_X, ALU.add))
                        DV.link(dve.reciprocal(stats[:, 1:2], stats[:, 0:1]))
                        DV.link(dve.tensor_scalar(G[:, i, :], SC, stats[:, 1:2], ROUTED_SCALE, ALU.mult, ALU.mult))

            def pe_expert(pe, b, x0, x1):
                wg, wu, wd = expert_view(b)
                pe.wait_ge(w_in[b], 48 * x1 + 48)
                for m in range(2):
                    for n, w in enumerate((wg, wu)):
                        for k in range(KD):
                            mm = pe.matmul(PS[2 * m + n][:, 0:n_tok], w[:, k, P * m:P * m + P], HTt[:, k, 0:n_tok], start=(k == 0), stop=(k == KD - 1))
                    mm.then_inc(up, 1)
                for i in range(nt):
                    for n in range(2):
                        j = 2 * i + n
                        if j == 0:
                            pe.wait_ge(mul, 2 * x0 + 2)
                        for m in range(2):
                            mm = pe.matmul(PS[4 + j % 4][:], lhs2(HB[b], m, i), wd[:, m, 512 * n:512 * n + 512], start=(m == 0), stop=(m == 1))
                        mm.then_inc(down, 1)
                        if j + 1 < 2 * nt and j + 1 >= 4:
                            pe.wait_ge(added, 2 * nt * x0 + j - 2)

            lhs2 = lambda t, m, i: t[:, m, P * i:P * i + P]

            def act_expert(act, b, x0):
                for m in range(2):
                    act.wait_ge(up, 2 * x0 + m + 1)
                    act.activation(HS[b][:, m, 0:n_tok], PS[2 * m][:, 0:n_tok], ACT.Silu).then_inc(act_done, 1)

            def dve_expert(dve, b, x0, gate):
                for m in range(2):
                    dve.wait_ge(act_done, 2 * x0 + m + 1)
                    dve.tensor_tensor(HB[b][:, m, 0:n_tok], HS[b][:, m, 0:n_tok], PS[2 * m + 1][:, 0:n_tok], ALU.mult).then_inc(mul, 1)
                for i in range(nt):
                    for n in range(2):
                        j = 2 * i + n
                        y = Y[:, i, 512 * n:512 * n + 512]
                        dve.wait_ge(down, 2 * nt * x0 + j + 1)
                        if gate is None:
                            dve.tensor_copy(y, PS[4 + j % 4][:]).then_inc(added, 1)
                        else:
                            dve.scalar_tensor_tensor(y, PS[4 + j % 4][:], gate(i), y, ALU.mult, ALU.add).then_inc(added, 1)

            with nc.Block() as block:
                @block.sync
                def _(sp):
                    with sp.Fori(0, E // 2 - 1) as r:
                        for b in range(2):
                            sp.wait_ge(down, 2 * nt * 2 * r + 2 * nt * (b + 1))
                            for v, w in zip(expert_view(b), ("exp_w_gate", "exp_w_up", "exp_w_down")):
                                lay = nat if w == "exp_w_down" else rows
                                src = a[w][l][bass.ds(2 * r + 1 + b, 1)]
                                src = src.rearrange("e (k p) n -> p (e k) n", p=P) if lay is nat else src.rearrange("e (p k) n -> p (e k) n", k=KD)
                                sp.dma_start(v, src).then_inc(w_in[b], 16)
                    sp.wait_ge(down, 2 * nt * (E - 1))
                    for v, w in zip(expert_view(0), sources(E - 1)):
                        sp.dma_start(v, w).then_inc(w_in[0], 16)

                @block.tensor
                def _(pe):
                    pe_expert(pe, 0, 0, 0)
                    with pe.Fori(0, E // 2) as r:
                        pe.wait_ge(added, 4 * nt * r + 2 * nt)
                        pe_expert(pe, 1, 2 * r + 1, r)
                        pe.wait_ge(added, 4 * nt * r + 4 * nt)
                        pe_expert(pe, 0, 2 * r + 2, r + 1)

                @block.scalar
                def _(act):
                    act_expert(act, 0, 0)
                    with act.Fori(0, E // 2) as r:
                        act_expert(act, 1, 2 * r + 1)
                        act_expert(act, 0, 2 * r + 2)

                @block.vector
                def _(dve):
                    dve_expert(dve, 0, 0, None)
                    with dve.Fori(0, E // 2) as r:
                        dve.wait_ge(added, 4 * nt * r + 2 * nt)
                        dve_expert(dve, 1, 2 * r + 1, lambda i: G[:, i, bass.ds(2 * r, 1)])
                        dve.wait_ge(added, 4 * nt * r + 4 * nt)
                        dve_expert(dve, 0, 2 * r + 2, lambda i: G[:, i, bass.ds(2 * r + 1, 1)])

        KJ = D // P
        GY = cut(A, 0, KJ, HALF)
        BD = cut(A, 8192, 4 * KJ, P)
        M1 = cut(A, 12288, KJ, HALF)
        obuf = lambda n: cut(A, 2048 + 512 * n, T)
        RR, II, AA, TT = ([obuf(2 * q + n) for n in range(2)] for q in range(4))
        UC, HH = ([obuf(8 + 2 * q + n) for n in range(2)] for q in range(2))
        coef, ncoef = small[:, 225:241], small[:, 48:64]
        lw = [cut(gates, 16 * n, 16) for n in range(4)]
        od = {n: sem("od_" + n) for n in ("zero", "bd_in", "y", "gelu", "u", "conv", "ga", "gates", "decay", "iu", "ratio",
                                          "root", "scan", "lam")}

        def recurrent_unit():
            with nc.Block() as block:
                @block.sync
                def _(sp):
                    for kind, w in enumerate(("lru_w_a", "lru_w_x")):
                        for d in range(2):
                            for h in range(2):
                                r = slice(64 * h, 64 * h + 64)
                                at = 16 * kind + 8 * d
                                sp.dma_start(BD[r, at:at + KJ, r], a[w][0, d].rearrange("(j h) r c -> h r j c", h=2)[h]).then_inc(od["bd_in"], 16)
                    send(sp, odi[3] + 1 + SLOTS)

                @block.tensor
                def _(pe):
                    for c in range(2):
                        arrived(pe, odi[c])
                        for q in range(4):
                            j = 4 * c + q
                            if j >= 2:
                                pe.wait_ge(od["gelu"], j - 1)
                            for k in range(KD):
                                mm = pe.matmul(PS[6 + j % 2][:, 0:HALF], view(odi[c])[:, k, P * q:P * q + P], HTt[:, k, HALF:T],
                                               start=(k == 0), stop=(k == KD - 1))
                            mm.then_inc(chunk_used if q == 3 else od["y"], 1)

                    def u_product(j):
                        c, q = 2 + j // 4, j % 4
                        if q == 0:
                            arrived(pe, odi[c])
                        if j >= 2:
                            pe.wait_ge(od["conv"], j - 1)
                        for k in range(KD):
                            mm = pe.matmul(PS[j % 2][:], view(odi[c])[:, k, P * q:P * q + P], HTt[:, k, :], start=(k == 0), stop=(k == KD - 1))
                        mm.then_inc(chunk_used if q == 3 else od["u"], 1)

                    u_product(0)
                    pe.wait_ge(od["bd_in"], 16 * 8)
                    for j in range(KJ):
                        if j + 1 < KJ:
                            u_product(j + 1)
                        pe.wait_ge(od["conv"], j + 1)
                        for d in range(2):
                            s = 2 * j + d
                            if s >= 2:
                                pe.wait_ge(od["gates"], s - 1)
                            for kind in range(2):
                                mm = pe.matmul(PS[2 + 2 * (s % 2) + kind][:], BD[:, 16 * kind + 8 * d + j, :], UC[j % 2], start=True, stop=True)
                            mm.then_inc(od["ga"], 1)

                @block.scalar
                def _(act):
                    act.activation(lw[0], lam, ACT.Abs).then_inc(od["lam"], 1)
                    act.wait_ge(od["lam"], 1)
                    act.activation(lw[0], lw[0], ACT.Exp, scale=-1.0).then_inc(od["lam"], 1)
                    for j in range(KJ):
                        if j % 4 == 3:
                            act.wait_ge(chunk_used, odi[j // 4] + 1)
                        else:
                            act.wait_ge(od["y"], 3 * (j // 4) + j % 4 + 1)
                        act.activation(GY[:, j, :], PS[6 + j % 2][:, 0:HALF], ACT.Gelu_apprx_tanh).then_inc(od["gelu"], 1)
                    act.wait_ge(od["lam"], 3)

                    def root(s):
                        act.wait_ge(od["ratio"], s + 1)
                        act.activation(RR[s % 2], TT[s % 2], ACT.Sqrt, scale=2.0).then_inc(od["root"], 1)

                    for s in range(2 * KJ):
                        j, d = s // 2, s % 2
                        act.wait_ge(od["ga"], s + 1)
                        if s >= 2:
                            act.wait_ge(od["scan"], s - 1)
                        n = 8 * d + j
                        AC.then(act.activation(RR[s % 2], PS[2 + 2 * (s % 2)][:], ACT.Sigmoid, bias=gbias[:, n:n + 1]))
                        act.activation(II[s % 2], PS[3 + 2 * (s % 2)][:], ACT.Sigmoid, bias=gbias[:, 16 + n:17 + n]).then_inc(od["gates"], 1)
                        AC.settle()
                        act.activation(AA[s % 2], RR[s % 2], ACT.Exp, scale=coef[:, n:n + 1])
                        act.activation(TT[s % 2], RR[s % 2], ACT.Tanh, scale=ncoef[:, n:n + 1]).then_inc(od["decay"], 1)
                        root(s)

                @block.gpsimd
                def _(pool):
                    for s in range(2 * KJ):
                        pool.wait_ge(od["gates"], s + 1)
                        pool.tensor_tensor(II[s % 2], II[s % 2], UC[(s // 2) % 2], ALU.mult).then_inc(od["iu"], 1)

                @block.vector
                def _(dve):
                    e, z, z2, q = lw
                    dve.wait_ge(od["lam"], 2)
                    DV.link(dve.tensor_scalar(z, e, 2.0, None, ALU.add))
                    DV.link(dve.reciprocal(z, z))
                    DV.link(dve.tensor_tensor(z, z, e, ALU.mult))
                    DV.link(dve.tensor_tensor(z2, z, z, ALU.mult))
                    DV.link(dve.tensor_scalar(q, z2, 1 / 15, None, ALU.mult))
                    for n in (13, 11, 9, 7, 5, 3):
                        DV.link(dve.scalar_tensor_tensor(q, q, 1 / n, z2, ALU.add, ALU.mult))
                    DV.link(dve.scalar_tensor_tensor(q, q, 1.0, z, ALU.add, ALU.mult))
                    DV.link(dve.tensor_scalar(z, lam, -1.0, 0.0, ALU.mult, ALU.max))
                    DV.link(dve.scalar_tensor_tensor(q, q, 2.0, z, ALU.mult, ALU.add))
                    DV.link(dve.tensor_scalar(coef, q, -LRU_C, None, ALU.mult))
                    dve.tensor_scalar(ncoef, q, LRU_C, None, ALU.mult).then_inc(od["lam"], 1)

                    def conv(j):
                        if j % 4 == 3:
                            dve.wait_ge(chunk_used, odi[2 + j // 4] + 1)
                        else:
                            dve.wait_ge(od["u"], 3 * (j // 4) + j % 4 + 1)
                        if j >= 2:
                            dve.wait_ge(od["iu"], 2 * (j - 1))
                        u = PS[j % 2][:].rearrange("p (s n) -> p s n", s=2)
                        o = UC[j % 2].rearrange("p (s n) -> p s n", s=2)
                        DV.link(dve.tensor_scalar(UC[j % 2], PS[j % 2][:], convw[:, 16 + j:17 + j], convb[:, j:j + 1], ALU.mult, ALU.add))
                        for tap, shift in ((0, -2), (1, -1), (3, 1)):
                            lo, hi = max(0, -shift), HALF - max(0, shift)
                            ins = dve.scalar_tensor_tensor(o[:, :, lo:hi], u[:, :, lo + shift:hi + shift], convw[:, 8 * tap + j:8 * tap + j + 1],
                                                           o[:, :, lo:hi], ALU.mult, ALU.add)
                            if tap == 3:
                                ins.then_inc(od["conv"], 1)
                            else:
                                DV.link(ins)

                    conv(0)
                    for s in range(2 * KJ):
                        j, d = s // 2, s % 2
                        x = s % 2
                        if d == 0 and j + 1 < KJ:
                            conv(j + 1)
                        dve.wait_ge(od["decay"], s + 1)
                        DV.link(dve.tensor_scalar(HH[d], TT[x], 1.0, None, ALU.add))
                        DV.link(dve.reciprocal(HH[d], HH[d]))
                        dve.tensor_tensor(TT[x], TT[x], HH[d], ALU.mult).then_inc(od["ratio"], 1)
                        dve.wait_ge(od["iu"], s + 1)
                        dve.wait_ge(od["root"], s + 1)
                        DV.link(dve.tensor_tensor(II[x], II[x], RR[x], ALU.mult))
                        if d == 0:
                            dve.tensor_tensor_scan(HH[0], AA[x], II[x], 0.0, ALU.mult, ALU.add).then_inc(od["scan"], 1)
                        else:
                            back = lambda v, q: v[:, HALF * q:HALF * q + HALF][:, ::-1]
                            DV.link(dve.tensor_tensor_scan(back(HH[1], 0), back(AA[x], 0), back(II[x], 0), 0.0, ALU.mult, ALU.add))
                            dve.tensor_tensor_scan(back(HH[1], 1), back(AA[x], 1), back(II[x], 1), HH[1][:, 0:1], ALU.mult, ALU.add).then_inc(od["scan"], 1)
                            dve.wait_ge(od["scan"], s + 1)
                            DV.link(dve.tensor_tensor(HH[0][:, HALF:T], HH[0][:, HALF:T], HH[1][:, HALF:T], ALU.add))
                            DV.link(dve.tensor_tensor(M1[:, j, :], HH[0][:, HALF:T], GY[:, j, :], ALU.mult))

        def clear_gate_weights():
            with nc.Block() as block:
                @block.gpsimd
                def _(pool):
                    pool.memset(A[:, 8192:12288], 0.0)

        def pack_latent():
            with nc.Block() as block:
                @block.vector
                def _(dve):
                    for i in range(2):
                        for s in range(2):
                            DV.link(dve.tensor_copy(Xt[64 * s:64 * s + 64, i, :], Xt[64:128, 2 * i + s, :]))

        def store():
            stored = sem("stored")
            with nc.Block() as block:
                @block.sync
                def _(sp):
                    for i in range(2):
                        sp.dma_start(out[P * i:P * i + P, :], Xt[:, i, :]).then_inc(stored, 16)
                    sp.wait_ge(stored, 32)


        def stop():
            with nc.Block() as block:
                @block.sync
                def _(sp):
                    for i in range(max(0, sent[0] - SLOTS), sent[0]):
                        arrived(sp, i)

        replicate("0", True)
        modulation(0, range(12))
        modulate("a0", 0, 1, NT, True, na_w[0] + SLOTS)
        if "stop1" in debug:
            return stop()
        clean_levels()
        for p in range(PAIRS):
            attention(p)
            hgrn(p)
        if "stop2" in debug:
            return stop()
        project_out("e0", evo, A[:, 12032:16128], 2, NT, plain_cols, len(chunks))
        residual_norm("e0", 0, 0, NT, H, None, 0)
        if "stop3" in debug:
            return stop()
        modulate("b0", 3, 4, NT, False, 0)
        moe("m0", 0, NT, plain_cols, T)
        if "stop4" in debug:
            return stop()
        residual_norm("f0", 0, 1, NT, Y, 5, 0)

        limit[0] = moe1_at
        clear_gate_weights()
        modulation(1, range(4))
        modulate("a1", 0, 1, NT, True, odi[0] + SLOTS)
        recurrent_unit()
        replicate("1", False)
        modulation(1, range(4, 12))
        pack_latent()
        if "stop5" in debug:
            return stop()
        project_out("o1", odo, A[:, 12288:14336], 2, 2, lambda t, k, i: t[:, HALF * k + P * i:HALF * k + P * i + P], len(chunks))
        residual_norm("e1", 1, 0, 2, H, None, 0)
        modulate("b1", 3, 4, 2, False, 0)
        moe("m1", 1, 2, plain_cols, HALF)
        residual_norm("f1", 1, 1, 2, Y, 5, 0)
        store()


def _constants(np):
    f = np.float32
    head = np.arange(P) // HD
    lev = np.zeros((2, NL, HD, CH), f)
    s, t = np.meshgrid(np.arange(CH), np.arange(CH), indexing="ij")
    for l, b in enumerate(LEVELS):
        same = (s // b) == (t // b)
        lev[0, l] = same & (s % b < b // 2) & (t % b >= b // 2)
        lev[1, l] = same & (s % b >= b // 2) & (t % b < b // 2)
    lev[:, NL - 1] = s == t
    lev = np.concatenate([lev, lev], 2).transpose(2, 0, 1, 3).reshape(P, -1)
    restart = np.tile((np.arange(T) % CH != 0).astype(f), (P, 1))
    w = np.arange(CH)
    lo = np.clip(w - 8, 0, CH - 16)[:, None]
    inside = (w[None] >= lo) & (w[None] < lo + 16)
    window = np.where(inside, 0.0, -1e30).astype(f)
    return {
        "k_ident": np.eye(P, dtype=f),
        "k_ones64": (head[:, None] == head[None]).astype(f) / HD,
        "k_levmask": np.ascontiguousarray(lev),
        "k_restart": restart,
        "k_iota": np.tile(np.arange(E, dtype=f), (P, 1)),
        "k_window": np.concatenate([window, window]),
    }


def _bias_layout(rpb, np):
    w = np.arange(CH)
    at = np.clip(w[None, :] - w[:, None] + 15, 0, 30)
    band = rpb[:, :, at]
    first, second = band[:, 5:11], band[:, 4:10]
    both = np.concatenate([first.transpose(2, 0, 1, 3), second.transpose(2, 0, 1, 3)])
    return np.ascontiguousarray(both)


def _vectors(given, np):
    turn = lambda v: v.reshape(-1, P).T
    norm = np.concatenate([given["hg_norm_g"][0]] * 2)
    return np.ascontiguousarray(np.concatenate([turn(v) for v in (
        given["hg_lb_raw"], norm, given["od_conv_w"], given["od_conv_b"], given["lru_b_a"], given["lru_b_x"],
        given["lru_lam"])], 1))


_INS = ["x", "c", "ctx", "c_ctx", "ada_w", "ada_b", "ln_g", "ln_b", "ev_w_in", "ev_w_out", "od_w_in", "lru_w_a", "lru_w_x", "od_w_out",
        "router_w", "router_bias", "exp_w_gate", "exp_w_up", "exp_w_down", "sh_w_gate", "sh_w_up", "sh_w_down"]


def kernel(**inputs):
    import numpy as _np
    import concourse.bacc as _bacc
    from concourse.bass_utils import run_bass_kernel_spmd as _run

    nc = _bacc.Bacc("TRN2", target_bir_lowering=False, num_devices=1)
    arrays, args = {}, {}
    given = {n: _np.ascontiguousarray(inputs[n]) for n in _INS}
    given["rpb_band"] = _bias_layout(_np.asarray(inputs["na_rpb"])[0], _np)
    given["vectors"] = _vectors({n: _np.asarray(inputs[n]) for n in inputs}, _np)
    given.update(_constants(_np))
    for name, v in given.items():
        arrays["in_" + name] = v
        args[name] = nc.dram_tensor("in_" + name, v.shape, F32, kind="ExternalInput").ap()
    out = nc.dram_tensor("out", (HALF, D), F32, kind="ExternalOutput").ap()
    trunk(nc, args, out)
    r = _run(nc, [arrays], core_ids=[0])
    return r.results[0]["out"].reshape(1, HALF, D)
```

```python
from contextlib import ExitStack

import numpy as np

import concourse.bass as bass
from concourse import mybir

F32 = mybir.dt.float32
U32 = mybir.dt.uint32
ALU = mybir.AluOpType
ACT = mybir.ActivationFunctionType
AX_X = mybir.AxisListType.X

P = 128
D = 1024
KD = D // P
T = 512
HALF = 256
NT = T // P
CH = 64
NC = T // CH
HD = 64
PAIRS = 4
LEVELS = (64, 32, 16, 8, 4, 2)
NL = len(LEVELS) + 1
E = 64
HID = 256
TOPK = 6
ROUTED_SCALE = 2.5
ALPHA = 4 ** 0.25
LN_EPS = 1e-5
RMS_EPS = 1e-6
FLOOR = 1e-30
LRU_C = 8.0
SLOT = KD * 512
SLOTS = 3
EXPERT = KD * 512 + 2 * D


class Chain:

    def __init__(self, eng, sem):
        self.eng, self.sem, self.n = eng, sem, 0

    def then(self, ins):
        self.n += 1
        ins.then_inc(self.sem, 1)

    def settle(self):
        self.eng.wait_ge(self.sem, self.n)

    def link(self, ins):
        self.then(ins)
        self.settle()


def trunk(nc, a, out, debug=()):
    ctx = ExitStack()
    with ctx:
        def sb(name, words):
            return ctx.enter_context(nc.sbuf_tensor(name, [P, words], F32))

        def sem(name):
            return ctx.enter_context(nc.semaphore(name))

        W = sb("W", 18432)
        X = sb("X", NT * D)
        MOD = sb("MOD", 6 * D)
        HT = sb("HT", KD * T)
        A = sb("A", 16128)
        ident = sb("ident", P)
        ones64 = sb("ones64", P)
        levmask = sb("levmask", 2 * NL * CH)
        restart = sb("restart", T)
        iota_s = sb("iota", P)
        iota = iota_s[:, 0:E]
        onesf = sb("onesf", P)
        half = sb("half", 268)
        CR = sb("CR", KD * P)
        small = sb("small", 256)
        gates = sb("gates", NT * E)
        PS = [ctx.enter_context(nc.psum_tensor(f"PS{i}", [P, 512], F32)) for i in range(8)]

        def cut(t, at, *dims):
            n = 1
            for d in dims:
                n *= d
            v = t[:, at:at + n]
            if len(dims) == 2:
                return v.rearrange("p (a b) -> p a b", b=dims[1])
            if len(dims) == 3:
                return v.rearrange("p (a b c) -> p a b c", b=dims[1], c=dims[2])
            return v

        Xt = cut(X, 0, NT, D)
        HTt = cut(HT, 0, KD, T)
        eps = small[:, 0:1]
        pcols = small[:, 241:244]
        rmseps = small[:, 1:2]
        cT = small[:, 8:24]
        lbr = small[:, 128:136]
        normg = small[:, 136:137]
        convw = small[:, 137:169]
        convb = small[:, 169:177]
        gbias = small[:, 177:209]
        lam = small[:, 209:225]
        lb = small[:, 32:40]
        omlb = small[:, 40:48]
        stats = small[:, 64:64 + 12]
        mv = small[:, 80:82]
        rstd = small[:, 82:84]
        chain = {n: sem("chain_" + n) for n in ("dve", "act", "pool")}
        DV = Chain(nc.vector, chain["dve"])
        AC = Chain(nc.scalar, chain["act"])
        GP = Chain(nc.gpsimd, chain["pool"])

        chunks = []

        def chunk(*parts):
            chunks.append(parts)
            return len(chunks) - 1

        rows = lambda w: w.rearrange("(p k) n -> p k n", k=KD)
        ada_chunk = lambda l, n: chunk(rows(a["ada_w"][l])[:, :, 512 * n:512 * n + 512])
        ada = [[ada_chunk(0, n) for n in range(12)], []]
        ev = rows(a["ev_w_in"][0])
        col = lambda part, p: ev[:, :, 512 * part + P * p:512 * part + P * p + P]
        na_w, hz_w, hv_w = [], [], []
        for p in range(PAIRS):
            na_w.append(chunk(col(0, p), col(1, p), col(2, p)))
            hz_w.append(chunk(col(3, p), col(4, p), col(5, p)))
            hv_w.append(chunk(col(6, p), col(7, p)))
        nat = lambda w: w.rearrange("(k p) n -> p k n", p=P)
        evo = [chunk(nat(a["ev_w_out"][0])[:, :, 512 * n:512 * n + 512]) for n in range(2)]
        moe0_at = len(chunks)
        ada[1] += [ada_chunk(1, n) for n in range(4)]
        odi = [chunk(rows(a["od_w_in"][0])[:, :, 512 * n:512 * n + 512]) for n in range(4)]
        ada[1] += [ada_chunk(1, n) for n in range(4, 12)]
        odo = [chunk(nat(a["od_w_out"][0])[:, :, 512 * n:512 * n + 512]) for n in range(2)]
        moe1_at = len(chunks)

        slot_sem = [sem(f"slot{i}") for i in range(SLOTS)]
        chunk_used = sem("chunk_used")
        landed, count = [], [0] * SLOTS
        for i, parts in enumerate(chunks):
            count[i % SLOTS] += 16 * len(parts)
            landed.append(count[i % SLOTS])
        sent, limit = [0], [moe0_at]

        def view(i, part=0):
            at = SLOT * (i % SLOTS)
            for q in chunks[i][:part]:
                at += q.shape[1] * q.shape[2]
            return cut(W, at, *chunks[i][part].shape[1:])

        def send(sp, upto):
            while sent[0] < min(upto, limit[0]):
                i = sent[0]
                if i >= SLOTS:
                    sp.wait_ge(chunk_used, i - SLOTS + 1)
                for j, q in enumerate(chunks[i]):
                    sp.dma_start(view(i, j), q).then_inc(slot_sem[i % SLOTS], 16)
                sent[0] += 1

        def arrived(eng, i):
            eng.wait_ge(slot_sem[i % SLOTS], landed[i])

        with nc.Block() as block:
            const = sem("const")
            cond = sem("cond")

            @block.sync
            def _(sp):
                sp.dma_start(cut(small, 8, 8), a["c_ctx"].rearrange("(p k) -> p k", k=KD)).then_inc(const, 16)
                sp.dma_start(cut(small, 16, 8), a["c"][0].rearrange("(p k) -> p k", k=KD)).then_inc(const, 16)
                send(sp, 3)
                for t, name in ((ident, "k_ident"), (ones64, "k_ones64"), (levmask, "k_levmask"),
                                (restart, "k_restart"), (iota_s, "k_iota")):
                    sp.dma_start(t[:], a[name]).then_inc(const, 16)
                sp.dma_start(pcols, a["k_columns"]).then_inc(const, 16)
                sp.dma_start(A[:, 0:P + 8], a["k_order"]).then_inc(const, 16)
                for s, name in enumerate(("ctx", "x")):
                    sp.dma_start(Xt[64 * s:64 * s + 64], a[name][0].rearrange("(i n) d -> n i d", n=CH)).then_inc(const, 16)
                sp.dma_start(small[:, 128:225], a["vectors"]).then_inc(const, 16)
                sp.wait_ge(const, 16 * 12)

            @block.gpsimd
            def _(pool):
                pool.memset(A[:, 256:], 0.0)
                pool.memset(onesf[:], 1.0)
                pool.memset(small[:, 0:1], LN_EPS)
                pool.memset(small[:, 1:2], RMS_EPS)

            @block.vector
            def _(dve):
                dve.wait_ge(const, 16 * 12)
                f16 = lambda lo, hi: half[:, lo:hi].bitcast(mybir.dt.float16)
                dve.tensor_copy(f16(0, 64), A[:, 0:P])
                dve.memset(f16(64, 128), 1.0)
                dve.tensor_copy(f16(128, 132), A[:, P:P + 8])

            @block.scalar
            def _(act):
                act.wait_ge(const, 16 * 12)
                act.activation(cT, cT, ACT.Silu).then_inc(cond, 1)

        def replicate(tag, split):
            with nc.Block() as block:
                @block.vector
                def _(dve):
                    cr = cut(CR, 0, KD, P)
                    if split:
                        dve.tensor_copy(cr[:, :, 0:64], cT[:, 0:8].unsqueeze(2).broadcast_to([P, KD, 64]))
                    else:
                        dve.tensor_copy(cr[:, :, 0:64], cT[:, 8:16].unsqueeze(2).broadcast_to([P, KD, 64]))
                    dve.tensor_copy(cr[:, :, 64:128], cT[:, 8:16].unsqueeze(2).broadcast_to([P, KD, 64]))

        with nc.Block() as block:
            lbs = sem("lbs")

            @block.vector
            def _(dve):
                DV.link(dve.tensor_tensor(lb, lbr, lbr, ALU.subtract))
                dve.wait_ge(cond, 1)
                dve.nop().then_inc(lbs, 1)
                dve.wait_ge(lbs, 2)
                DV.link(dve.reciprocal(omlb, lb))
                DV.link(dve.tensor_tensor(lb, lb, omlb, ALU.mult))
                DV.link(dve.tensor_tensor(lb, lb, lb, ALU.subtract))
                DV.link(dve.tensor_scalar(omlb, lb, -1.0, 1.0, ALU.mult, ALU.add))

            @block.scalar
            def _(act):
                act.wait_ge(lbs, 1)
                act.activation(lb, lb, ACT.Exp).then_inc(lbs, 1)

        def modulation(l, ns):
            bias_in, prod, added = sem(f"bias_in{l}{ns[0]}"), sem(f"mod_prod{l}{ns[0]}"), sem(f"mod_added{l}{ns[0]}")
            cr = cut(CR, 0, KD, P)
            lo, hi = 512 * ns[0], 512 * ns[-1] + 512
            with nc.Block() as block:
                @block.sync
                def _(sp):
                    sp.dma_start(MOD[:, lo:hi], a["ada_b"][l:l + 1, lo:hi].broadcast_to([P, hi - lo])).then_inc(bias_in, 16)
                    send(sp, ada[l][ns[-1]] + 1 + SLOTS)

                @block.tensor
                def _(pe):
                    for j, n in enumerate(ns):
                        i = ada[l][n]
                        arrived(pe, i)
                        if j >= 4:
                            pe.wait_ge(added, j - 3)
                        for k in range(KD):
                            mm = pe.matmul(PS[j % 4][:], cr[:, k, :], view(i)[:, k, :], start=(k == 0), stop=(k == KD - 1))
                        mm.then_inc(chunk_used, 1)

                @block.vector
                def _(dve):
                    dve.wait_ge(bias_in, 16)
                    for j, n in enumerate(ns):
                        dve.wait_ge(chunk_used, ada[l][n] + 1)
                        m = MOD[:, 512 * n:512 * n + 512]
                        dve.tensor_tensor(m, PS[j % 4][:], m, ALU.add).then_inc(added, 1)

        H = cut(A, 0, NT, D)

        def modulate(tag, shift, scale, nt, mixed, upto):
            h_ready, turned, copied = sem("h_ready" + tag), sem("turned" + tag), sem("copied" + tag)
            if mixed:
                cols = HT[:].rearrange("p (k s i n) -> p k s i n", k=KD, s=2, i=NT)
            with nc.Block() as block:
                @block.sync
                def _(sp):
                    send(sp, upto)

                @block.vector
                def _(dve):
                    for i in range(nt):
                        DV.link(dve.scalar_tensor_tensor(H[:, i, :], MOD[:, D * scale:D * scale + D], 1.0, Xt[:, i, :], ALU.add, ALU.mult))
                        dve.tensor_tensor(H[:, i, :], H[:, i, :], MOD[:, D * shift:D * shift + D], ALU.add).then_inc(h_ready, 1)

                @block.tensor
                def _(pe):
                    for i in range(nt):
                        pe.wait_ge(h_ready, i + 1)
                        h = H[:, i, :].rearrange("t (p k) -> t k p", k=KD)
                        for g in range(2):
                            b = (2 * i + g) % 4
                            if 2 * i + g >= 4:
                                pe.wait_ge(copied, 2 * i + g - 3)
                            for k in range(4):
                                tr = pe.transpose(PS[b][:, P * k:P * k + P], h[:, 4 * g + k, :], ident[:])
                            tr.then_inc(turned, 1)

                @block.scalar
                def _(act):
                    for i in range(nt):
                        for g in range(2):
                            act.wait_ge(turned, 2 * i + g + 1)
                            src = PS[(2 * i + g) % 4]
                            if mixed:
                                for s in range(2):
                                    ins = act.activation(cols[:, 4 * g:4 * g + 4, s, i, :],
                                                         src[:].rearrange("p (k s n) -> p k s n", s=2, n=CH)[:, :, s, :], ACT.Copy)
                            else:
                                ins = act.activation(HTt[:, 4 * g:4 * g + 4, P * i:P * i + P],
                                                     src[:].rearrange("p (k n) -> p k n", n=P), ACT.Copy)
                            ins.then_inc(copied, 1)

        LNG, LNB = cut(A, 8192, D), cut(A, 8192 + D, D)

        def project_out(tag, cks, srcT, gate, nt, lhs, upto):
            done, freed = sem("out_done" + tag), sem("out_freed" + tag)
            with nc.Block() as block:
                @block.sync
                def _(sp):
                    send(sp, upto)

                @block.tensor
                def _(pe):
                    for n in range(2):
                        arrived(pe, cks[n])
                        for i in range(nt):
                            j = nt * n + i
                            if j >= 4:
                                pe.wait_ge(freed, j - 3)
                            for k in range(KD):
                                mm = pe.matmul(PS[j % 4][:], lhs(srcT, k, i), view(cks[n])[:, k, :], start=(k == 0), stop=(k == KD - 1))
                            if i == nt - 1:
                                mm.then_inc(chunk_used, 1)
                            else:
                                mm.then_inc(done, 1)

                @block.vector
                def _(dve):
                    for n in range(2):
                        for i in range(nt):
                            if i == nt - 1:
                                dve.wait_ge(chunk_used, cks[n] + 1)
                            else:
                                dve.wait_ge(done, (nt - 1) * n + i + 1)
                            dve.tensor_tensor(H[:, i, 512 * n:512 * n + 512], PS[(nt * n + i) % 4][:],
                                              MOD[:, D * gate + 512 * n:D * gate + 512 * n + 512], ALU.mult).then_inc(freed, 1)

        def residual_norm(tag, l, which, nt, src, gate, upto):
            ln_in, var, root, normed = sem("ln_in" + tag), sem("ln_var" + tag), sem("ln_root" + tag), sem("ln_normed" + tag)
            with nc.Block() as block:
                @block.sync
                def _(sp):
                    sp.dma_start(LNG, a["ln_g"][l, which:which + 1, :].broadcast_to([P, D])).then_inc(ln_in, 16)
                    sp.dma_start(LNB, a["ln_b"][l, which:which + 1, :].broadcast_to([P, D])).then_inc(ln_in, 16)
                    send(sp, upto)

                @block.vector
                def _(dve):
                    for i in range(nt):
                        x = Xt[:, i, :]
                        if gate is not None:
                            DV.link(dve.tensor_tensor(src[:, i, :], src[:, i, :], MOD[:, D * gate:D * gate + D], ALU.mult))
                        DV.link(dve.scalar_tensor_tensor(x, x, ALPHA, src[:, i, :], ALU.mult, ALU.add))
                        for s in range(2):
                            DV.then(dve.bn_stats(stats[:, 6 * s:6 * s + 6], x[:, 512 * s:512 * s + 512]))
                        DV.settle()
                        dve.bn_aggr(mv, stats).then_inc(var, 1)
                        dve.wait_ge(root, i + 1)
                        DV.link(dve.reciprocal(rstd[:, 1:2], rstd[:, 0:1]))
                        dve.tensor_scalar(x, x, mv[:, 0:1], rstd[:, 1:2], ALU.subtract, ALU.mult).then_inc(normed, 1)

                @block.scalar
                def _(act):
                    for i in range(nt):
                        act.wait_ge(var, i + 1)
                        act.activation(rstd[:, 0:1], mv[:, 1:2], ACT.Sqrt, bias=eps).then_inc(root, 1)

                @block.gpsimd
                def _(pool):
                    pool.wait_ge(ln_in, 32)
                    for i in range(nt):
                        x = Xt[:, i, :]
                        pool.wait_ge(normed, i + 1)
                        GP.link(pool.tensor_tensor(x, x, LNG, ALU.mult))
                        pool.tensor_tensor(x, x, LNB, ALU.add)

        pass
        plain_cols = lambda t, k, i: t[:, T * k + P * i:T * k + P * i + P]

        mixT = cut(A, 12032, 2 * PAIRS, T)
        by_tile = lambda v: v.rearrange("p (i s n) -> p s i n", s=2, n=CH)
        TAIL = SLOTS * SLOT

        def tail(at, *dims):
            return cut(W, TAIL + at, *dims)

        qT, kT, vT = tail(0, T), tail(512, T), tail(1024, NT, P)
        BT = tail(1536, 2, 6, CH)
        Sb = [tail(2304 + 512 * i, 512) for i in range(2)]
        Pr = [tail(3328 + 512 * i, 512) for i in range(2)]
        PT = [tail(4352 + 512 * i, 512) for i in range(2)]
        window = cut(MOD, 448, CH)
        na = {n: sem("na_" + n) for n in ("proj", "evac", "bias_in", "bias", "score", "biased", "negmax", "exp", "prob", "turn",
                                          "turned", "pv", "win")}
        UNITS = [(t, h) for t in range(NT) for h in range(2)]
        NU = len(UNITS)

        def attention(p):
            i = na_w[p]
            with nc.Block() as block:
                @block.sync
                def _(sp):
                    if p == 0:
                        sp.dma_start(window, a["k_window"]).then_inc(na["win"], 16)
                    sp.dma_start(BT, a["rpb_band"][:, 2 * p:2 * p + 2]).then_inc(na["bias_in"], 16)
                    send(sp, i + 1 + SLOTS)

                @block.tensor
                def _(pe):
                    arrived(pe, i)
                    for part in range(2):
                        for k in range(KD):
                            mm = pe.matmul(PS[part][:], view(i, part)[:, k, :], HTt[:, k, :], start=(k == 0), stop=(k == KD - 1))
                        mm.then_inc(na["proj"], 1)
                    for t in range(NT):
                        for k in range(KD):
                            mm = pe.matmul(PS[2][:, P * t:P * t + P], HTt[:, k, P * t:P * t + P], view(i, 2)[:, k, :],
                                           start=(k == 0), stop=(k == KD - 1))
                    mm.then_inc(chunk_used, 1)
                    pe.wait_ge(na["evac"], 3 * p + 3)

                    def scores(u):
                        t, h = UNITS[u]
                        if u >= 2:
                            pe.wait_ge(na["exp"], NU * p + u - 1)
                        n = T if t >= 2 else HALF
                        pe.matmul(PS[3 + h][:, 0:n], qT[64 * h:64 * h + 64, P * t:P * t + P], kT[64 * h:64 * h + 64, 0:n],
                                  start=True, stop=True).then_inc(na["score"], 1)

                    scores(0)
                    for u, (t, h) in enumerate(UNITS):
                        if u + 1 < NU:
                            scores(u + 1)
                        kt = 4 if t >= 2 else 2
                        pe.wait_ge(na["prob"], NU * p + u + 1)
                        if u >= 2:
                            pe.wait_ge(na["turned"], NU * p + u - 1)
                        for j in range(kt):
                            tr = pe.transpose(PS[5 + u % 2][:, P * j:P * j + P], Pr[u % 2][:, P * j:P * j + P], ident[:])
                        tr.then_inc(na["turn"], 1)
                        pe.wait_ge(na["turned"], NU * p + u + 1)
                        for j in range(kt):
                            mm = pe.matmul(PS[7][64 * h:64 * h + 64, P * t:P * t + P], vT[:, j, 64 * h:64 * h + 64],
                                           PT[u % 2][:, P * j:P * j + P], start=(j == 0), stop=(j == kt - 1))
                        mm.then_inc(na["pv"], 1)

                @block.scalar
                def _(act):
                    act.wait_ge(na["proj"], 2 * p + 1)
                    act.activation(qT, PS[0][:], ACT.Copy, scale=HD ** -0.5).then_inc(na["evac"], 1)
                    act.wait_ge(na["proj"], 2 * p + 2)
                    act.activation(kT, PS[1][:], ACT.Copy).then_inc(na["evac"], 1)
                    act.wait_ge(chunk_used, i + 1)
                    act.activation(vT, PS[2][:].rearrange("p (t n) -> p t n", n=P), ACT.Copy).then_inc(na["evac"], 1)

                    def turned(u):
                        t, h = UNITS[u]
                        n = T if t >= 2 else HALF
                        act.wait_ge(na["turn"], NU * p + u + 1)
                        if u >= 2:
                            act.wait_ge(na["pv"], NU * p + u - 1)
                        act.activation(PT[u % 2][:, 0:n], PS[5 + u % 2][:, 0:n], ACT.Copy).then_inc(na["turned"], 1)

                    for u, (t, h) in enumerate(UNITS):
                        act.wait_ge(na["negmax"], NU * p + u + 1)
                        if u >= 2:
                            act.wait_ge(na["turn"], NU * p + u - 1)
                        if t >= 2:
                            src, n = Sb[u % 2], T
                        else:
                            src, n = PS[3 + h][:, 0:HALF], HALF
                        act.activation(Pr[u % 2][:, 0:n], src, ACT.Exp, bias=small[:, 88 + u % 2:89 + u % 2],
                                       accum_out=small[:, 90 + u % 2:91 + u % 2]).then_inc(na["exp"], 1)
                        if u >= 1:
                            turned(u - 1)
                    turned(NU - 1)
                    act.wait_ge(na["pv"], NU * (p + 1))
                    act.activation(by_tile(mixT[:, p, :]), PS[7][:].rearrange("p (s i n) -> p s i n", s=2, n=CH), ACT.Copy)

                @block.vector
                def _(dve):
                    if p == 0:
                        dve.wait_ge(na["win"], 16)
                    dve.wait_ge(na["bias_in"], 16 * (p + 1))
                    bt = BT.rearrange("p h o w -> p (h o) w") if len(BT.shape) == 4 else BT
                    DV.link(dve.tensor_tensor(bt, bt, window.unsqueeze(1).broadcast_to([P, 12, CH]), ALU.add))
                    band = tail(1536, 2, 6 * CH)

                    def norm(u):
                        t, h = UNITS[u]
                        n = T if t >= 2 else HALF
                        dve.wait_ge(na["exp"], NU * p + u + 1)
                        r = small[:, 92 + u % 2:93 + u % 2]
                        DV.link(dve.reciprocal(r, small[:, 90 + u % 2:91 + u % 2]))
                        dve.tensor_scalar(Pr[u % 2][:, 0:n], Pr[u % 2][:, 0:n], r, None, ALU.mult).then_inc(na["prob"], 1)

                    for u, (t, h) in enumerate(UNITS):
                        dve.wait_ge(na["score"], NU * p + u + 1)
                        ps = PS[3 + h]
                        if t >= 2:
                            if u >= 2:
                                dve.wait_ge(na["exp"], NU * p + u - 1)
                            DV.then(dve.tensor_copy(Sb[u % 2][:, 0:HALF], ps[:, 0:HALF]))
                            at = CH * (2 - 2 * (t - 2))
                            DV.link(dve.tensor_tensor(Sb[u % 2][:, HALF:T], ps[:, HALF:T], band[:, h, at:at + HALF], ALU.add))
                            src = Sb[u % 2]
                        else:
                            src = ps[:, 0:HALF]
                        dve.tensor_reduce(small[:, 88 + u % 2:89 + u % 2], src, AX_X, ALU.max, negate=True).then_inc(na["negmax"], 1)
                        if u >= 1:
                            norm(u - 1)
                    norm(NU - 1)

        HQ, SG, F, KK, CUM, QS, KS = (tail(512 * n, T) for n in range(7))
        KST = tail(3584, NT, P)
        DD = [tail(4096 + HALF * n, HALF) for n in range(2)]
        EE = [tail(4608 + HALF * n, HALF) for n in range(2)]
        OS, SQ = tail(5120, T), tail(5632, T)
        NCH = NC // 2
        KB = [cut(A, 3584 * n, NL * NCH, P) for n in range(2)]
        QB = [cut(A, 7168 + 1536 * n, NL - 1, HALF) for n in range(2)]
        VB = cut(A, 10240, NC, P)
        MK = [cut(A, 11264, NL, CH), cut(MOD, 0, NL, CH)]
        SM = [cut(A, 11712 + CH * n, CH) for n in range(2)]
        ST = cut(MOD, 1024, NC, P)
        V = cut(MOD, 512, NT, P)
        TL, ET = small[:, 96:104], small[:, 104:112]
        lm = cut(levmask, 0, 2 * NL, CH)
        hg = {n: sem("hg_" + n) for n in (
            "proj", "query", "values", "gate", "sig", "forget", "log", "cum", "factor", "inter", "kturn", "kturned",
            "update", "state", "diff", "exp", "level", "diag", "score", "masked", "summed", "out", "out1", "osum", "square",
            "mean", "root", "clean")}
        ORDER = [list(range(NC)), [3, 2, 1, 0, 7, 6, 5, 4]]

        def hgrn(p):
            iz, iv = hz_w[p], hv_w[p]
            U = [(d, hf) for d in range(2) for hf in range(2)]
            with nc.Block() as block:
                @block.sync
                def _(sp):
                    send(sp, iv + 1 + SLOTS)

                @block.tensor
                def _(pe):
                    arrived(pe, iz)
                    for part in range(3):
                        for k in range(KD):
                            mm = pe.matmul(PS[part][:], view(iz, part)[:, k, :], HTt[:, k, :], start=(k == 0), stop=(k == KD - 1))
                        mm.then_inc(chunk_used if part == 2 else hg["proj"], 1)
                    arrived(pe, iv)
                    for t in range(NT):
                        for k in range(KD):
                            mm = pe.matmul(PS[3][:, P * t:P * t + P], HTt[:, k, P * t:P * t + P], view(iv, 0)[:, k, :],
                                           start=(k == 0), stop=(k == KD - 1))
                    mm.then_inc(hg["proj"], 1)
                    for k in range(KD):
                        mm = pe.matmul(PS[4][:], view(iv, 1)[:, k, :], HTt[:, k, :], start=(k == 0), stop=(k == KD - 1))
                    mm.then_inc(chunk_used, 1)

                    def turn_keys(d):
                        pe.wait_ge(hg["inter"], 2 * p + d + 1)
                        if d:
                            pe.wait_ge(hg["kturned"], 2 * p + d)
                        for t in range(NT):
                            tr = pe.transpose(PS[6][:, P * t:P * t + P], KS[:, P * t:P * t + P], ident[:])
                        tr.then_inc(hg["kturn"], 1)

                    def updates(d):
                        pe.wait_ge(hg["kturned"], 2 * p + d + 1)
                        pe.wait_ge(hg["values"], p + 1)
                        if d:
                            pe.wait_ge(hg["state"], 2 * p + d)
                        for t in range(NT):
                            for j in range(2):
                                mm = pe.matmul(PS[3 + 2 * j][:, P * t:P * t + P], KST[64 * j:64 * j + 64, t, :],
                                               V[64 * j:64 * j + 64, t, :], start=True, stop=True)
                        mm.then_inc(hg["update"], 1)

                    def level_scores(n, c):
                        d, hf = U[n]
                        s = NCH * n + c
                        if s >= 2:
                            pe.wait_ge(hg["masked"], 16 * p + s - 1)
                        for l in range(NL):
                            rhs = QB[n % 2][:, l, CH * c:CH * c + CH] if l < NL - 1 else HQ[:, HALF * hf + CH * c:HALF * hf + CH * c + CH]
                            mm = pe.matmul(PS[4 * (s % 2)][:, CH * l:CH * l + CH], KB[n % 2][:, NCH * l + c, :], rhs, start=True, stop=True)
                        mm.then_inc(hg["score"], 1)

                    def outputs(n, c):
                        d, hf = U[n]
                        s = NCH * n + c
                        g = NCH * hf + c
                        o = PS[(7, 1)[d]][:, CH * g:CH * g + CH]
                        pe.wait_ge(hg["summed"], 16 * p + s + 1)
                        pe.matmul(o, VB[:, g, :], SM[s % 2], start=True, stop=False)
                        pe.matmul(o, ST[:, g, :], QS[:, CH * g:CH * g + CH], start=False, stop=True).then_inc(hg["out"], 1)

                    for n, (d, hf) in enumerate(U):
                        if hf == 0:
                            turn_keys(d)
                            updates(d)
                        if n == 0:
                            pe.wait_ge(hg["query"], p + 1)
                            pe.wait_ge(hg["gate"], p + 1)
                        pe.wait_ge(hg["level"], 6 * (4 * p + n + 1))
                        pe.wait_ge(hg["diag"], 4 * p + n + 1)
                        level_scores(n, 0)
                        if hf == 0:
                            pe.wait_ge(hg["state"], 2 * p + d + 1)
                        for c in range(NCH):
                            if c + 1 < NCH:
                                level_scores(n, c + 1)
                            outputs(n, c)
                    pe.wait_ge(hg["square"], p + 1)
                    pe.matmul(PS[3][:], ones64[:], SQ, start=True, stop=True).then_inc(hg["mean"], 1)

                @block.scalar
                def _(act):
                    def sigmoids(d):
                        z = PS[1 + d]
                        act.activation(F, z[:], ACT.Sigmoid)
                        act.activation(KK, z[:], ACT.Sigmoid, scale=-1.0).then_inc(hg["sig"], 1)

                    act.wait_ge(hg["proj"], 3 * p + 1)
                    act.activation(HQ, PS[0][:], ACT.Silu).then_inc(hg["query"], 1)
                    act.wait_ge(hg["proj"], 3 * p + 2)
                    sigmoids(0)
                    act.wait_ge(hg["proj"], 3 * p + 3)
                    src = PS[3][:].rearrange("p (t n) -> p t n", n=P)
                    act.activation(V, src, ACT.Copy)
                    for j in range(2):
                        for h in range(2):
                            ins = act.activation(VB[64 * h:64 * h + 64, j::2, 64 * h:64 * h + 64],
                                                 src[64 * j:64 * j + 64, :, 64 * h:64 * h + 64], ACT.Copy)
                    ins.then_inc(hg["values"], 1)
                    act.wait_ge(chunk_used, iv + 1)
                    act.activation(SG, PS[4][:], ACT.Silu).then_inc(hg["gate"], 1)
                    for n, (d, hf) in enumerate(U):
                        if hf == 0:
                            if d:
                                act.wait_ge(hg["level"], 24 * p + 12)
                                act.wait_ge(hg["diag"], 4 * p + 2)
                                sigmoids(1)
                            act.wait_ge(hg["forget"], 2 * p + d + 1)
                            act.activation(F, F, ACT.Ln).then_inc(hg["log"], 1)
                            act.wait_ge(hg["cum"], 2 * p + d + 1)
                            if d:
                                act.wait_ge(hg["out"], 16 * p + 8)
                                act.wait_ge(hg["kturn"], 2 * p + 1)
                            act.activation(ET, TL, ACT.Exp)
                            act.activation((QS, KS)[d], CUM, ACT.Exp)
                            act.activation((KS, QS)[d], F, ACT.Exp).then_inc(hg["factor"], 1)
                            act.wait_ge(hg["kturn"], 2 * p + d + 1)
                            if d:
                                act.wait_ge(hg["update"], 2 * p + d)
                            act.activation(KST, PS[6][:].rearrange("p (t n) -> p t n", n=P), ACT.Copy).then_inc(hg["kturned"], 1)
                        for l in range(NL - 1):
                            s = 24 * p + 6 * n + l
                            act.wait_ge(hg["diff"], s + 1)
                            if s % 24 >= 2:
                                act.wait_ge(hg["level"], s - 1)
                            act.activation(EE[l % 2], DD[l % 2], ACT.Exp).then_inc(hg["exp"], 1)
                    act.wait_ge(hg["out"], 16 * p + 16)
                    act.activation(OS, PS[1][:], ACT.Copy).then_inc(hg["out1"], 1)
                    act.wait_ge(hg["osum"], p + 1)
                    act.activation(SQ, OS, ACT.Square).then_inc(hg["square"], 1)
                    act.wait_ge(hg["mean"], p + 1)
                    act.activation(SQ, PS[3][:], ACT.Sqrt, bias=rmseps).then_inc(hg["root"], 1)

                @block.gpsimd
                def _(pool):
                    pool.memset(ST, 0.0).then_inc(hg["clean"], 1)
                    pool.wait_ge(hg["clean"], p + 1)
                    for n, (d, hf) in enumerate(U):
                        pool.wait_ge(hg["cum"], 2 * p + d + 1)
                        if n:
                            pool.wait_ge(hg["diff"], 24 * p + 6 * n)
                        if n >= 2:
                            pool.wait_ge(hg["score"], 16 * p + NCH * (n - 1))
                        for h in range(2):
                            r = slice(64 * h, 64 * h + 64)
                            ins = pool.tensor_copy(KB[n % 2][r, NCH * (NL - 1):, r],
                                                   KK[r, HALF * hf:HALF * hf + HALF].rearrange("p (c s) -> p c s", s=CH))
                        ins.then_inc(hg["diag"], 1)
                        pool.wait_ge(hg["diag"], 4 * p + n + 1)
                        for l, b in enumerate(LEVELS):
                            s = 24 * p + 6 * n + l
                            if s % 24 >= 2:
                                pool.wait_ge(hg["exp"], s - 1)
                            m = b // 2 - 1 + d
                            v = CUM[:, HALF * hf:HALF * hf + HALF].rearrange("p (n b) -> p n b", b=b)
                            o = DD[l % 2].rearrange("p (n b) -> p n b", b=b)
                            ref = v[:, :, m:m + 1].broadcast_to([P, HALF // b, b // 2])
                            pool.tensor_tensor(o[:, :, 0:b // 2], ref, v[:, :, 0:b // 2], ALU.subtract)
                            pool.tensor_tensor(o[:, :, b // 2:], v[:, :, b // 2:], ref, ALU.subtract).then_inc(hg["diff"], 1)

                @block.vector
                def _(dve):
                    dve.wait_ge(hg["query"], p + 1)
                    DV.link(dve.tensor_scalar(HQ, HQ, HD ** -0.5, None, ALU.mult))
                    for n, (d, hf) in enumerate(U):
                        if hf == 0:
                            j = PAIRS * d + p
                            dve.wait_ge(hg["sig"], 2 * p + d + 1)
                            DV.then(dve.tensor_scalar(F, F, omlb[:, j:j + 1], lb[:, j:j + 1], ALU.mult, ALU.add))
                            DV.then(dve.tensor_scalar(KK, KK, omlb[:, j:j + 1], None, ALU.mult))
                            DV.settle()
                            dve.tensor_scalar(F, F, FLOOR, None, ALU.max).then_inc(hg["forget"], 1)
                            dve.wait_ge(hg["log"], 2 * p + d + 1)
                            if d:
                                dve.wait_ge(hg["diff"], 24 * p + 12)
                            DV.link(dve.tensor_tensor_scan(CUM, restart[:], F, 0.0, ALU.mult, ALU.add))
                            c3 = CUM.rearrange("p (c s) -> p c s", s=CH)
                            DV.link(dve.tensor_copy(TL, c3[:, :, CH - 1]))
                            if d:
                                DV.link(dve.tensor_tensor(CUM, CUM, F, ALU.subtract))
                            dve.tensor_tensor(F.rearrange("p (c s) -> p c s", s=CH), TL.unsqueeze(2).broadcast_to([P, NC, CH]),
                                              c3, ALU.subtract).then_inc(hg["cum"], 1)
                            dve.wait_ge(hg["factor"], 2 * p + d + 1)
                            DV.link(dve.tensor_tensor(QS, QS, HQ, ALU.mult))
                            dve.tensor_tensor(KS, KS, KK, ALU.mult).then_inc(hg["inter"], 1)
                        if n >= 2:
                            dve.wait_ge(hg["score"], 16 * p + NCH * (n - 1))
                        for l, b in enumerate(LEVELS):
                            dve.wait_ge(hg["exp"], 24 * p + 6 * n + l + 1)
                            ksl = slice(0, b // 2) if d == 0 else slice(b // 2, b)
                            qsl = slice(b // 2, b) if d == 0 else slice(0, b // 2)
                            blk = lambda v: v.rearrange("p (n b) -> p n b", b=b)
                            dve.tensor_tensor(blk(QB[n % 2][:, l, :])[:, :, qsl], blk(EE[l % 2])[:, :, qsl],
                                              blk(HQ[:, HALF * hf:HALF * hf + HALF])[:, :, qsl], ALU.mult)
                            four = lambda v: v.rearrange("p c (n b) -> p c n b", b=b)
                            for h in range(2):
                                r = slice(64 * h, 64 * h + 64)
                                e3 = EE[l % 2][r, :].rearrange("p (c s) -> p c s", s=CH)
                                k3 = KK[r, HALF * hf:HALF * hf + HALF].rearrange("p (c s) -> p c s", s=CH)
                                ins = dve.tensor_tensor(four(KB[n % 2][r, NCH * l:NCH * l + NCH, r])[:, :, :, ksl],
                                                        four(e3)[:, :, :, ksl], four(k3)[:, :, :, ksl], ALU.mult)
                            ins.then_inc(hg["level"], 1)
                        if hf == 0:
                            dve.wait_ge(hg["update"], 2 * p + d + 1)
                            dve.wait_ge(hg["clean"], p + 1)
                            if d:
                                dve.wait_ge(hg["out"], 16 * p + 8)
                            o = ORDER[d]
                            for h in range(2):
                                DV.then(dve.memset(ST[64 * h:64 * h + 64, o[0], 64 * h:64 * h + 64], 0.0))
                            DV.settle()
                            for q in range(NC - 1):
                                for h in range(2):
                                    r = slice(64 * h, 64 * h + 64)
                                    upd = PS[3 + 2 * (o[q] % 2)][r, P * (o[q] // 2) + 64 * h:P * (o[q] // 2) + 64 * h + 64]
                                    ins = dve.scalar_tensor_tensor(ST[r, o[q + 1], r], ST[r, o[q], r], ET[r, o[q]:o[q] + 1], upd,
                                                                   ALU.mult, ALU.add)
                                    if q < NC - 2 or h == 0:
                                        DV.then(ins)
                                    else:
                                        ins.then_inc(hg["state"], 1)
                                if q < NC - 2:
                                    DV.settle()
                        for c in range(NCH):
                            s = NCH * n + c
                            dve.wait_ge(hg["score"], 16 * p + s + 1)
                            dve.tensor_tensor(MK[s % 2], PS[4 * (s % 2)][:, 0:NL * CH].rearrange("p (l t) -> p l t", t=CH),
                                              lm[:, NL * d:NL * d + NL, :], ALU.mult).then_inc(hg["masked"], 1)
                            dve.wait_ge(hg["masked"], 16 * p + s + 1)
                            if s >= 2:
                                dve.wait_ge(hg["out"], 16 * p + s - 1)
                            dve.tensor_reduce(SM[s % 2], MK[s % 2].rearrange("p l t -> p t l"), AX_X, ALU.add).then_inc(hg["summed"], 1)
                    dve.wait_ge(hg["out1"], p + 1)
                    dve.tensor_tensor(OS, PS[7][:], OS, ALU.add).then_inc(hg["osum"], 1)
                    dve.wait_ge(hg["root"], p + 1)
                    DV.link(dve.reciprocal(SQ, SQ))
                    DV.link(dve.tensor_tensor(OS, OS, SQ, ALU.mult))
                    for s in range(2):
                        tokens = lambda v: v[:, HALF * s:HALF * s + HALF].rearrange("p (i n) -> p i n", n=CH)
                        dve.scalar_tensor_tensor(by_tile(mixT[:, PAIRS + p, :])[:, s], tokens(OS), normg, tokens(SG), ALU.mult, ALU.mult)

        def clean_levels():
            with nc.Block() as block:
                @block.gpsimd
                def _(pool):
                    pool.memset(A[:, 0:11264], 0.0)

        TRASH = 1024
        ROW = D + E
        hd = nc.dram_tensor("token_rows", (T, ROW), F32, kind="Internal").ap()
        yd = nc.dram_tensor("token_sums", (TRASH + P, D), F32, kind="Internal").ap()
        F16 = mybir.dt.float16
        GU = KD * HID
        ebase = [(W, EXPERT * b, W, EXPERT * b + 2 * GU) for b in range(3)] + [(HT, 0, A, 0)]

        def expert_view(b):
            t, g, u, d = ebase[b]
            return cut(t, g, KD, HID), cut(t, g + GU, KD, HID), cut(u, d, 2, D)

        Y = cut(A, 4096, NT, D)
        XG = [cut(A, 8192 + ROW * i, ROW) for i in range(2)]
        XT = [cut(A, 10368 + 1024 * i, 1024) for i in range(2)]
        YS = [cut(A, 12416 + 1024 * i, D) for i in range(2)]
        SU = [cut(A, 14464 + HID * i, HID) for i in range(2)]
        HM = [cut(A, 14976 + HID * i, HID) for i in range(2)]
        HX = [cut(A, 15488 + HID * i, HID) for i in range(2)]
        RW, RB = cut(A, 10368, KD, E), cut(A, 10880, E)
        BI, SEL = cut(A, 10944, E), cut(A, 11008, E)
        H6, W6 = cut(A, 11072, TOPK, E), cut(A, 11456, TOPK, E)
        HS, HB = cut(A, 12416, 2, 512), cut(A, 13440, 2, 512)
        TOP, IDX, IDF = cut(A, 16000, 8), cut(A, 16008, 8), cut(A, 16016, 8)
        EP = E + 2
        PM = cut(levmask, 0, NT, EP)
        CNT, CUMB, NB = cut(levmask, 264, E), cut(levmask, 328, E), cut(levmask, 392, E)
        SC1, SC2 = cut(levmask, 456, E), cut(levmask, 520, P)
        LISTE, LISTB = cut(levmask, 648, 32), cut(levmask, 680, 32)
        LISTI = cut(levmask, 712, 33).bitcast(mybir.dt.int32)
        SH = [cut(restart, 256 * i, 256).bitcast(F16) for i in range(2)]
        tri16, ones16, tok16 = (half[:, 0:64].bitcast(F16), half[:, 64:128].bitcast(F16), half[:, 128:132].bitcast(F16))
        M16 = half[:, 132:132 + NT * 32].bitcast(F16).rearrange("p (i e) -> p i e", e=E)
        IX = [half[:, 260 + i:261 + i].bitcast(U32) for i in range(4)]
        IXT = half[:, 264:265]
        negp, trp = small[:, 241:242], small[:, 242:243]
        pcol = small[:, 243:244]
        G = cut(gates, 0, NT, E)
        from_rows = lambda v, e: v[bass.ds(e, 1)].rearrange("e (p k) n -> p (e k) n", k=KD)
        from_tiles = lambda v, e: v[bass.ds(e, 1)].rearrange("e (k p) n -> p (e k) n", p=P)

        moe_sems = {}

        def clear_moe():
            with nc.Block() as block:
                @block.gpsimd
                def _(pool):
                    for s in moe_sems.values():
                        pool.sem_clear(s)

        def moe(l, nt, n_tok, sl):
            def s_(n):
                if n not in moe_sems:
                    moe_sems[n] = sem("moe_" + n)
                return moe_sems[n]

            weights = lambda e: (from_rows(a["exp_w_gate"][l], e), from_rows(a["exp_w_up"][l], e), from_tiles(a["exp_w_down"][l], e))
            w_in = [s_(f"w_in{b}") for b in range(4)]
            listed = n_tok * TOPK // sl

            def load(sp, b, e):
                for v, w in zip(expert_view(b), weights(e)):
                    sp.dma_start(v, w).then_inc(w_in[b], 16)

            r_in, rprod, sig, picked, ranks, gates_out, hd_out = (s_(n) for n in ("r_in", "rprod", "sig", "picked", "ranks", "gates_out", "hd_out"))
            up, silu, mul, down, moved, yd_out, zero = (s_(n) for n in ("sh_up", "sh_silu", "sh_mul", "sh_down", "sh_moved", "yd_out", "zero"))
            passed, placed, spread, diag = s_("passed"), s_("placed"), s_("spread"), s_("diag")
            with nc.Block() as block:
                @block.sync
                def _(sp):
                    sp.dma_start(RW, rows(a["router_w"][l])).then_inc(r_in, 16)
                    sp.dma_start(RB, a["router_bias"][l:l + 1, :].broadcast_to([P, E])).then_inc(r_in, 16)
                    for v, w in zip(expert_view(2), (rows(a["sh_w_gate"][l]), rows(a["sh_w_up"][l]), nat(a["sh_w_down"][l]))):
                        sp.dma_start(v, w).then_inc(w_in[2], 16)
                    for i in range(nt):
                        sp.dma_start(hd[P * i:P * i + P, 0:D], H[:, i, :]).then_inc(hd_out, 16)
                    load(sp, 0, 0)
                    load(sp, 1, 1)
                    sp.wait_ge(zero, 1)
                    sp.dma_start(yd[TRASH:TRASH + P, :], YS[1]).then_inc(yd_out, 16)
                    sp.wait_ge(gates_out, nt)
                    for i in range(nt):
                        sp.dma_start(hd[P * i:P * i + P, D:ROW], G[:, i, :]).then_inc(hd_out, 16)
                    for i in range(nt):
                        sp.wait_ge(moved, 2 * i + 2)
                        sp.dma_start(yd[P * i:P * i + P, :], Y[:, i, :]).then_inc(yd_out, 16)
                    sp.wait_ge(hd_out, 32 * nt)
                    load(sp, 2, 2)
                    load(sp, 3, 3)
                    sp.wait_ge(yd_out, 16 * (nt + 1))

                @block.gpsimd
                def _(pool):
                    pool.memset(XG[0], 0.0)
                    pool.memset(XG[1], 0.0)
                    pool.wait_ge(mul, 2)
                    pool.wait_ge(down, 2 * nt)
                    pool.memset(YS[1], 0.0).then_inc(zero, 1)

                @block.tensor
                def _(pe):
                    pe.wait_ge(r_in, 32)
                    for i in range(nt):
                        for k in range(KD):
                            mm = pe.matmul(PS[i][:, 0:E], plain_cols(HT[:], k, i), RW[:, k, :], start=(k == 0), stop=(k == KD - 1))
                        mm.then_inc(rprod, 1)
                    pe.wait_ge(w_in[2], 48)
                    wg, wu, wd = expert_view(2)
                    for m in range(2):
                        for n, w in enumerate((wg, wu)):
                            for k in range(KD):
                                mm = pe.matmul(PS[4 + 2 * m + n][:, 0:n_tok], w[:, k, P * m:P * m + P], HTt[:, k, 0:n_tok], start=(k == 0), stop=(k == KD - 1))
                        mm.then_inc(up, 1)
                    for i in range(nt):
                        pe.wait_ge(picked, i + 1)
                        for q in range(i + 1):
                            mm = pe.matmul(PS[i][:, E:2 * E], tri16 if q == i else ones16, M16[:, q, :], start=(q == 0), stop=(q == i))
                        mm.then_inc(ranks, 1)
                    for q in range(nt):
                        mm = pe.matmul(PS[nt - 1][:, 2 * E:3 * E], ones16, M16[:, q, :], start=(q == 0), stop=(q == nt - 1))
                    mm.then_inc(ranks, 1)
                    pe.wait_ge(mul, 2)
                    for i in range(nt):
                        for n in range(2):
                            j = 2 * i + n
                            if j >= 4:
                                pe.wait_ge(moved, j - 3)
                            for m in range(2):
                                mm = pe.matmul(PS[4 + j % 4][:], HB[:, m, P * i:P * i + P], wd[:, m, 512 * n:512 * n + 512], start=(m == 0), stop=(m == 1))
                            mm.then_inc(down, 1)
                    pe.wait_ge(diag, 1)
                    pe.matmul(PS[0][:, 384:512], onesf[:], SC2, start=True, stop=True).then_inc(spread, 1)
                    pe.wait_ge(diag, 2)
                    pe.matmul(PS[0][:, 256:384], onesf[:], SC2, start=True, stop=True).then_inc(spread, 1)

                @block.scalar
                def _(act):
                    for i in range(nt):
                        act.wait_ge(rprod, i + 1)
                        act.activation(G[:, i, :], PS[i][:, 0:E], ACT.Sigmoid).then_inc(sig, 1)
                    for m in range(2):
                        act.wait_ge(up, m + 1)
                        act.activation(HS[:, m, 0:n_tok], PS[4 + 2 * m][:, 0:n_tok], ACT.Silu).then_inc(silu, 1)
                    for i in range(nt):
                        act.wait_ge(down, 2 * i + 2)
                        for n in range(2):
                            act.activation(Y[:, i, 512 * n:512 * n + 512], PS[4 + (2 * i + n) % 4][:], ACT.Copy).then_inc(moved, 1)

                @block.vector
                def _(dve):
                    dve.wait_ge(r_in, 32)
                    DV.then(dve.memset(PM, -1.0))
                    for i in range(nt):
                        g = G[:, i, :]
                        dve.wait_ge(sig, i + 1)
                        DV.link(dve.tensor_tensor(BI, g, RB, ALU.add))
                        DV.link(dve.max(TOP, BI))
                        DV.link(dve.max_index(IDX.bitcast(U32), TOP, BI))
                        DV.link(dve.tensor_copy(IDF, IDX.bitcast(U32)))
                        DV.link(dve.tensor_tensor(H6, iota.unsqueeze(1).broadcast_to([P, TOPK, E]),
                                                  IDF[:, 0:TOPK].unsqueeze(2).broadcast_to([P, TOPK, E]), ALU.is_equal))
                        DV.link(dve.tensor_reduce(SEL, H6.rearrange("p k e -> p e k"), AX_X, ALU.add))
                        dve.tensor_copy(M16[:, i, :], SEL).then_inc(picked, 1)
                        DV.link(dve.tensor_tensor(g, g, SEL, ALU.mult))
                        DV.link(dve.tensor_reduce(stats[:, 0:1], g, AX_X, ALU.add))
                        DV.link(dve.reciprocal(stats[:, 1:2], stats[:, 0:1]))
                        dve.tensor_scalar(g, g, stats[:, 1:2], ROUTED_SCALE, ALU.mult, ALU.mult).then_inc(gates_out, 1)
                    for i in range(nt):
                        dve.wait_ge(ranks, i + 1 if i < nt - 1 else nt + 1)
                        DV.link(dve.tensor_copy(SEL, M16[:, i, :]))
                        DV.link(dve.scalar_tensor_tensor(SEL, PS[i][:, E:2 * E], 1.0, SEL, ALU.add, ALU.mult))
                        DV.link(dve.tensor_scalar(PM[:, i, 0:E], SEL, -1.0, None, ALU.add))
                    for m in range(2):
                        dve.wait_ge(silu, m + 1)
                        dve.tensor_tensor(HB[:, m, 0:n_tok], HS[:, m, 0:n_tok], PS[5 + 2 * m][:, 0:n_tok], ALU.mult).then_inc(mul, 1)
                    dve.wait_ge(ranks, nt + 1)
                    DV.link(dve.tensor_copy(CNT, PS[nt - 1][:, 2 * E:3 * E]))
                    DV.link(dve.tensor_scalar(NB, CNT, float(sl), None, ALU.is_gt))
                    for j in range(2, -(-n_tok // sl)):
                        DV.link(dve.scalar_tensor_tensor(NB, CNT, float(sl * j), NB, ALU.is_gt, ALU.add))
                    DV.link(dve.memset(SC1, 1.0))
                    DV.link(dve.tensor_tensor_scan(CUMB, SC1, NB, 0.0, ALU.mult, ALU.add))
                    DV.link(dve.tensor_scalar(SC1, CUMB, pcol, None, ALU.is_le))
                    DV.link(dve.tensor_reduce(stats[:, 0:1], SC1, AX_X, ALU.add))
                    DV.link(dve.tensor_scalar(SC2, ident[:], stats[:, 0:1], None, ALU.mult))
                    dve.nop().then_inc(diag, 1)
                    DV.link(dve.tensor_tensor(NB, CUMB, NB, ALU.subtract))
                    DV.link(dve.tensor_scalar(SC1, iota, stats[:, 0:1], None, ALU.is_equal))
                    DV.link(dve.tensor_tensor(SC1, SC1, NB, ALU.mult))
                    DV.link(dve.tensor_reduce(stats[:, 1:2], SC1, AX_X, ALU.add))
                    DV.link(dve.tensor_tensor(stats[:, 1:2], pcol, stats[:, 1:2], ALU.subtract))
                    DV.link(dve.tensor_scalar(stats[:, 1:2], stats[:, 1:2], 1.0, float(sl), ALU.add, ALU.mult))
                    dve.wait_ge(spread, 1)
                    DV.then(dve.tensor_copy(LISTE, PS[0][:, 384:416]))
                    DV.link(dve.tensor_copy(LISTI[:, 0:32], PS[0][:, 384:416]))
                    DV.link(dve.tensor_copy(LISTI[:, 32:33], CUMB[:, E - 1:E]))
                    DV.link(dve.tensor_scalar(SC2, ident[:], stats[:, 1:2], None, ALU.mult))
                    dve.nop().then_inc(diag, 1)
                    dve.wait_ge(spread, 2)
                    dve.tensor_copy(LISTB, PS[0][:, 256:288])

            def select(dve, q, e, slots):
                return dve.tensor_tensor(SH[q][:, 0:nt * sl].rearrange("p (i s) -> p i s", s=sl),
                                         slots.unsqueeze(1).broadcast_to([P, nt, sl]),
                                         PM[:, 0:nt, bass.ds(e, 1)].broadcast_to([P, nt, sl]), ALU.is_equal)

            def index_products(pe, q):
                sh = SH[q][:, 0:nt * sl].rearrange("p (i s) -> p i s", s=sl)
                for i in range(nt):
                    mm = pe.matmul(PS[5][0:sl, 0:2], sh[:, i, :], tok16[:, 2 * i:2 * i + 2], start=(i == 0), stop=(i == nt - 1))
                return mm

            def index(dve, q, half_done, n):
                dve.tensor_scalar(IXT[0:sl], PS[5][0:sl, 1:2], negp[0:sl], trp[0:sl], ALU.mult, ALU.add).then_inc(half_done, 1)
                dve.wait_ge(half_done, n)
                return dve.tensor_tensor(IX[q][0:sl], PS[5][0:sl, 0:1], IXT[0:sl], ALU.add)

            def carry(eng):
                eng.sem_inc(passed, 1)

            def gather(pool, q, o):
                return pool.indirect_dma_start(XG[o][0:sl, :], None, hd, bass.IndirectOffsetOnAxis(ap=IX[q][0:sl], axis=0),
                                               bounds_check=n_tok - 1, oob_is_err=False)

            def scatter(pool, q, o):
                return pool.indirect_dma_start(yd, bass.IndirectOffsetOnAxis(ap=IX[q][0:sl], axis=0), YS[o][0:sl, :], None,
                                               bounds_check=TRASH + P - 1, oob_is_err=True, compute_op=ALU.add)

            def turn_rows(pe, o):
                x = XG[o][0:sl, 0:D].rearrange("t (p k) -> t k p", k=KD)
                for k in range(KD):
                    mm = pe.transpose(PS[2 + k // 4][:, sl * (k % 4):sl * (k % 4) + sl], x[:, k, :], ident[0:sl, 0:sl])
                return mm

            xt = lambda o, g: XT[o][:, 4 * sl * g:4 * sl * g + 4 * sl]

            def gate_up(pe, b, o, g):
                t, at = ebase[b][0:2]
                w = cut(t, at, 2, KD, HID)
                for k in range(KD):
                    x = XT[o][:, sl * k:sl * k + sl]
                    if sl == 64:
                        for n in range(2):
                            mm = pe.matmul(PS[g][64 * n:64 * n + 64, 0:HID], x, w[:, n, k, :], start=(k == 0), stop=(k == KD - 1))
                    else:
                        mm = pe.matmul(PS[g][0:sl, :], x, w[:, :, k, :], start=(k == 0), stop=(k == KD - 1))
                return mm

            up_of = lambda g: PS[g][64:128, 0:HID] if sl == 64 else PS[g][0:sl, HID:2 * HID]

            def turn_hidden(pe, o):
                for m in range(2):
                    mm = pe.transpose(PS[4][:, sl * m:sl * m + sl], HM[o][0:sl, P * m:P * m + P], ident[0:sl, 0:sl])
                return mm

            def down_product(pe, b, o):
                wd = expert_view(b)[2]
                for m in range(2):
                    for n in range(2):
                        y = PS[6][64 * n:64 * n + 64, :] if sl == 64 else PS[6 + n][0:sl, :]
                        mm = pe.matmul(y, HX[o][:, sl * m:sl * m + sl], wd[:, m, 512 * n:512 * n + 512], start=(m == 0), stop=(m == 1))
                return mm

            y_of = lambda n: PS[6][64 * n:64 * n + 64, :] if sl == 64 else PS[6 + n][0:sl, :]
            weigh = lambda dve, o, g, e: dve.scalar_tensor_tensor(HM[o][0:sl], SU[o][0:sl], XG[o][0:sl, bass.ds(e + D, 1)], up_of(g), ALU.mult, ALU.mult)

            selected, indexed, index_half, index_made, turned, xt_half, xt_made, gu, silud, hid, hturn, hx, yprod, y_half, y_made = (
                s_(n) for n in ("selected", "indexed", "index_half", "index_made", "turned", "xt_half", "xt_made", "gu", "silud", "hid", "hturn", "hx", "yprod",
                                "y_half", "y_made"))
            x_in = [sem(f"x_in{o}_{l}") for o in range(2)]
            y_out = [sem(f"y_out{o}_{l}") for o in range(2)]

            def run(eng, first, step):
                for e in range(first):
                    step(e, e % 4, e)
                left = (E - first) % 4
                with eng.Fori(0, (E - first) // 4) as r:
                    for i in range(4):
                        step(4 * r + (first + i), (first + i) % 4, None)
                for e in range(E - left, E):
                    step(e, e % 4, e)

            with nc.Block() as block:
                @block.sync
                def _(sp):
                    with sp.Fori(0, E // 4 - 1) as r:
                        for q in range(4):
                            sp.wait_ge(yprod, 4 * r + q + 1)
                            load(sp, q, 4 * r + (4 + q))

                @block.tensor
                def _(pe):
                    def step(e, q, at):
                        pe.wait_ge(w_in[q], 12 * (e - q) + 48 + (48 if q == 2 else 0))
                        pe.wait_ge(xt_made, e + 1)
                        pe.wait_ge(xt_half, e + 1)
                        if at is None or at >= 2:
                            pe.wait_ge(hid, e - 1)
                        gate_up(pe, q, q % 2, q % 2).then_inc(gu, 1)
                        if at is None or at < E - 1:
                            o = (q + 1) % 2
                            pe.wait_ge(x_in[o], 16 * ((e + 1) // 2) + 16 if at is not None else 8 * (e + 1 - o) + 16)
                        if at != 0:
                            pe.wait_ge(hx, e)
                            if at != 1:
                                pe.wait_ge(y_made, e - 1)
                                pe.wait_ge(y_half, e - 1)
                            down_product(pe, (q - 1) % 4, (q - 1) % 2).then_inc(yprod, 1)
                        if at is None or at < E - 1:
                            turn_rows(pe, (q + 1) % 2).then_inc(turned, 1)
                        pe.wait_ge(selected, e + 3)
                        pe.wait_ge(index_made, e + 2)
                        pe.wait_ge(hid, e + 1)
                        index_products(pe, q % 2).then_inc(indexed, 1)
                        turn_hidden(pe, q % 2).then_inc(hturn, 1)

                    for e in range(2):
                        pe.wait_ge(selected, e + 1)
                        if e:
                            pe.wait_ge(index_made, e)
                        index_products(pe, e).then_inc(indexed, 1)
                    pe.wait_ge(x_in[0], 16)
                    turn_rows(pe, 0).then_inc(turned, 1)
                    run(pe, 2, step)
                    pe.wait_ge(hx, E)
                    pe.wait_ge(y_made, E - 1)
                    pe.wait_ge(y_half, E - 1)
                    down_product(pe, (E - 1) % 4, (E - 1) % 2).then_inc(yprod, 1)

                @block.scalar
                def _(act):
                    def xt_copy(o, n):
                        act.wait_ge(turned, n)
                        act.activation(xt(o, 0), PS[2][:, 0:4 * sl], ACT.Copy).then_inc(xt_half, 1)

                    def y_copy(o, n, first=False):
                        act.wait_ge(yprod, n)
                        if not first:
                            act.wait_ge(y_out[o], 8 * (n - 1 - o))
                        act.activation(YS[o][0:sl, 0:512], y_of(0), ACT.Copy).then_inc(y_half, 1)

                    def step(e, q, at):
                        act.wait_ge(gu, e + 1)
                        act.activation(SU[q % 2][0:sl], PS[q % 2][0:sl, 0:HID], ACT.Silu).then_inc(silud, 1)
                        if at != 0:
                            y_copy((q - 1) % 2, e, at in (1, 2))
                        if at is None or at < E - 1:
                            if at is None or at >= 1:
                                act.wait_ge(gu, e)
                            xt_copy((q + 1) % 2, e + 2)

                    xt_copy(0, 1)
                    run(act, 3, step)
                    y_copy((E - 1) % 2, E)

                @block.vector
                def _(dve):
                    def y_copy(o, n, first=False):
                        dve.wait_ge(yprod, n)
                        if not first:
                            dve.wait_ge(y_out[o], 8 * (n - 1 - o))
                        dve.tensor_copy(YS[o][0:sl, 512:D], y_of(1)).then_inc(y_made, 1)

                    def xt_copy(o, n):
                        dve.wait_ge(turned, n)
                        dve.tensor_copy(xt(o, 1), PS[3][:, 0:4 * sl]).then_inc(xt_made, 1)

                    def indices(e, q):
                        dve.wait_ge(indexed, e + 1)
                        index(dve, q, index_half, e + 1).then_inc(index_made, 1)

                    def step(e, q, at):
                        if at is None or at < E - 1:
                            select(dve, (q + 1) % 2, e + 3 if at is None or at < E - 3 else E + 1, iota_s[:, 0:sl]).then_inc(selected, 1)
                        dve.wait_ge(silud, e + 1)
                        weigh(dve, q % 2, q % 2, e).then_inc(hid, 1)
                        if at != 0:
                            y_copy((q - 1) % 2, e, at in (1, 2))
                        if at is None or at < E - 1:
                            xt_copy((q + 1) % 2, e + 2)
                        if at not in (0, 1):
                            dve.wait_ge(y_out[q % 2], 8 * (e - q % 2))
                        indices(e + 2, (q + 2) % 4)
                        dve.wait_ge(hturn, e + 1)
                        dve.tensor_copy(HX[q % 2][:, 0:2 * sl], PS[4][:, 0:2 * sl]).then_inc(hx, 1)

                    for e in range(2):
                        select(dve, e, e, iota_s[:, 0:sl]).then_inc(selected, 1)
                    indices(0, 0)
                    select(dve, 0, 2, iota_s[:, 0:sl]).then_inc(selected, 1)
                    indices(1, 1)
                    xt_copy(0, 1)
                    run(dve, 3, step)
                    y_copy((E - 1) % 2, E)

                @block.gpsimd
                def _(pool):
                    def get(n, o, q, used=None):
                        pool.wait_ge(index_made, n)
                        if used is not None:
                            pool.wait_ge(turned, used)
                            pool.wait_ge(hid, used)
                        carry(pool)
                        gather(pool, q, o).then_inc(x_in[o], 16)

                    def put(e, q, at):
                        pool.wait_ge(y_half, e + 1)
                        pool.wait_ge(y_made, e + 1)
                        if at != 0:
                            o = (q - 1) % 2
                            pool.wait_ge(y_out[o], 8 * (e - 1 - o) + 16)
                        carry(pool)
                        scatter(pool, q, q % 2).then_inc(y_out[q % 2], 16)

                    def step(e, q, at):
                        if at is None or at < E - 2:
                            get(e + 3, q % 2, (q + 2) % 4, e + 1)
                        if at != 0:
                            put(e - 1, (q - 1) % 4, None if at is None else at - 1)

                    get(1, 0, 0)
                    get(2, 1, 1)
                    run(pool, 2, step)
                    put(E - 1, (E - 1) % 4, E - 1)
                    pool.wait_ge(y_out[(E - 1) % 2], 8 * E)
                    pool.wait_ge(y_out[E % 2], 8 * E)

            ALL = E + 2
            def more(eng, body):
                n = eng.value_load(LISTI[0:1, 32:33], min_val=0, max_val=listed)
                with eng.Fori(0, listed) as i:
                    with eng.If(n > i):
                        body(i, eng.value_load(LISTI[0:1, bass.ds(i, 1)], min_val=0, max_val=E - 1))
                    with eng.Else():
                        eng.nop()

            with nc.Block() as block:
                @block.sync
                def _(sp):
                    def body(i, e):
                        sp.wait_ge(yprod, i + E)
                        for v, w in zip(expert_view(0), weights(e)):
                            sp.dma_start(v, w).then_inc(w_in[0], 16)
                    more(sp, body)

                @block.tensor
                def _(pe):
                    def body(i, e):
                        pe.wait_ge(selected, i + (ALL + 1))
                        index_products(pe, 0).then_inc(indexed, 1)
                        pe.wait_ge(x_in[0], 16 * i + (8 * E + 16))
                        carry(pe)
                        turn_rows(pe, 0).then_inc(turned, 1)
                        pe.wait_ge(xt_half, i + (E + 1))
                        pe.wait_ge(xt_made, i + (E + 1))
                        pe.wait_ge(w_in[0], 48 * i + (12 * E + 48))
                        gate_up(pe, 0, 0, 0).then_inc(gu, 1)
                        pe.wait_ge(hid, i + (E + 1))
                        carry(pe)
                        turn_hidden(pe, 0).then_inc(hturn, 1)
                        pe.wait_ge(hx, i + (E + 1))
                        down_product(pe, 0, 0).then_inc(yprod, 1)
                    more(pe, body)

                @block.scalar
                def _(act):
                    def body(i, e):
                        act.wait_ge(turned, i + (E + 1))
                        act.activation(xt(0, 0), PS[2][:, 0:4 * sl], ACT.Copy).then_inc(xt_half, 1)
                        act.wait_ge(gu, i + (E + 1))
                        act.activation(SU[0][0:sl], PS[0][0:sl, 0:HID], ACT.Silu).then_inc(silud, 1)
                        act.wait_ge(yprod, i + (E + 1))
                        act.activation(YS[0][0:sl, 0:512], y_of(0), ACT.Copy).then_inc(y_half, 1)
                    more(act, body)

                @block.vector
                def _(dve):
                    slots = XT[1][:, 0:sl]
                    def body(i, e):
                        dve.tensor_scalar(slots, iota_s[:, 0:sl], LISTB[:, bass.ds(i, 1)], None, ALU.add).then_inc(placed, 1)
                        dve.wait_ge(placed, i + 1)
                        select(dve, 0, e, slots).then_inc(selected, 1)
                        dve.wait_ge(indexed, i + (ALL + 1))
                        dve.wait_ge(y_out[0], 16 * i + 8 * E)
                        index(dve, 0, index_half, i + (ALL + 1)).then_inc(index_made, 1)
                        dve.wait_ge(turned, i + (E + 1))
                        dve.tensor_copy(xt(0, 1), PS[3][:, 0:4 * sl]).then_inc(xt_made, 1)
                        dve.wait_ge(silud, i + (E + 1))
                        weigh(dve, 0, 0, e).then_inc(hid, 1)
                        dve.wait_ge(hturn, i + (E + 1))
                        dve.tensor_copy(HX[0][:, 0:2 * sl], PS[4][:, 0:2 * sl]).then_inc(hx, 1)
                        dve.wait_ge(yprod, i + (E + 1))
                        dve.tensor_copy(YS[0][0:sl, 512:D], y_of(1)).then_inc(y_made, 1)
                    more(dve, body)

                @block.gpsimd
                def _(pool):
                    def body(i, e):
                        pool.wait_ge(index_made, i + (ALL + 1))
                        carry(pool)
                        gather(pool, 0, 0).then_inc(x_in[0], 16)
                        pool.wait_ge(y_half, i + (E + 1))
                        pool.wait_ge(y_made, i + (E + 1))
                        carry(pool)
                        scatter(pool, 0, 0).then_inc(y_out[0], 16)
                        pool.wait_ge(y_out[0], 16 * i + (8 * E + 16))
                        carry(pool)
                    more(pool, body)

            y_in = s_("y_in")
            with nc.Block() as block:
                @block.sync
                def _(sp):
                    for i in range(nt):
                        sp.dma_start(Y[:, i, :], yd[P * i:P * i + P, :]).then_inc(y_in, 16)
                    sp.wait_ge(y_in, 16 * nt)

        KJ = D // P
        GY = cut(A, 0, KJ, HALF)
        BD = cut(A, 8192, 4 * KJ, P)
        M1 = cut(A, 12288, KJ, HALF)
        obuf = lambda n: cut(A, 2048 + 512 * n, T)
        RR, II, AA, TT = ([obuf(2 * q + n) for n in range(2)] for q in range(4))
        UC, HH = ([obuf(8 + 2 * q + n) for n in range(2)] for q in range(2))
        coef, ncoef = small[:, 225:241], small[:, 48:64]
        lw = [cut(gates, 16 * n, 16) for n in range(4)]
        od = {n: sem("od_" + n) for n in ("zero", "bd_in", "y", "gelu", "u", "conv", "ga", "gates", "decay", "iu", "ratio",
                                          "root", "scan", "lam")}

        def recurrent_unit():
            with nc.Block() as block:
                @block.sync
                def _(sp):
                    for kind, w in enumerate(("lru_w_a", "lru_w_x")):
                        for d in range(2):
                            for h in range(2):
                                r = slice(64 * h, 64 * h + 64)
                                at = 16 * kind + 8 * d
                                sp.dma_start(BD[r, at:at + KJ, r], a[w][0, d].rearrange("(j h) r c -> h r j c", h=2)[h]).then_inc(od["bd_in"], 16)
                    send(sp, odi[3] + 1 + SLOTS)

                @block.tensor
                def _(pe):
                    for c in range(2):
                        arrived(pe, odi[c])
                        for q in range(4):
                            j = 4 * c + q
                            if j >= 2:
                                pe.wait_ge(od["gelu"], j - 1)
                            for k in range(KD):
                                mm = pe.matmul(PS[6 + j % 2][:, 0:HALF], view(odi[c])[:, k, P * q:P * q + P], HTt[:, k, HALF:T],
                                               start=(k == 0), stop=(k == KD - 1))
                            mm.then_inc(chunk_used if q == 3 else od["y"], 1)

                    def u_product(j):
                        c, q = 2 + j // 4, j % 4
                        if q == 0:
                            arrived(pe, odi[c])
                        if j >= 2:
                            pe.wait_ge(od["conv"], j - 1)
                        for k in range(KD):
                            mm = pe.matmul(PS[j % 2][:], view(odi[c])[:, k, P * q:P * q + P], HTt[:, k, :], start=(k == 0), stop=(k == KD - 1))
                        mm.then_inc(chunk_used if q == 3 else od["u"], 1)

                    u_product(0)
                    pe.wait_ge(od["bd_in"], 16 * 8)
                    for j in range(KJ):
                        if j + 1 < KJ:
                            u_product(j + 1)
                        pe.wait_ge(od["conv"], j + 1)
                        for d in range(2):
                            s = 2 * j + d
                            if s >= 2:
                                pe.wait_ge(od["gates"], s - 1)
                            for kind in range(2):
                                mm = pe.matmul(PS[2 + 2 * (s % 2) + kind][:], BD[:, 16 * kind + 8 * d + j, :], UC[j % 2], start=True, stop=True)
                            mm.then_inc(od["ga"], 1)

                @block.scalar
                def _(act):
                    act.activation(lw[0], lam, ACT.Abs).then_inc(od["lam"], 1)
                    act.wait_ge(od["lam"], 1)
                    act.activation(lw[0], lw[0], ACT.Exp, scale=-1.0).then_inc(od["lam"], 1)
                    for j in range(KJ):
                        if j % 4 == 3:
                            act.wait_ge(chunk_used, odi[j // 4] + 1)
                        else:
                            act.wait_ge(od["y"], 3 * (j // 4) + j % 4 + 1)
                        act.activation(GY[:, j, :], PS[6 + j % 2][:, 0:HALF], ACT.Gelu_apprx_tanh).then_inc(od["gelu"], 1)
                    act.wait_ge(od["lam"], 3)

                    def root(s):
                        act.wait_ge(od["ratio"], s + 1)
                        act.activation(RR[s % 2], TT[s % 2], ACT.Sqrt, scale=2.0).then_inc(od["root"], 1)

                    for s in range(2 * KJ):
                        j, d = s // 2, s % 2
                        act.wait_ge(od["ga"], s + 1)
                        if s >= 2:
                            act.wait_ge(od["scan"], s - 1)
                        n = 8 * d + j
                        AC.then(act.activation(RR[s % 2], PS[2 + 2 * (s % 2)][:], ACT.Sigmoid, bias=gbias[:, n:n + 1]))
                        act.activation(II[s % 2], PS[3 + 2 * (s % 2)][:], ACT.Sigmoid, bias=gbias[:, 16 + n:17 + n]).then_inc(od["gates"], 1)
                        AC.settle()
                        act.activation(AA[s % 2], RR[s % 2], ACT.Exp, scale=coef[:, n:n + 1])
                        act.activation(TT[s % 2], RR[s % 2], ACT.Tanh, scale=ncoef[:, n:n + 1]).then_inc(od["decay"], 1)
                        root(s)

                @block.gpsimd
                def _(pool):
                    for s in range(2 * KJ):
                        pool.wait_ge(od["gates"], s + 1)
                        pool.tensor_tensor(II[s % 2], II[s % 2], UC[(s // 2) % 2], ALU.mult).then_inc(od["iu"], 1)

                @block.vector
                def _(dve):
                    e, z, z2, q = lw
                    dve.wait_ge(od["lam"], 2)
                    DV.link(dve.tensor_scalar(z, e, 2.0, None, ALU.add))
                    DV.link(dve.reciprocal(z, z))
                    DV.link(dve.tensor_tensor(z, z, e, ALU.mult))
                    DV.link(dve.tensor_tensor(z2, z, z, ALU.mult))
                    DV.link(dve.tensor_scalar(q, z2, 1 / 15, None, ALU.mult))
                    for n in (13, 11, 9, 7, 5, 3):
                        DV.link(dve.scalar_tensor_tensor(q, q, 1 / n, z2, ALU.add, ALU.mult))
                    DV.link(dve.scalar_tensor_tensor(q, q, 1.0, z, ALU.add, ALU.mult))
                    DV.link(dve.tensor_scalar(z, lam, -1.0, 0.0, ALU.mult, ALU.max))
                    DV.link(dve.scalar_tensor_tensor(q, q, 2.0, z, ALU.mult, ALU.add))
                    DV.link(dve.tensor_scalar(coef, q, -LRU_C, None, ALU.mult))
                    dve.tensor_scalar(ncoef, q, LRU_C, None, ALU.mult).then_inc(od["lam"], 1)

                    def conv(j):
                        if j % 4 == 3:
                            dve.wait_ge(chunk_used, odi[2 + j // 4] + 1)
                        else:
                            dve.wait_ge(od["u"], 3 * (j // 4) + j % 4 + 1)
                        if j >= 2:
                            dve.wait_ge(od["iu"], 2 * (j - 1))
                        u = PS[j % 2][:].rearrange("p (s n) -> p s n", s=2)
                        o = UC[j % 2].rearrange("p (s n) -> p s n", s=2)
                        DV.link(dve.tensor_scalar(UC[j % 2], PS[j % 2][:], convw[:, 16 + j:17 + j], convb[:, j:j + 1], ALU.mult, ALU.add))
                        for tap, shift in ((0, -2), (1, -1), (3, 1)):
                            lo, hi = max(0, -shift), HALF - max(0, shift)
                            ins = dve.scalar_tensor_tensor(o[:, :, lo:hi], u[:, :, lo + shift:hi + shift], convw[:, 8 * tap + j:8 * tap + j + 1],
                                                           o[:, :, lo:hi], ALU.mult, ALU.add)
                            if tap == 3:
                                ins.then_inc(od["conv"], 1)
                            else:
                                DV.link(ins)

                    conv(0)
                    for s in range(2 * KJ):
                        j, d = s // 2, s % 2
                        x = s % 2
                        if d == 0 and j + 1 < KJ:
                            conv(j + 1)
                        dve.wait_ge(od["decay"], s + 1)
                        DV.link(dve.tensor_scalar(HH[d], TT[x], 1.0, None, ALU.add))
                        DV.link(dve.reciprocal(HH[d], HH[d]))
                        dve.tensor_tensor(TT[x], TT[x], HH[d], ALU.mult).then_inc(od["ratio"], 1)
                        dve.wait_ge(od["iu"], s + 1)
                        dve.wait_ge(od["root"], s + 1)
                        DV.link(dve.tensor_tensor(II[x], II[x], RR[x], ALU.mult))
                        if d == 0:
                            dve.tensor_tensor_scan(HH[0], AA[x], II[x], 0.0, ALU.mult, ALU.add).then_inc(od["scan"], 1)
                        else:
                            back = lambda v, q: v[:, HALF * q:HALF * q + HALF][:, ::-1]
                            DV.link(dve.tensor_tensor_scan(back(HH[1], 0), back(AA[x], 0), back(II[x], 0), 0.0, ALU.mult, ALU.add))
                            dve.tensor_tensor_scan(back(HH[1], 1), back(AA[x], 1), back(II[x], 1), HH[1][:, 0:1], ALU.mult, ALU.add).then_inc(od["scan"], 1)
                            dve.wait_ge(od["scan"], s + 1)
                            DV.link(dve.tensor_tensor(HH[0][:, HALF:T], HH[0][:, HALF:T], HH[1][:, HALF:T], ALU.add))
                            DV.link(dve.tensor_tensor(M1[:, j, :], HH[0][:, HALF:T], GY[:, j, :], ALU.mult))

        def clear_gate_weights():
            with nc.Block() as block:
                @block.gpsimd
                def _(pool):
                    pool.memset(A[:, 8192:12288], 0.0)

        def pack_latent():
            with nc.Block() as block:
                @block.vector
                def _(dve):
                    for i in range(2):
                        for s in range(2):
                            DV.link(dve.tensor_copy(Xt[64 * s:64 * s + 64, i, :], Xt[64:128, 2 * i + s, :]))

        def store():
            stored = sem("stored")
            with nc.Block() as block:
                @block.sync
                def _(sp):
                    for i in range(2):
                        sp.dma_start(out[P * i:P * i + P, :], Xt[:, i, :]).then_inc(stored, 16)
                    sp.wait_ge(stored, 32)


        def stop():
            with nc.Block() as block:
                @block.sync
                def _(sp):
                    for i in range(max(0, sent[0] - SLOTS), sent[0]):
                        arrived(sp, i)

        replicate("0", True)
        modulation(0, range(12))
        modulate("a0", 0, 1, NT, True, na_w[0] + SLOTS)
        if "stop1" in debug:
            return stop()
        clean_levels()
        for p in range(PAIRS):
            attention(p)
            hgrn(p)
        if "stop2" in debug:
            return stop()
        project_out("e0", evo, A[:, 12032:16128], 2, NT, plain_cols, len(chunks))
        residual_norm("e0", 0, 0, NT, H, None, 0)
        if "stop3" in debug:
            return stop()
        modulate("b0", 3, 4, NT, False, 0)
        moe(0, NT, T, 128)
        if "stop4" in debug:
            return stop()
        residual_norm("f0", 0, 1, NT, Y, 5, 0)

        limit[0] = moe1_at
        clear_gate_weights()
        modulation(1, range(4))
        modulate("a1", 0, 1, NT, True, odi[0] + SLOTS)
        recurrent_unit()
        replicate("1", False)
        modulation(1, range(4, 12))
        pack_latent()
        if "stop5" in debug:
            return stop()
        project_out("o1", odo, A[:, 12288:14336], 2, 2, lambda t, k, i: t[:, HALF * k + P * i:HALF * k + P * i + P], len(chunks))
        residual_norm("e1", 1, 0, 2, H, None, 0)
        modulate("b1", 3, 4, 2, False, 0)
        clear_moe()
        moe(1, 2, HALF, 64)
        residual_norm("f1", 1, 1, 2, Y, 5, 0)
        store()


def _constants(np):
    f = np.float32
    head = np.arange(P) // HD
    lev = np.zeros((2, NL, HD, CH), f)
    s, t = np.meshgrid(np.arange(CH), np.arange(CH), indexing="ij")
    for l, b in enumerate(LEVELS):
        same = (s // b) == (t // b)
        lev[0, l] = same & (s % b < b // 2) & (t % b >= b // 2)
        lev[1, l] = same & (s % b >= b // 2) & (t % b < b // 2)
    lev[:, NL - 1] = s == t
    lev = np.concatenate([lev, lev], 2).transpose(2, 0, 1, 3).reshape(P, -1)
    restart = np.tile((np.arange(T) % CH != 0).astype(f), (P, 1))
    w = np.arange(CH)
    lo = np.clip(w - 8, 0, CH - 16)[:, None]
    inside = (w[None] >= lo) & (w[None] < lo + 16)
    window = np.where(inside, 0.0, -1e30).astype(f)
    return {
        "k_ident": np.eye(P, dtype=f),
        "k_ones64": (head[:, None] == head[None]).astype(f) / HD,
        "k_levmask": np.ascontiguousarray(lev),
        "k_restart": restart,
        "k_iota": np.tile(np.arange(P, dtype=f), (P, 1)),
        "k_columns": np.stack([-np.arange(P), 1024 + np.arange(P), np.arange(P)], 1).astype(f),
        "k_order": np.concatenate([np.triu(np.ones((P, P)), 1),
                                   np.stack([c for i in range(NT) for c in (P * i + np.arange(P) - 1024, np.ones(P))], 1)], 1).astype(f),
        "k_window": np.concatenate([window, window]),
    }


def _bias_layout(rpb, np):
    w = np.arange(CH)
    at = np.clip(w[None, :] - w[:, None] + 15, 0, 30)
    band = rpb[:, :, at]
    first, second = band[:, 5:11], band[:, 4:10]
    both = np.concatenate([first.transpose(2, 0, 1, 3), second.transpose(2, 0, 1, 3)])
    return np.ascontiguousarray(both)


def _vectors(given, np):
    turn = lambda v: v.reshape(-1, P).T
    norm = np.concatenate([given["hg_norm_g"][0]] * 2)
    return np.ascontiguousarray(np.concatenate([turn(v) for v in (
        given["hg_lb_raw"], norm, given["od_conv_w"], given["od_conv_b"], given["lru_b_a"], given["lru_b_x"],
        given["lru_lam"])], 1))


_INS = ["x", "c", "ctx", "c_ctx", "ada_w", "ada_b", "ln_g", "ln_b", "ev_w_in", "ev_w_out", "od_w_in", "lru_w_a", "lru_w_x", "od_w_out",
        "router_w", "router_bias", "exp_w_gate", "exp_w_up", "exp_w_down", "sh_w_gate", "sh_w_up", "sh_w_down"]


def kernel(**inputs):
    import numpy as _np
    import concourse.bacc as _bacc
    from concourse.bass_utils import run_bass_kernel_spmd as _run

    nc = _bacc.Bacc("TRN2", target_bir_lowering=False, num_devices=1)
    arrays, args = {}, {}
    given = {n: _np.ascontiguousarray(inputs[n]) for n in _INS}
    given["rpb_band"] = _bias_layout(_np.asarray(inputs["na_rpb"])[0], _np)
    given["vectors"] = _vectors({n: _np.asarray(inputs[n]) for n in inputs}, _np)
    given.update(_constants(_np))
    for name, v in given.items():
        arrays["in_" + name] = v
        args[name] = nc.dram_tensor("in_" + name, v.shape, F32, kind="ExternalInput").ap()
    out = nc.dram_tensor("out", (HALF, D), F32, kind="ExternalOutput").ap()
    trunk(nc, args, out)
    r = _run(nc, [arrays], core_ids=[0])
    return r.results[0]["out"].reshape(1, HALF, D)
```

```python
from contextlib import ExitStack

import numpy as np

import concourse.bass as bass
from concourse import mybir

F32 = mybir.dt.float32
U32 = mybir.dt.uint32
ALU = mybir.AluOpType
ACT = mybir.ActivationFunctionType
AX_X = mybir.AxisListType.X

P = 128
D = 1024
KD = D // P
T = 512
HALF = 256
NT = T // P
CH = 64
NC = T // CH
HD = 64
PAIRS = 4
LEVELS = (64, 32, 16, 8, 4, 2)
NL = len(LEVELS) + 1
E = 64
HID = 256
TOPK = 6
ROUTED_SCALE = 2.5
ALPHA = 4 ** 0.25
LN_EPS = 1e-5
RMS_EPS = 1e-6
FLOOR = 1e-30
LRU_C = 8.0
SLOT = KD * 512
SLOTS = 3
EXPERT = KD * 512 + 2 * D


class Chain:

    def __init__(self, eng, sem):
        self.eng, self.sem, self.n = eng, sem, 0

    def then(self, ins):
        self.n += 1
        ins.then_inc(self.sem, 1)

    def settle(self):
        self.eng.wait_ge(self.sem, self.n)

    def link(self, ins):
        self.then(ins)
        self.settle()


def trunk(nc, a, out):
    ctx = ExitStack()
    with ctx:
        def sb(name, words):
            return ctx.enter_context(nc.sbuf_tensor(name, [P, words], F32))

        def sem(name):
            return ctx.enter_context(nc.semaphore(name))

        W = sb("W", 18432)
        X = sb("X", NT * D)
        MOD = sb("MOD", 6 * D)
        HT = sb("HT", KD * T)
        A = sb("A", 16128)
        ident = sb("ident", P)
        ones64 = sb("ones64", P)
        levmask = sb("levmask", 2 * NL * CH)
        restart = sb("restart", T)
        iota_s = sb("iota", P)
        iota = iota_s[:, 0:E]
        onesf = sb("onesf", P)
        half = sb("half", 270)
        CR = sb("CR", KD * P)
        small = sb("small", 256)
        gates = sb("gates", NT * E)
        PS = [ctx.enter_context(nc.psum_tensor(f"PS{i}", [P, 512], F32)) for i in range(8)]

        def cut(t, at, *dims):
            n = 1
            for d in dims:
                n *= d
            v = t[:, at:at + n]
            if len(dims) == 2:
                return v.rearrange("p (a b) -> p a b", b=dims[1])
            if len(dims) == 3:
                return v.rearrange("p (a b c) -> p a b c", b=dims[1], c=dims[2])
            return v

        Xt = cut(X, 0, NT, D)
        HTt = cut(HT, 0, KD, T)
        eps = small[:, 0:1]
        pcols = small[:, 241:244]
        rmseps = small[:, 1:2]
        cT = small[:, 8:24]
        lbr = small[:, 128:136]
        normg = small[:, 136:137]
        convw = small[:, 137:169]
        convb = small[:, 169:177]
        gbias = small[:, 177:209]
        lam = small[:, 209:225]
        lb = small[:, 32:40]
        omlb = small[:, 40:48]
        stats = small[:, 64:64 + 12]
        mv = small[:, 80:82]
        rstd = small[:, 82:84]
        chain = {n: sem("chain_" + n) for n in ("dve", "act", "pool")}
        DV = Chain(nc.vector, chain["dve"])
        AC = Chain(nc.scalar, chain["act"])
        GP = Chain(nc.gpsimd, chain["pool"])

        chunks = []

        def chunk(*parts):
            chunks.append(parts)
            return len(chunks) - 1

        rows = lambda w: w.rearrange("(p k) n -> p k n", k=KD)
        ada_chunk = lambda l, n: chunk(rows(a["ada_w"][l])[:, :, 512 * n:512 * n + 512])
        ada = [[ada_chunk(0, n) for n in range(12)], []]
        ev = rows(a["ev_w_in"][0])
        col = lambda part, p: ev[:, :, 512 * part + P * p:512 * part + P * p + P]
        na_w, hz_w, hv_w = [], [], []
        for p in range(PAIRS):
            na_w.append(chunk(col(0, p), col(1, p), col(2, p)))
            hz_w.append(chunk(col(3, p), col(4, p), col(5, p)))
            hv_w.append(chunk(col(6, p), col(7, p)))
        nat = lambda w: w.rearrange("(k p) n -> p k n", p=P)
        evo = [chunk(nat(a["ev_w_out"][0])[:, :, 512 * n:512 * n + 512]) for n in range(2)]
        moe0_at = len(chunks)
        ada[1] += [ada_chunk(1, n) for n in range(4)]
        odi_chunk = lambda n: chunk(rows(a["od_w_in"][0])[:, :, 512 * n:512 * n + 512])
        odi = [odi_chunk(0), odi_chunk(1)]
        ada[1] += [ada_chunk(1, 4), ada_chunk(1, 5)]
        odi.append(odi_chunk(2))
        ada[1] += [ada_chunk(1, 6), ada_chunk(1, 7)]
        odi.append(odi_chunk(3))
        ada[1] += [ada_chunk(1, n) for n in range(8, 12)]
        odo = [chunk(nat(a["od_w_out"][0])[:, :, 512 * n:512 * n + 512]) for n in range(2)]
        moe1_at = len(chunks)

        slot_sem = [sem(f"slot{i}") for i in range(SLOTS)]
        chunk_used = sem("chunk_used")
        landed, count = [], [0] * SLOTS
        for i, parts in enumerate(chunks):
            count[i % SLOTS] += 16 * len(parts)
            landed.append(count[i % SLOTS])
        sent, limit = [0], [moe0_at]

        def view(i, part=0):
            at = SLOT * (i % SLOTS)
            for q in chunks[i][:part]:
                at += q.shape[1] * q.shape[2]
            return cut(W, at, *chunks[i][part].shape[1:])

        def send(sp, upto):
            while sent[0] < min(upto, limit[0]):
                i = sent[0]
                if i >= SLOTS:
                    sp.wait_ge(chunk_used, i - SLOTS + 1)
                for j, q in enumerate(chunks[i]):
                    sp.dma_start(view(i, j), q).then_inc(slot_sem[i % SLOTS], 16)
                sent[0] += 1

        def arrived(eng, i):
            eng.wait_ge(slot_sem[i % SLOTS], landed[i])

        with nc.Block() as block:
            const = sem("const")
            cond = sem("cond")

            @block.sync
            def _(sp):
                sp.dma_start(cut(small, 8, 8), a["c_ctx"].rearrange("(p k) -> p k", k=KD)).then_inc(const, 16)
                sp.dma_start(cut(small, 16, 8), a["c"][0].rearrange("(p k) -> p k", k=KD)).then_inc(const, 16)
                sp.dma_start(small[:, 128:225], a["vectors"]).then_inc(const, 16)
                send(sp, 3)
                sp.wait_ge(const, 16 * 3)

            @block.gpsimd
            def _(pool):
                pool.memset(A[:, 256:], 0.0)
                pool.memset(onesf[:], 1.0)
                pool.memset(small[:, 0:1], LN_EPS)
                pool.memset(small[:, 1:2], RMS_EPS)

            @block.scalar
            def _(act):
                act.wait_ge(const, 16 * 3)
                act.activation(cT, cT, ACT.Silu).then_inc(cond, 1)

        CRs = [CR[:, P * k:P * k + P] for k in range(KD)]
        CR1 = [levmask[:, P * k:P * k + P] for k in range(KD - 1)] + [restart[:, 0:P]]

        def replicate():
            with nc.Block() as block:
                @block.vector
                def _(dve):
                    for k in range(KD):
                        dve.tensor_copy(CRs[k][:, 0:64], cT[:, k:k + 1].broadcast_to([P, 64]))
                        dve.tensor_copy(CRs[k][:, 64:128], cT[:, 8 + k:9 + k].broadcast_to([P, 64]))

        with nc.Block() as block:
            lbs = sem("lbs")

            @block.vector
            def _(dve):
                DV.link(dve.tensor_tensor(lb, lbr, lbr, ALU.subtract))
                dve.wait_ge(cond, 1)
                dve.nop().then_inc(lbs, 1)
                dve.wait_ge(lbs, 2)
                DV.link(dve.reciprocal(omlb, lb))
                DV.link(dve.tensor_tensor(lb, lb, omlb, ALU.mult))
                DV.link(dve.tensor_tensor(lb, lb, lb, ALU.subtract))
                DV.link(dve.tensor_scalar(omlb, lb, -1.0, 1.0, ALU.mult, ALU.add))

            @block.scalar
            def _(act):
                act.wait_ge(lbs, 1)
                act.activation(lb, lb, ACT.Exp).then_inc(lbs, 1)

        def load_constants(sp):
            for t, name in ((ident, "k_ident"), (ones64, "k_ones64"), (levmask, "k_levmask"),
                            (restart, "k_restart"), (iota_s, "k_iota")):
                sp.dma_start(t[:], a[name]).then_inc(const, 16)
            sp.dma_start(pcols, a["k_columns"]).then_inc(const, 16)
            sp.dma_start(A[:, 0:P + 8], a["k_order"]).then_inc(const, 16)
            for s, name in enumerate(("ctx", "x")):
                sp.dma_start(Xt[64 * s:64 * s + 64], a[name][0].rearrange("(i n) d -> n i d", n=CH)).then_inc(const, 16)

        def convert_constants(dve):
            dve.wait_ge(const, 16 * 12)
            f16 = lambda lo, hi: half[:, lo:hi].bitcast(mybir.dt.float16)
            dve.tensor_copy(f16(0, 64), A[:, 0:P])
            dve.memset(f16(64, 128), 1.0)
            dve.tensor_copy(f16(128, 132), A[:, P:P + 8])

        def modulation_steps(l, ns):
            bias_in, added = sem(f"bias_in{l}{ns[0]}"), sem(f"mod_added{l}{ns[0]}")
            cr = CRs if ns[0] == 0 else CR1
            banks = PS[6:8] if ns[0] == 4 else PS[0:4]
            nb = len(banks)
            lo, hi = 512 * ns[0], 512 * ns[-1] + 512

            def loads(sp):
                sp.dma_start(MOD[:, lo:hi], a["ada_b"][l:l + 1, lo:hi].broadcast_to([P, hi - lo])).then_inc(bias_in, 16)
                send(sp, ada[l][ns[0]] + 2 + SLOTS)
                if l == 0:
                    load_constants(sp)
                send(sp, ada[l][ns[-1]] + 1 + SLOTS)

            def products(pe, which=None):
                for j, n in list(enumerate(ns))[which or slice(None)]:
                    i = ada[l][n]
                    arrived(pe, i)
                    if j >= nb:
                        pe.wait_ge(added, j - nb + 1)
                    for k in range(KD):
                        mm = pe.matmul(banks[j % nb][:], cr[k], view(i)[:, k, :], start=(k == 0), stop=(k == KD - 1))
                    mm.then_inc(chunk_used, 1)

            def sums(dve, which=None):
                dve.wait_ge(bias_in, 16)
                for j, n in list(enumerate(ns))[which or slice(None)]:
                    dve.wait_ge(chunk_used, ada[l][n] + 1)
                    m = MOD[:, 512 * n:512 * n + 512]
                    dve.tensor_tensor(m, banks[j % nb][:], m, ALU.add).then_inc(added, 1)
                if l == 0:
                    convert_constants(dve)

            return loads, products, sums

        def modulation(l, ns):
            loads, products, sums = modulation_steps(l, ns)
            with nc.Block() as block:
                @block.sync
                def _(sp):
                    loads(sp)

                @block.tensor
                def _(pe):
                    products(pe)

                @block.vector
                def _(dve):
                    sums(dve)

        H = cut(A, 0, NT, D)

        def modulate(tag, shift, scale, nt, mixed, upto, clear=None):
            h_ready, turned, copied = sem("h_ready" + tag), sem("turned" + tag), sem("copied" + tag)
            if mixed:
                cols = HT[:].rearrange("p (k s i n) -> p k s i n", k=KD, s=2, i=NT)
            with nc.Block() as block:
                @block.sync
                def _(sp):
                    send(sp, upto)

                @block.gpsimd
                def _(pool):
                    if clear is not None:
                        pool.memset(clear, 0.0)

                @block.vector
                def _(dve):
                    for i in range(nt):
                        DV.link(dve.scalar_tensor_tensor(H[:, i, :], MOD[:, D * scale:D * scale + D], 1.0, Xt[:, i, :], ALU.add, ALU.mult))
                        dve.tensor_tensor(H[:, i, :], H[:, i, :], MOD[:, D * shift:D * shift + D], ALU.add).then_inc(h_ready, 1)

                @block.tensor
                def _(pe):
                    for i in range(nt):
                        pe.wait_ge(h_ready, i + 1)
                        h = H[:, i, :].rearrange("t (p k) -> t k p", k=KD)
                        for g in range(2):
                            b = (2 * i + g) % 4
                            if 2 * i + g >= 4:
                                pe.wait_ge(copied, 2 * i + g - 3)
                            for k in range(4):
                                tr = pe.transpose(PS[b][:, P * k:P * k + P], h[:, 4 * g + k, :], ident[:])
                            tr.then_inc(turned, 1)

                @block.scalar
                def _(act):
                    for i in range(nt):
                        for g in range(2):
                            act.wait_ge(turned, 2 * i + g + 1)
                            src = PS[(2 * i + g) % 4]
                            if mixed:
                                for s in range(2):
                                    ins = act.activation(cols[:, 4 * g:4 * g + 4, s, i, :],
                                                         src[:].rearrange("p (k s n) -> p k s n", s=2, n=CH)[:, :, s, :], ACT.Copy)
                            else:
                                ins = act.activation(HTt[:, 4 * g:4 * g + 4, P * i:P * i + P],
                                                     src[:].rearrange("p (k n) -> p k n", n=P), ACT.Copy)
                            ins.then_inc(copied, 1)

        LNG, LNB = cut(A, 8192, D), cut(A, 8192 + D, D)

        def project_out(tag, cks, srcT, gate, nt, lhs, upto):
            done, freed = sem("out_done" + tag), sem("out_freed" + tag)
            with nc.Block() as block:
                @block.sync
                def _(sp):
                    send(sp, upto)

                @block.tensor
                def _(pe):
                    for n in range(2):
                        arrived(pe, cks[n])
                        for i in range(nt):
                            j = nt * n + i
                            if j >= 4:
                                pe.wait_ge(freed, j - 3)
                            for k in range(KD):
                                mm = pe.matmul(PS[j % 4][:], lhs(srcT, k, i), view(cks[n])[:, k, :], start=(k == 0), stop=(k == KD - 1))
                            if i == nt - 1:
                                mm.then_inc(chunk_used, 1)
                            else:
                                mm.then_inc(done, 1)

                @block.vector
                def _(dve):
                    for n in range(2):
                        for i in range(nt):
                            if i == nt - 1:
                                dve.wait_ge(chunk_used, cks[n] + 1)
                            else:
                                dve.wait_ge(done, (nt - 1) * n + i + 1)
                            dve.tensor_tensor(H[:, i, 512 * n:512 * n + 512], PS[(nt * n + i) % 4][:],
                                              MOD[:, D * gate + 512 * n:D * gate + 512 * n + 512], ALU.mult).then_inc(freed, 1)

        def residual_norm(tag, l, which, nt, src, gate, upto, beside=None):
            ln_in, var, root, normed = sem("ln_in" + tag), sem("ln_var" + tag), sem("ln_root" + tag), sem("ln_normed" + tag)
            with nc.Block() as block:
                @block.sync
                def _(sp):
                    sp.dma_start(LNG, a["ln_g"][l, which:which + 1, :].broadcast_to([P, D])).then_inc(ln_in, 16)
                    sp.dma_start(LNB, a["ln_b"][l, which:which + 1, :].broadcast_to([P, D])).then_inc(ln_in, 16)
                    if beside:
                        beside[0](sp)
                    send(sp, upto)

                @block.tensor
                def _(pe):
                    if beside:
                        beside[1](pe)

                @block.vector
                def _(dve):
                    for i in range(nt):
                        x = Xt[:, i, :]
                        if gate is not None:
                            DV.link(dve.tensor_tensor(src[:, i, :], src[:, i, :], MOD[:, D * gate:D * gate + D], ALU.mult))
                        DV.link(dve.scalar_tensor_tensor(x, x, ALPHA, src[:, i, :], ALU.mult, ALU.add))
                        for s in range(2):
                            DV.then(dve.bn_stats(stats[:, 6 * s:6 * s + 6], x[:, 512 * s:512 * s + 512]))
                        DV.settle()
                        dve.bn_aggr(mv, stats).then_inc(var, 1)
                        dve.wait_ge(root, i + 1)
                        DV.link(dve.reciprocal(rstd[:, 1:2], rstd[:, 0:1]))
                        ins = dve.tensor_scalar(x, x, mv[:, 0:1], rstd[:, 1:2], ALU.subtract, ALU.mult)
                        if i < nt // 2:
                            ins.then_inc(normed, 1)
                        else:
                            DV.link(ins)
                            dve.wait_ge(ln_in, 32)
                            DV.link(dve.tensor_tensor(x, x, LNG, ALU.mult))
                            dve.tensor_tensor(x, x, LNB, ALU.add)
                    if beside:
                        beside[2](dve)

                @block.scalar
                def _(act):
                    for i in range(nt):
                        act.wait_ge(var, i + 1)
                        act.activation(rstd[:, 0:1], mv[:, 1:2], ACT.Sqrt, bias=eps).then_inc(root, 1)

                @block.gpsimd
                def _(pool):
                    pool.wait_ge(ln_in, 32)
                    for i in range(nt // 2):
                        x = Xt[:, i, :]
                        pool.wait_ge(normed, i + 1)
                        GP.link(pool.tensor_tensor(x, x, LNG, ALU.mult))
                        pool.tensor_tensor(x, x, LNB, ALU.add)

        plain_cols = lambda t, k, i: t[:, T * k + P * i:T * k + P * i + P]

        mixT = cut(A, 12032, 2 * PAIRS, T)
        by_tile = lambda v: v.rearrange("p (i s n) -> p s i n", s=2, n=CH)
        TAIL = SLOTS * SLOT

        def tail(at, *dims):
            return cut(W, TAIL + at, *dims)

        qT, kT, vT = tail(0, T), tail(512, T), tail(1024, NT, P)
        BT = tail(1536, 2, 6, CH)
        Sb = [tail(2304 + 512 * i, 512) for i in range(2)]
        Pr = [tail(3328 + 512 * i, 512) for i in range(2)]
        PT = [tail(4352 + 512 * i, 512) for i in range(2)]
        window = cut(MOD, 448, CH)
        na = {n: sem("na_" + n) for n in ("proj", "evac", "bias_in", "bias", "score", "biased", "negmax", "exp", "prob", "turn",
                                          "turned", "pv", "win")}
        UNITS = [(t, h) for t in range(NT) for h in range(2)]
        NU = len(UNITS)

        hg = {n: sem("hg_" + n) for n in (
            "proj", "query", "values", "gate", "sig", "forget", "log", "cum", "factor", "inter", "kturn", "kturned",
            "update", "state", "diff", "exp", "level", "diag", "score", "masked", "summed", "out", "out1", "osum", "square",
            "mean", "root", "clean")}

        def attention(p):
            i = na_w[p]
            with nc.Block() as block:
                @block.sync
                def _(sp):
                    if p == 0:
                        sp.dma_start(window, a["k_window"]).then_inc(na["win"], 16)
                    sp.dma_start(BT, a["rpb_band"][:, 2 * p:2 * p + 2]).then_inc(na["bias_in"], 16)
                    send(sp, i + 1 + SLOTS)

                @block.gpsimd
                def _(pool):
                    if p == 0:
                        pool.memset(A[:, 0:4096], 0.0)

                @block.tensor
                def _(pe):
                    arrived(pe, i)
                    for part in range(2):
                        for k in range(KD):
                            mm = pe.matmul(PS[part][:], view(i, part)[:, k, :], HTt[:, k, :], start=(k == 0), stop=(k == KD - 1))
                        mm.then_inc(na["proj"], 1)
                    for t in range(NT):
                        for k in range(KD):
                            mm = pe.matmul(PS[2][:, P * t:P * t + P], HTt[:, k, P * t:P * t + P], view(i, 2)[:, k, :],
                                           start=(k == 0), stop=(k == KD - 1))
                    mm.then_inc(chunk_used, 1)
                    pe.wait_ge(na["evac"], 3 * p + 3)

                    def scores(u):
                        t, h = UNITS[u]
                        if u >= 2:
                            pe.wait_ge(na["exp"], NU * p + u - 1)
                        n = T if t >= 2 else HALF
                        pe.matmul(PS[3 + h][:, 0:n], qT[64 * h:64 * h + 64, P * t:P * t + P], kT[64 * h:64 * h + 64, 0:n],
                                  start=True, stop=True).then_inc(na["score"], 1)

                    def recurrence_products(lo, hi):
                        for m in range(lo, hi):
                            part, k = m // KD, m % KD
                            mm = pe.matmul(PS[part][:], view(hz_w[p], part)[:, k, :], HTt[:, k, :], start=(k == 0), stop=(k == KD - 1))
                            if k == KD - 1:
                                mm.then_inc(chunk_used if part == 2 else hg["proj"], 1)

                    scores(0)
                    arrived(pe, hz_w[p])
                    for u, (t, h) in enumerate(UNITS):
                        if u + 1 < NU:
                            scores(u + 1)
                        recurrence_products(3 * u, 3 * u + 3)
                        kt = 4 if t >= 2 else 2
                        pe.wait_ge(na["prob"], NU * p + u + 1)
                        if u >= 2:
                            pe.wait_ge(na["turned"], NU * p + u - 1)
                        for j in range(kt):
                            tr = pe.transpose(PS[5 + u % 2][:, P * j:P * j + P], Pr[u % 2][:, P * j:P * j + P], ident[:])
                        tr.then_inc(na["turn"], 1)
                        pe.wait_ge(na["turned"], NU * p + u + 1)
                        for j in range(kt):
                            mm = pe.matmul(PS[7][64 * h:64 * h + 64, P * t:P * t + P], vT[:, j, 64 * h:64 * h + 64],
                                           PT[u % 2][:, P * j:P * j + P], start=(j == 0), stop=(j == kt - 1))
                        mm.then_inc(na["pv"], 1)

                @block.scalar
                def _(act):
                    act.wait_ge(na["proj"], 2 * p + 1)
                    act.activation(qT, PS[0][:], ACT.Copy, scale=HD ** -0.5).then_inc(na["evac"], 1)
                    act.wait_ge(na["proj"], 2 * p + 2)
                    act.activation(kT, PS[1][:], ACT.Copy).then_inc(na["evac"], 1)
                    act.wait_ge(chunk_used, i + 1)
                    act.activation(vT, PS[2][:].rearrange("p (t n) -> p t n", n=P), ACT.Copy).then_inc(na["evac"], 1)

                    def turned(u):
                        t, h = UNITS[u]
                        n = T if t >= 2 else HALF
                        act.wait_ge(na["turn"], NU * p + u + 1)
                        if u >= 2:
                            act.wait_ge(na["pv"], NU * p + u - 1)
                        act.activation(PT[u % 2][:, 0:n], PS[5 + u % 2][:, 0:n], ACT.Copy).then_inc(na["turned"], 1)

                    for u, (t, h) in enumerate(UNITS):
                        act.wait_ge(na["negmax"], NU * p + u + 1)
                        if u >= 2:
                            act.wait_ge(na["turn"], NU * p + u - 1)
                        if t >= 2:
                            src, n = Sb[u % 2], T
                        else:
                            src, n = PS[3 + h][:, 0:HALF], HALF
                        act.activation(Pr[u % 2][:, 0:n], src, ACT.Exp, bias=small[:, 88 + u % 2:89 + u % 2],
                                       accum_out=small[:, 90 + u % 2:91 + u % 2]).then_inc(na["exp"], 1)
                        if u >= 1:
                            turned(u - 1)
                    turned(NU - 1)
                    act.wait_ge(na["pv"], NU * (p + 1))
                    act.activation(by_tile(mixT[:, p, :]), PS[7][:].rearrange("p (s i n) -> p s i n", s=2, n=CH), ACT.Copy)

                @block.vector
                def _(dve):
                    if p == 0:
                        dve.wait_ge(na["win"], 16)
                    dve.wait_ge(na["bias_in"], 16 * (p + 1))
                    bt = BT.rearrange("p h o w -> p (h o) w") if len(BT.shape) == 4 else BT
                    DV.link(dve.tensor_tensor(bt, bt, window.unsqueeze(1).broadcast_to([P, 12, CH]), ALU.add))
                    band = tail(1536, 2, 6 * CH)

                    def norm(u):
                        t, h = UNITS[u]
                        n = T if t >= 2 else HALF
                        dve.wait_ge(na["exp"], NU * p + u + 1)
                        r = small[:, 92 + u % 2:93 + u % 2]
                        DV.link(dve.reciprocal(r, small[:, 90 + u % 2:91 + u % 2]))
                        dve.tensor_scalar(Pr[u % 2][:, 0:n], Pr[u % 2][:, 0:n], r, None, ALU.mult).then_inc(na["prob"], 1)

                    for u, (t, h) in enumerate(UNITS):
                        dve.wait_ge(na["score"], NU * p + u + 1)
                        ps = PS[3 + h]
                        if t >= 2:
                            if u >= 2:
                                dve.wait_ge(na["exp"], NU * p + u - 1)
                            DV.then(dve.tensor_copy(Sb[u % 2][:, 0:HALF], ps[:, 0:HALF]))
                            at = CH * (2 - 2 * (t - 2))
                            DV.link(dve.tensor_tensor(Sb[u % 2][:, HALF:T], ps[:, HALF:T], band[:, h, at:at + HALF], ALU.add))
                            src = Sb[u % 2]
                        else:
                            src = ps[:, 0:HALF]
                        dve.tensor_reduce(small[:, 88 + u % 2:89 + u % 2], src, AX_X, ALU.max, negate=True).then_inc(na["negmax"], 1)
                        if u >= 1:
                            norm(u - 1)
                    norm(NU - 1)

        HQ, SG, F, KK, CUM, QS, KS = (tail(512 * n, T) for n in range(7))
        KST = tail(3584, NT, P)
        DD = [tail(4096 + HALF * n, HALF) for n in range(2)]
        EE = [tail(4608 + HALF * n, HALF) for n in range(2)]
        OS, SQ = tail(5120, T), tail(5632, T)
        NCH = NC // 2
        KB = [cut(A, 3584 * n, NL * NCH, P) for n in range(2)]
        QB = [cut(A, 7168 + 1536 * n, NL - 1, HALF) for n in range(2)]
        VB = cut(A, 10240, NC, P)
        MK = [cut(A, 11264, NL, CH), cut(MOD, 0, NL, CH)]
        SM = [cut(A, 11712 + CH * n, CH) for n in range(2)]
        ST = cut(MOD, 1024, NC, P)
        V = cut(MOD, 512, NT, P)
        TL, ET = small[:, 96:104], small[:, 104:112]
        lm = cut(levmask, 0, 2 * NL, CH)
        ORDER = [list(range(NC)), [3, 2, 1, 0, 7, 6, 5, 4]]

        def hgrn(p):
            iz, iv = hz_w[p], hv_w[p]
            U = [(d, hf) for d in range(2) for hf in range(2)]
            with nc.Block() as block:
                @block.sync
                def _(sp):
                    send(sp, iv + 1 + SLOTS)

                @block.tensor
                def _(pe):
                    arrived(pe, iv)
                    for t in range(NT):
                        for k in range(KD):
                            mm = pe.matmul(PS[3][:, P * t:P * t + P], HTt[:, k, P * t:P * t + P], view(iv, 0)[:, k, :],
                                           start=(k == 0), stop=(k == KD - 1))
                    mm.then_inc(hg["proj"], 1)
                    for k in range(KD):
                        mm = pe.matmul(PS[4][:], view(iv, 1)[:, k, :], HTt[:, k, :], start=(k == 0), stop=(k == KD - 1))
                    mm.then_inc(chunk_used, 1)

                    def turn_keys(d):
                        pe.wait_ge(hg["inter"], 2 * p + d + 1)
                        if d:
                            pe.wait_ge(hg["kturned"], 2 * p + d)
                        for t in range(NT):
                            tr = pe.transpose(PS[6][:, P * t:P * t + P], KS[:, P * t:P * t + P], ident[:])
                        tr.then_inc(hg["kturn"], 1)

                    def updates(d):
                        pe.wait_ge(hg["kturned"], 2 * p + d + 1)
                        pe.wait_ge(hg["values"], p + 1)
                        if d:
                            pe.wait_ge(hg["state"], 2 * p + d)
                        for t in range(NT):
                            for j in range(2):
                                mm = pe.matmul(PS[3 + 2 * j][:, P * t:P * t + P], KST[64 * j:64 * j + 64, t, :],
                                               V[64 * j:64 * j + 64, t, :], start=True, stop=True)
                        mm.then_inc(hg["update"], 1)

                    def level_scores(n, c):
                        d, hf = U[n]
                        s = NCH * n + c
                        if s >= 2:
                            pe.wait_ge(hg["masked"], 16 * p + s - 1)
                        for l in range(NL):
                            rhs = QB[n % 2][:, l, CH * c:CH * c + CH] if l < NL - 1 else HQ[:, HALF * hf + CH * c:HALF * hf + CH * c + CH]
                            mm = pe.matmul(PS[4 * (s % 2)][:, CH * l:CH * l + CH], KB[n % 2][:, NCH * l + c, :], rhs, start=True, stop=True)
                        mm.then_inc(hg["score"], 1)

                    def outputs(n, c):
                        d, hf = U[n]
                        s = NCH * n + c
                        g = NCH * hf + c
                        o = PS[(7, 1)[d]][:, CH * g:CH * g + CH]
                        pe.wait_ge(hg["summed"], 16 * p + s + 1)
                        pe.matmul(o, VB[:, g, :], SM[s % 2], start=True, stop=False)
                        pe.matmul(o, ST[:, g, :], QS[:, CH * g:CH * g + CH], start=False, stop=True).then_inc(hg["out"], 1)

                    for n, (d, hf) in enumerate(U):
                        if hf == 0:
                            turn_keys(d)
                            updates(d)
                        if n == 0:
                            pe.wait_ge(hg["query"], p + 1)
                            pe.wait_ge(hg["gate"], p + 1)
                        pe.wait_ge(hg["level"], 6 * (4 * p + n + 1))
                        pe.wait_ge(hg["diag"], 4 * p + n + 1)
                        level_scores(n, 0)
                        if hf == 0:
                            pe.wait_ge(hg["state"], 2 * p + d + 1)
                        for c in range(NCH):
                            if c + 1 < NCH:
                                level_scores(n, c + 1)
                            outputs(n, c)
                    pe.wait_ge(hg["square"], p + 1)
                    pe.matmul(PS[3][:], ones64[:], SQ, start=True, stop=True).then_inc(hg["mean"], 1)

                @block.scalar
                def _(act):
                    def sigmoids(d):
                        z = PS[1 + d]
                        act.activation(F, z[:], ACT.Sigmoid)
                        act.activation(KK, z[:], ACT.Sigmoid, scale=-1.0).then_inc(hg["sig"], 1)

                    def exps(n):
                        for l in range(NL - 1):
                            s = 24 * p + 6 * n + l
                            act.wait_ge(hg["diff"], s + 1)
                            if s % 24 >= 2:
                                act.wait_ge(hg["level"], s - 1)
                            act.activation(EE[l % 2], DD[l % 2], ACT.Exp).then_inc(hg["exp"], 1)

                    act.wait_ge(hg["proj"], 3 * p + 1)
                    act.activation(HQ, PS[0][:], ACT.Silu).then_inc(hg["query"], 1)
                    act.wait_ge(hg["proj"], 3 * p + 2)
                    sigmoids(0)
                    act.wait_ge(hg["proj"], 3 * p + 3)
                    src = PS[3][:].rearrange("p (t n) -> p t n", n=P)
                    act.activation(V, src, ACT.Copy)
                    for j in range(2):
                        for h in range(2):
                            ins = act.activation(VB[64 * h:64 * h + 64, j::2, 64 * h:64 * h + 64],
                                                 src[64 * j:64 * j + 64, :, 64 * h:64 * h + 64], ACT.Copy)
                    ins.then_inc(hg["values"], 1)
                    act.wait_ge(chunk_used, iv + 1)
                    act.activation(SG, PS[4][:], ACT.Silu).then_inc(hg["gate"], 1)
                    for n, (d, hf) in enumerate(U):
                        if hf == 0:
                            if d:
                                act.wait_ge(hg["level"], 24 * p + 12)
                                act.wait_ge(hg["diag"], 4 * p + 2)
                                sigmoids(1)
                            act.wait_ge(hg["forget"], 2 * p + d + 1)
                            act.activation(F, F, ACT.Ln).then_inc(hg["log"], 1)
                            act.wait_ge(hg["cum"], 2 * p + d + 1)
                        if n == 2:
                            exps(n)
                        if hf == 0:
                            if d:
                                act.wait_ge(hg["out"], 16 * p + 8)
                                act.wait_ge(hg["kturn"], 2 * p + 1)
                            act.activation(ET, TL, ACT.Exp)
                            act.activation((QS, KS)[d], CUM, ACT.Exp)
                            act.activation((KS, QS)[d], F, ACT.Exp).then_inc(hg["factor"], 1)
                            act.wait_ge(hg["kturn"], 2 * p + d + 1)
                            if d:
                                act.wait_ge(hg["update"], 2 * p + d)
                            act.activation(KST, PS[6][:].rearrange("p (t n) -> p t n", n=P), ACT.Copy).then_inc(hg["kturned"], 1)
                        if n != 2:
                            exps(n)
                    act.wait_ge(hg["out"], 16 * p + 16)
                    act.activation(OS, PS[1][:], ACT.Copy).then_inc(hg["out1"], 1)
                    act.wait_ge(hg["osum"], p + 1)
                    act.activation(SQ, OS, ACT.Square).then_inc(hg["square"], 1)
                    act.wait_ge(hg["mean"], p + 1)
                    act.activation(SQ, PS[3][:], ACT.Sqrt, bias=rmseps).then_inc(hg["root"], 1)

                @block.gpsimd
                def _(pool):
                    pool.memset(ST, 0.0).then_inc(hg["clean"], 1)
                    pool.wait_ge(hg["clean"], p + 1)
                    for n, (d, hf) in enumerate(U):
                        pool.wait_ge(hg["cum"], 2 * p + d + 1)
                        if n:
                            pool.wait_ge(hg["diff"], 24 * p + 6 * n)
                        if n >= 2:
                            pool.wait_ge(hg["score"], 16 * p + NCH * (n - 1))
                        for h in range(2):
                            r = slice(64 * h, 64 * h + 64)
                            ins = pool.tensor_copy(KB[n % 2][r, NCH * (NL - 1):, r],
                                                   KK[r, HALF * hf:HALF * hf + HALF].rearrange("p (c s) -> p c s", s=CH))
                        ins.then_inc(hg["diag"], 1)
                        pool.wait_ge(hg["diag"], 4 * p + n + 1)
                        for l, b in enumerate(LEVELS):
                            s = 24 * p + 6 * n + l
                            if s % 24 >= 2:
                                pool.wait_ge(hg["exp"], s - 1)
                            m = b // 2 - 1 + d
                            v = CUM[:, HALF * hf:HALF * hf + HALF].rearrange("p (n b) -> p n b", b=b)
                            o = DD[l % 2].rearrange("p (n b) -> p n b", b=b)
                            ref = v[:, :, m:m + 1].broadcast_to([P, HALF // b, b // 2])
                            pool.tensor_tensor(o[:, :, 0:b // 2], ref, v[:, :, 0:b // 2], ALU.subtract)
                            pool.tensor_tensor(o[:, :, b // 2:], v[:, :, b // 2:], ref, ALU.subtract).then_inc(hg["diff"], 1)

                @block.vector
                def _(dve):
                    dve.wait_ge(hg["query"], p + 1)
                    DV.link(dve.tensor_scalar(HQ, HQ, HD ** -0.5, None, ALU.mult))
                    def forget(d):
                        j = PAIRS * d + p
                        dve.wait_ge(hg["sig"], 2 * p + d + 1)
                        DV.then(dve.tensor_scalar(F, F, omlb[:, j:j + 1], lb[:, j:j + 1], ALU.mult, ALU.add))
                        DV.then(dve.tensor_scalar(KK, KK, omlb[:, j:j + 1], None, ALU.mult))
                        DV.settle()
                        dve.tensor_scalar(F, F, FLOOR, None, ALU.max).then_inc(hg["forget"], 1)

                    def decays(d):
                        dve.wait_ge(hg["log"], 2 * p + d + 1)
                        if d:
                            dve.wait_ge(hg["diff"], 24 * p + 12)
                        DV.link(dve.tensor_tensor_scan(CUM, restart[:], F, 0.0, ALU.mult, ALU.add))
                        c3 = CUM.rearrange("p (c s) -> p c s", s=CH)
                        DV.link(dve.tensor_copy(TL, c3[:, :, CH - 1]))
                        if d:
                            DV.link(dve.tensor_tensor(CUM, CUM, F, ALU.subtract))
                        dve.tensor_tensor(F.rearrange("p (c s) -> p c s", s=CH), TL.unsqueeze(2).broadcast_to([P, NC, CH]),
                                          c3, ALU.subtract).then_inc(hg["cum"], 1)

                    def factors(d):
                        dve.wait_ge(hg["factor"], 2 * p + d + 1)
                        DV.link(dve.tensor_tensor(QS, QS, HQ, ALU.mult))
                        dve.tensor_tensor(KS, KS, KK, ALU.mult).then_inc(hg["inter"], 1)

                    def levels(n, lo, hi):
                        d, hf = U[n]
                        if n >= 2:
                            dve.wait_ge(hg["score"], 16 * p + NCH * (n - 1))
                        for l in range(lo, hi):
                            b = LEVELS[l]
                            dve.wait_ge(hg["exp"], 24 * p + 6 * n + l + 1)
                            ksl = slice(0, b // 2) if d == 0 else slice(b // 2, b)
                            qsl = slice(b // 2, b) if d == 0 else slice(0, b // 2)
                            blk = lambda v: v.rearrange("p (n b) -> p n b", b=b)
                            dve.tensor_tensor(blk(QB[n % 2][:, l, :])[:, :, qsl], blk(EE[l % 2])[:, :, qsl],
                                              blk(HQ[:, HALF * hf:HALF * hf + HALF])[:, :, qsl], ALU.mult)
                            four = lambda v: v.rearrange("p c (n b) -> p c n b", b=b)
                            for h in range(2):
                                r = slice(64 * h, 64 * h + 64)
                                e3 = EE[l % 2][r, :].rearrange("p (c s) -> p c s", s=CH)
                                k3 = KK[r, HALF * hf:HALF * hf + HALF].rearrange("p (c s) -> p c s", s=CH)
                                ins = dve.tensor_tensor(four(KB[n % 2][r, NCH * l:NCH * l + NCH, r])[:, :, :, ksl],
                                                        four(e3)[:, :, :, ksl], four(k3)[:, :, :, ksl], ALU.mult)
                            ins.then_inc(hg["level"], 1)

                    def states(d):
                        dve.wait_ge(hg["update"], 2 * p + d + 1)
                        dve.wait_ge(hg["clean"], p + 1)
                        if d:
                            dve.wait_ge(hg["out"], 16 * p + 8)
                        o = ORDER[d]
                        for h in range(2):
                            DV.then(dve.memset(ST[64 * h:64 * h + 64, o[0], 64 * h:64 * h + 64], 0.0))
                        DV.settle()
                        for q in range(NC - 1):
                            for h in range(2):
                                r = slice(64 * h, 64 * h + 64)
                                upd = PS[3 + 2 * (o[q] % 2)][r, P * (o[q] // 2) + 64 * h:P * (o[q] // 2) + 64 * h + 64]
                                ins = dve.scalar_tensor_tensor(ST[r, o[q + 1], r], ST[r, o[q], r], ET[r, o[q]:o[q] + 1], upd,
                                                               ALU.mult, ALU.add)
                                if q < NC - 2 or h == 0:
                                    DV.then(ins)
                                else:
                                    ins.then_inc(hg["state"], 1)
                            if q < NC - 2:
                                DV.settle()

                    def mask(n, c):
                        d, hf = U[n]
                        s = NCH * n + c
                        dve.wait_ge(hg["score"], 16 * p + s + 1)
                        dve.tensor_tensor(MK[s % 2], PS[4 * (s % 2)][:, 0:NL * CH].rearrange("p (l t) -> p l t", t=CH),
                                          lm[:, NL * d:NL * d + NL, :], ALU.mult).then_inc(hg["masked"], 1)
                        dve.wait_ge(hg["masked"], 16 * p + s + 1)
                        if s >= 2:
                            dve.wait_ge(hg["out"], 16 * p + s - 1)
                        dve.tensor_reduce(SM[s % 2], MK[s % 2].rearrange("p l t -> p t l"), AX_X, ALU.add).then_inc(hg["summed"], 1)

                    for d in range(2):
                        if d == 0:
                            forget(0)
                            decays(0)
                            factors(0)
                            levels(0, 0, NL - 1)
                        states(d)
                        for c, (lo, hi) in enumerate(((0, 2), (2, 4), (4, 5), (5, 6))):
                            mask(2 * d, c)
                            levels(2 * d + 1, lo, hi)
                        for c in range(NCH):
                            if d == 0 and c < 2:
                                (forget, decays)[c](1)
                            mask(2 * d + 1, c)
                            if d == 0 and c > 0:
                                levels(2, 2 * c - 2, 2 * c)
                        if d == 0:
                            factors(1)
                    dve.wait_ge(hg["out1"], p + 1)
                    dve.tensor_tensor(OS, PS[7][:], OS, ALU.add).then_inc(hg["osum"], 1)
                    dve.wait_ge(hg["root"], p + 1)
                    DV.link(dve.reciprocal(SQ, SQ))
                    DV.link(dve.tensor_tensor(OS, OS, SQ, ALU.mult))
                    for s in range(2):
                        tokens = lambda v: v[:, HALF * s:HALF * s + HALF].rearrange("p (i n) -> p i n", n=CH)
                        dve.scalar_tensor_tensor(by_tile(mixT[:, PAIRS + p, :])[:, s], tokens(OS), normg, tokens(SG), ALU.mult, ALU.mult)
        TRASH = 1024
        ROW = D + E
        hd = nc.dram_tensor("token_rows", (T, ROW), F32, kind="Internal").ap()
        yd = nc.dram_tensor("token_sums", (TRASH + P, D), F32, kind="Internal").ap()
        F16 = mybir.dt.float16
        GU = KD * HID
        ebase = [(W, EXPERT * b, W, EXPERT * b + 2 * GU) for b in range(3)] + [(HT, 0, A, 0)]

        def expert_view(b):
            t, g, u, d = ebase[b]
            return cut(t, g, KD, HID), cut(t, g + GU, KD, HID), cut(u, d, 2, D)

        Y = cut(A, 4096, NT, D)
        XG = [cut(A, 4096 + ROW * i, ROW) for i in range(4)]
        XT = [cut(A, 10368 + 1024 * i, 1024) for i in range(2)]
        YS = [cut(A, 12416 + 1024 * i, D) for i in range(2)]
        SU = [cut(A, 14464 + HID * i, HID) for i in range(2)]
        HM = [cut(A, 14976 + HID * i, HID) for i in range(2)]
        HX = [cut(A, 15488 + HID * i, HID) for i in range(2)]
        RW, RB = cut(A, 10368, KD, E), cut(A, 10880, E)
        BI, SEL = cut(A, 10944, E), cut(A, 11008, E)
        H6 = cut(A, 11072, TOPK, E)
        HS, HB = cut(A, 12416, 2, 512), cut(A, 13440, 2, 512)
        TOP, IDX, IDF = cut(A, 16000, 8), cut(A, 16008, 8), cut(A, 16016, 8)
        AHEAD = 3
        EP = E + 2
        PM = cut(levmask, 0, NT, EP)
        CNT, CUMB, NB = cut(levmask, 264, E), cut(levmask, 328, E), cut(levmask, 392, E)
        SC1, SC2 = cut(levmask, 456, E), cut(levmask, 520, P)
        LISTE, LISTB = cut(levmask, 648, 32), cut(levmask, 680, 32)
        LISTI = cut(levmask, 712, 33).bitcast(mybir.dt.int32)
        SH = [cut(restart, 256 * i, 256).bitcast(F16) for i in range(2)]
        tri16, ones16, tok16 = (half[:, 0:64].bitcast(F16), half[:, 64:128].bitcast(F16), half[:, 128:132].bitcast(F16))
        M16 = half[:, 132:132 + NT * 32].bitcast(F16).rearrange("p (i e) -> p i e", e=E)
        IX = [half[:, 260 + i:261 + i].bitcast(U32) for i in range(8)]
        IXT = half[:, 268:269]
        negp, trp = small[:, 241:242], small[:, 242:243]
        pcol = small[:, 243:244]
        G = cut(gates, 0, NT, E)
        from_rows = lambda v, e: v[bass.ds(e, 1)].rearrange("e (p k) n -> p (e k) n", k=KD)
        from_tiles = lambda v, e: v[bass.ds(e, 1)].rearrange("e (k p) n -> p (e k) n", p=P)

        moe_sems = {}

        def clear_moe():
            with nc.Block() as block:
                @block.gpsimd
                def _(pool):
                    for s in moe_sems.values():
                        pool.sem_clear(s)

        def moe(l, nt, n_tok, sl):
            def s_(n):
                if n not in moe_sems:
                    moe_sems[n] = sem("moe_" + n)
                return moe_sems[n]

            weights = lambda e: (from_rows(a["exp_w_gate"][l], e), from_rows(a["exp_w_up"][l], e), from_tiles(a["exp_w_down"][l], e))
            w_in = [s_(f"w_in{b}") for b in range(4)]
            listed = n_tok * TOPK // sl

            def load(sp, b, e):
                for v, w in zip(expert_view(b), weights(e)):
                    sp.dma_start(v, w).then_inc(w_in[b], 16)

            r_in, rprod, sig, picked, ranks, gates_out, hd_out = (s_(n) for n in ("r_in", "rprod", "sig", "picked", "ranks", "gates_out", "hd_out"))
            up, silu, mul, down, moved, yd_out, zero = (s_(n) for n in ("sh_up", "sh_silu", "sh_mul", "sh_down", "sh_moved", "yd_out", "zero"))
            passed, placed, spread, diag = s_("passed"), s_("placed"), s_("spread"), s_("diag")
            with nc.Block() as block:
                @block.sync
                def _(sp):
                    sp.dma_start(RW, rows(a["router_w"][l])).then_inc(r_in, 16)
                    sp.dma_start(RB, a["router_bias"][l:l + 1, :].broadcast_to([P, E])).then_inc(r_in, 16)
                    for v, w in zip(expert_view(2), (rows(a["sh_w_gate"][l]), rows(a["sh_w_up"][l]), nat(a["sh_w_down"][l]))):
                        sp.dma_start(v, w).then_inc(w_in[2], 16)
                    for i in range(nt):
                        sp.dma_start(hd[P * i:P * i + P, 0:D], H[:, i, :]).then_inc(hd_out, 16)
                    load(sp, 0, 0)
                    load(sp, 1, 1)
                    sp.wait_ge(zero, 1)
                    sp.dma_start(yd[TRASH:TRASH + P, :], YS[1]).then_inc(yd_out, 16)
                    sp.wait_ge(gates_out, nt)
                    for i in range(nt):
                        sp.dma_start(hd[P * i:P * i + P, D:ROW], G[:, i, :]).then_inc(hd_out, 16)
                    for i in range(nt):
                        sp.wait_ge(moved, 2 * i + 2)
                        sp.dma_start(yd[P * i:P * i + P, :], Y[:, i, :]).then_inc(yd_out, 16)
                    sp.wait_ge(hd_out, 32 * nt)
                    sp.wait_ge(yd_out, 16 * (nt + 1))

                @block.gpsimd
                def _(pool):
                    pool.wait_ge(mul, 2)
                    pool.wait_ge(down, 2 * nt)
                    pool.memset(YS[1], 0.0).then_inc(zero, 1)

                @block.tensor
                def _(pe):
                    pe.wait_ge(r_in, 32)
                    for i in range(nt):
                        for k in range(KD):
                            mm = pe.matmul(PS[i][:, 0:E], plain_cols(HT[:], k, i), RW[:, k, :], start=(k == 0), stop=(k == KD - 1))
                        mm.then_inc(rprod, 1)
                    pe.wait_ge(w_in[2], 48)
                    wg, wu, wd = expert_view(2)
                    for m in range(2):
                        for n, w in enumerate((wg, wu)):
                            for k in range(KD):
                                mm = pe.matmul(PS[4 + 2 * m + n][:, 0:n_tok], w[:, k, P * m:P * m + P], HTt[:, k, 0:n_tok], start=(k == 0), stop=(k == KD - 1))
                        mm.then_inc(up, 1)
                    for i in range(nt):
                        pe.wait_ge(picked, i + 1)
                        for q in range(i + 1):
                            mm = pe.matmul(PS[i][:, E:2 * E], tri16 if q == i else ones16, M16[:, q, :], start=(q == 0), stop=(q == i))
                        mm.then_inc(ranks, 1)
                    for q in range(nt):
                        mm = pe.matmul(PS[nt - 1][:, 2 * E:3 * E], ones16, M16[:, q, :], start=(q == 0), stop=(q == nt - 1))
                    mm.then_inc(ranks, 1)
                    pe.wait_ge(mul, 2)
                    for i in range(nt):
                        for n in range(2):
                            j = 2 * i + n
                            if j >= 4:
                                pe.wait_ge(moved, j - 3)
                            for m in range(2):
                                mm = pe.matmul(PS[4 + j % 4][:], HB[:, m, P * i:P * i + P], wd[:, m, 512 * n:512 * n + 512], start=(m == 0), stop=(m == 1))
                            mm.then_inc(down, 1)
                    pe.wait_ge(diag, 1)
                    pe.matmul(PS[0][:, 384:512], onesf[:], SC2, start=True, stop=True).then_inc(spread, 1)
                    pe.wait_ge(diag, 2)
                    pe.matmul(PS[0][:, 256:384], onesf[:], SC2, start=True, stop=True).then_inc(spread, 1)

                @block.scalar
                def _(act):
                    for i in range(nt):
                        act.wait_ge(rprod, i + 1)
                        act.activation(G[:, i, :], PS[i][:, 0:E], ACT.Sigmoid).then_inc(sig, 1)
                    for m in range(2):
                        act.wait_ge(up, m + 1)
                        act.activation(HS[:, m, 0:n_tok], PS[4 + 2 * m][:, 0:n_tok], ACT.Silu).then_inc(silu, 1)
                    for i in range(nt):
                        act.wait_ge(down, 2 * i + 2)
                        for n in range(2):
                            act.activation(Y[:, i, 512 * n:512 * n + 512], PS[4 + (2 * i + n) % 4][:], ACT.Copy).then_inc(moved, 1)

                @block.vector
                def _(dve):
                    dve.wait_ge(r_in, 32)
                    DV.then(dve.memset(PM, -1.0))
                    for i in range(nt):
                        g = G[:, i, :]
                        dve.wait_ge(sig, i + 1)
                        DV.link(dve.tensor_tensor(BI, g, RB, ALU.add))
                        DV.link(dve.max(TOP, BI))
                        DV.link(dve.max_index(IDX.bitcast(U32), TOP, BI))
                        DV.link(dve.tensor_copy(IDF, IDX.bitcast(U32)))
                        DV.link(dve.tensor_tensor(H6, iota.unsqueeze(1).broadcast_to([P, TOPK, E]),
                                                  IDF[:, 0:TOPK].unsqueeze(2).broadcast_to([P, TOPK, E]), ALU.is_equal))
                        DV.link(dve.tensor_reduce(SEL, H6.rearrange("p k e -> p e k"), AX_X, ALU.add))
                        dve.tensor_copy(M16[:, i, :], SEL).then_inc(picked, 1)
                        DV.link(dve.tensor_tensor(g, g, SEL, ALU.mult))
                        DV.link(dve.tensor_reduce(stats[:, 0:1], g, AX_X, ALU.add))
                        DV.link(dve.reciprocal(stats[:, 1:2], stats[:, 0:1]))
                        dve.tensor_scalar(g, g, stats[:, 1:2], ROUTED_SCALE, ALU.mult, ALU.mult).then_inc(gates_out, 1)
                    for i in range(nt):
                        dve.wait_ge(ranks, i + 1 if i < nt - 1 else nt + 1)
                        DV.link(dve.tensor_copy(SEL, M16[:, i, :]))
                        DV.link(dve.scalar_tensor_tensor(SEL, PS[i][:, E:2 * E], 1.0, SEL, ALU.add, ALU.mult))
                        DV.link(dve.tensor_scalar(PM[:, i, 0:E], SEL, -1.0, None, ALU.add))
                    for m in range(2):
                        dve.wait_ge(silu, m + 1)
                        dve.tensor_tensor(HB[:, m, 0:n_tok], HS[:, m, 0:n_tok], PS[5 + 2 * m][:, 0:n_tok], ALU.mult).then_inc(mul, 1)
                    dve.wait_ge(ranks, nt + 1)
                    DV.link(dve.tensor_copy(CNT, PS[nt - 1][:, 2 * E:3 * E]))
                    DV.link(dve.tensor_scalar(NB, CNT, float(sl), None, ALU.is_gt))
                    for j in range(2, -(-n_tok // sl)):
                        DV.link(dve.scalar_tensor_tensor(NB, CNT, float(sl * j), NB, ALU.is_gt, ALU.add))
                    DV.link(dve.memset(SC1, 1.0))
                    DV.link(dve.tensor_tensor_scan(CUMB, SC1, NB, 0.0, ALU.mult, ALU.add))
                    DV.link(dve.tensor_scalar(SC1, CUMB, pcol, None, ALU.is_le))
                    DV.link(dve.tensor_reduce(stats[:, 0:1], SC1, AX_X, ALU.add))
                    DV.link(dve.tensor_scalar(SC2, ident[:], stats[:, 0:1], None, ALU.mult))
                    dve.nop().then_inc(diag, 1)
                    DV.link(dve.tensor_tensor(NB, CUMB, NB, ALU.subtract))
                    DV.link(dve.tensor_scalar(SC1, iota, stats[:, 0:1], None, ALU.is_equal))
                    DV.link(dve.tensor_tensor(SC1, SC1, NB, ALU.mult))
                    DV.link(dve.tensor_reduce(stats[:, 1:2], SC1, AX_X, ALU.add))
                    DV.link(dve.tensor_tensor(stats[:, 1:2], pcol, stats[:, 1:2], ALU.subtract))
                    DV.link(dve.tensor_scalar(stats[:, 1:2], stats[:, 1:2], 1.0, float(sl), ALU.add, ALU.mult))
                    dve.wait_ge(spread, 1)
                    DV.then(dve.tensor_copy(LISTE, PS[0][:, 384:416]))
                    DV.link(dve.tensor_copy(LISTI[:, 0:32], PS[0][:, 384:416]))
                    DV.link(dve.tensor_copy(LISTI[:, 32:33], CUMB[:, E - 1:E]))
                    DV.link(dve.tensor_scalar(SC2, ident[:], stats[:, 1:2], None, ALU.mult))
                    dve.nop().then_inc(diag, 1)
                    dve.wait_ge(spread, 2)
                    dve.tensor_copy(LISTB, PS[0][:, 256:288])

            def select(dve, q, e, slots):
                return dve.tensor_tensor(SH[q][:, 0:nt * sl].rearrange("p (i s) -> p i s", s=sl),
                                         slots.unsqueeze(1).broadcast_to([P, nt, sl]),
                                         PM[:, 0:nt, bass.ds(e, 1)].broadcast_to([P, nt, sl]), ALU.is_equal)

            def index_products(pe, q):
                sh = SH[q][:, 0:nt * sl].rearrange("p (i s) -> p i s", s=sl)
                for i in range(nt):
                    mm = pe.matmul(PS[5][0:sl, 0:2], sh[:, i, :], tok16[:, 2 * i:2 * i + 2], start=(i == 0), stop=(i == nt - 1))
                return mm

            def index(dve, q, half_done, n):
                dve.tensor_scalar(IXT[0:sl], PS[5][0:sl, 1:2], negp[0:sl], trp[0:sl], ALU.mult, ALU.add).then_inc(half_done, 1)
                dve.wait_ge(half_done, n)
                return dve.tensor_tensor(IX[q][0:sl], PS[5][0:sl, 0:1], IXT[0:sl], ALU.add)

            def carry(eng):
                eng.sem_inc(passed, 1)

            def gather(pool, q, o):
                return pool.indirect_dma_start(XG[o][0:sl, :], None, hd, bass.IndirectOffsetOnAxis(ap=IX[q][0:sl], axis=0),
                                               bounds_check=n_tok - 1, oob_is_err=False)

            def scatter(pool, q, o):
                return pool.indirect_dma_start(yd, bass.IndirectOffsetOnAxis(ap=IX[q][0:sl], axis=0), YS[o][0:sl, :], None,
                                               bounds_check=TRASH + P - 1, oob_is_err=True, compute_op=ALU.add)

            def turn_rows(pe, g, o):
                x = XG[g][0:sl, 0:D].rearrange("t (p k) -> t k p", k=KD)
                for k in range(KD):
                    mm = pe.transpose(PS[2 + k // 4][:, sl * (k % 4):sl * (k % 4) + sl], x[:, k, :], ident[0:sl, 0:sl])
                return mm

            xt = lambda o, g: XT[o][:, 4 * sl * g:4 * sl * g + 4 * sl]

            def gate_up(pe, b, o, g):
                t, at = ebase[b][0:2]
                w = cut(t, at, 2, KD, HID)
                for k in range(KD):
                    x = XT[o][:, sl * k:sl * k + sl]
                    if sl == 64:
                        for n in range(2):
                            mm = pe.matmul(PS[g][64 * n:64 * n + 64, 0:HID], x, w[:, n, k, :], start=(k == 0), stop=(k == KD - 1))
                    else:
                        mm = pe.matmul(PS[g][0:sl, :], x, w[:, :, k, :], start=(k == 0), stop=(k == KD - 1))
                return mm

            up_of = lambda g: PS[g][64:128, 0:HID] if sl == 64 else PS[g][0:sl, HID:2 * HID]

            def turn_hidden(pe, o):
                for m in range(2):
                    mm = pe.transpose(PS[4][:, sl * m:sl * m + sl], HM[o][0:sl, P * m:P * m + P], ident[0:sl, 0:sl])
                return mm

            def down_product(pe, b, o):
                wd = expert_view(b)[2]
                for m in range(2):
                    for n in range(2):
                        y = PS[6][64 * n:64 * n + 64, :] if sl == 64 else PS[6 + n][0:sl, :]
                        mm = pe.matmul(y, HX[o][:, sl * m:sl * m + sl], wd[:, m, 512 * n:512 * n + 512], start=(m == 0), stop=(m == 1))
                return mm

            y_of = lambda n: PS[6][64 * n:64 * n + 64, :] if sl == 64 else PS[6 + n][0:sl, :]
            weigh = lambda dve, o, g, e: dve.scalar_tensor_tensor(HM[o][0:sl], SU[o][0:sl], XG[g][0:sl, bass.ds(e + D, 1)], up_of(o), ALU.mult, ALU.mult)

            selected, indexed, index_half, index_made, turned, xt_half, xt_made, gu, silud, hid, hturn, hx, yprod, y_half, y_made = (
                s_(n) for n in ("selected", "indexed", "index_half", "index_made", "turned", "xt_half", "xt_made", "gu", "silud", "hid", "hturn", "hx", "yprod",
                                "y_half", "y_made"))
            x_in = [sem(f"x_in{o}_{l}") for o in range(4)]
            y_out = [sem(f"y_out{o}_{l}") for o in range(2)]

            def run(eng, first, step):
                for e in range(first):
                    step(e, e % 8, e)
                left = (E - first) % 8
                with eng.Fori(0, (E - first) // 8) as r:
                    for i in range(8):
                        step(8 * r + (first + i), (first + i) % 8, None)
                for e in range(E - left, E):
                    step(e, e % 8, e)

            with nc.Block() as block:
                @block.sync
                def _(sp):
                    sp.wait_ge(x_in[AHEAD - 1], 16)
                    load(sp, 2, 2)
                    load(sp, 3, 3)
                    with sp.Fori(0, E // 4 - 1) as r:
                        for q in range(4):
                            sp.wait_ge(yprod, 4 * r + q + 1)
                            load(sp, q, 4 * r + (4 + q))

                @block.tensor
                def _(pe):
                    def step(e, q, at):
                        pe.wait_ge(w_in[q % 4], 12 * (e - q % 4) + 48 + (48 if q % 4 == 2 else 0))
                        pe.wait_ge(xt_made, e + 1)
                        pe.wait_ge(xt_half, e + 1)
                        if at is None or at >= 2:
                            pe.wait_ge(hid, e - 1)
                        gate_up(pe, q % 4, q % 2, q % 2).then_inc(gu, 1)
                        if at is None or at < E - 1:
                            o = (q + 1) % 4
                            pe.wait_ge(x_in[o], 4 * (e + 1 - o) + 16)
                        if at != 0:
                            pe.wait_ge(hx, e)
                            if at != 1:
                                pe.wait_ge(y_made, e - 1)
                                pe.wait_ge(y_half, e - 1)
                            down_product(pe, (q - 1) % 4, (q - 1) % 2).then_inc(yprod, 1)
                        if at is None or at < E - 1:
                            turn_rows(pe, (q + 1) % 4, (q + 1) % 2).then_inc(turned, 1)
                        pe.wait_ge(selected, e + AHEAD + 1)
                        pe.wait_ge(index_made, e + AHEAD)
                        pe.wait_ge(hid, e + 1)
                        index_products(pe, (q + AHEAD) % 2).then_inc(indexed, 1)
                        turn_hidden(pe, q % 2).then_inc(hturn, 1)

                    for e in range(AHEAD):
                        pe.wait_ge(selected, e + 1)
                        if e:
                            pe.wait_ge(index_made, e)
                        index_products(pe, e % 2).then_inc(indexed, 1)
                    pe.wait_ge(x_in[0], 16)
                    turn_rows(pe, 0, 0).then_inc(turned, 1)
                    run(pe, 2, step)
                    pe.wait_ge(hx, E)
                    pe.wait_ge(y_made, E - 1)
                    pe.wait_ge(y_half, E - 1)
                    down_product(pe, (E - 1) % 4, (E - 1) % 2).then_inc(yprod, 1)

                @block.scalar
                def _(act):
                    def xt_copy(o, n):
                        act.wait_ge(turned, n)
                        act.activation(xt(o, 0), PS[2][:, 0:4 * sl], ACT.Copy).then_inc(xt_half, 1)

                    def y_copy(o, n, first=False):
                        act.wait_ge(yprod, n)
                        if not first:
                            act.wait_ge(y_out[o], 8 * (n - 1 - o))
                        act.activation(YS[o][0:sl, 0:512], y_of(0), ACT.Copy).then_inc(y_half, 1)

                    def step(e, q, at):
                        act.wait_ge(gu, e + 1)
                        act.activation(SU[q % 2][0:sl], PS[q % 2][0:sl, 0:HID], ACT.Silu).then_inc(silud, 1)
                        if at != 0:
                            y_copy((q - 1) % 2, e, at in (1, 2))
                        if at is None or at < E - 1:
                            if at is None or at >= 1:
                                act.wait_ge(gu, e)
                            xt_copy((q + 1) % 2, e + 2)

                    xt_copy(0, 1)
                    run(act, 3, step)
                    y_copy((E - 1) % 2, E)

                @block.vector
                def _(dve):
                    def y_copy(o, n, first=False):
                        dve.wait_ge(yprod, n)
                        if not first:
                            dve.wait_ge(y_out[o], 8 * (n - 1 - o))
                        dve.tensor_copy(YS[o][0:sl, 512:D], y_of(1)).then_inc(y_made, 1)

                    def xt_copy(o, n):
                        dve.wait_ge(turned, n)
                        dve.tensor_copy(xt(o, 1), PS[3][:, 0:4 * sl]).then_inc(xt_made, 1)

                    def indices(e, q):
                        dve.wait_ge(indexed, e + 1)
                        index(dve, q, index_half, e + 1).then_inc(index_made, 1)

                    def step(e, q, at):
                        if at is None or at < E - 1:
                            n = e + AHEAD + 1 if at is None or at < E - AHEAD - 1 else E
                            select(dve, (q + AHEAD + 1) % 2, n, iota_s[:, 0:sl]).then_inc(selected, 1)
                        dve.wait_ge(silud, e + 1)
                        weigh(dve, q % 2, q % 4, e).then_inc(hid, 1)
                        if at != 0:
                            y_copy((q - 1) % 2, e, at in (1, 2))
                        if at is None or at < E - 1:
                            xt_copy((q + 1) % 2, e + 2)
                        indices(e + AHEAD, (q + AHEAD) % 8)
                        dve.wait_ge(hturn, e + 1)
                        dve.tensor_copy(HX[q % 2][:, 0:2 * sl], PS[4][:, 0:2 * sl]).then_inc(hx, 1)

                    for e in range(2):
                        select(dve, e, e, iota_s[:, 0:sl]).then_inc(selected, 1)
                    for e in range(AHEAD):
                        indices(e, e)
                        if e + 2 <= AHEAD:
                            select(dve, e % 2, e + 2, iota_s[:, 0:sl]).then_inc(selected, 1)
                    xt_copy(0, 1)
                    run(dve, 3, step)
                    y_copy((E - 1) % 2, E)

                @block.gpsimd
                def _(pool):
                    def get(n, o, q, used=None):
                        pool.wait_ge(index_made, n)
                        if used is not None:
                            pool.wait_ge(turned, used)
                            pool.wait_ge(hid, used)
                        carry(pool)
                        gather(pool, q, o).then_inc(x_in[o], 16)

                    def put(e, q, at):
                        pool.wait_ge(y_half, e + 1)
                        pool.wait_ge(y_made, e + 1)
                        if at != 0:
                            o = (q - 1) % 2
                            pool.wait_ge(y_out[o], 8 * (e - 1 - o) + 16)
                        carry(pool)
                        scatter(pool, q, q % 2).then_inc(y_out[q % 2], 16)

                    def step(e, q, at):
                        if at is None or at < E - AHEAD:
                            get(e + (AHEAD + 1), (q + AHEAD) % 4, (q + AHEAD) % 8, None if at == 0 else e)
                        if at != 0:
                            put(e - 1, (q - 1) % 8, None if at is None else at - 1)

                    for x in XG:
                        cleared = pool.memset(x, 0.0)
                    cleared.then_inc(zero, 1)
                    pool.wait_ge(zero, 2)
                    for e in range(AHEAD):
                        get(e + 1, e, e)
                    run(pool, 2, step)
                    put(E - 1, (E - 1) % 8, E - 1)
                    pool.wait_ge(y_out[(E - 1) % 2], 8 * E)
                    pool.wait_ge(y_out[E % 2], 8 * E)

            ALL = E + AHEAD

            def more(eng, body):
                n = eng.value_load(LISTI[0:1, 32:33], min_val=0, max_val=listed)
                with eng.Fori(0, listed // 4) as g:
                    with eng.If(n > 4 * g):
                        with eng.Fori(0, 2) as f:
                            for h in range(2):
                                with eng.If(n > 4 * g + 2 * f + h):
                                    i = 4 * g + 2 * f + h
                                    body(i, eng.value_load(LISTI[0:1, bass.ds(i, 1)], min_val=0, max_val=E - 1), h, 2 * g + f)
                                with eng.Else():
                                    eng.nop()
                    with eng.Else():
                        eng.nop()

            with nc.Block() as block:
                @block.sync
                def _(sp):
                    def body(i, e, h, r):
                        sp.wait_ge(yprod, i + (E - 1))
                        load(sp, h, e)
                    more(sp, body)

                @block.tensor
                def _(pe):
                    def body(i, e, h, r):
                        pe.wait_ge(selected, i + (ALL + 1))
                        index_products(pe, 0).then_inc(indexed, 1)
                        pe.wait_ge(x_in[0], 16 * i + (4 * E + 16))
                        carry(pe)
                        turn_rows(pe, 0, 0).then_inc(turned, 1)
                        pe.wait_ge(xt_half, i + (E + 1))
                        pe.wait_ge(xt_made, i + (E + 1))
                        pe.wait_ge(w_in[h], 48 * r + (12 * E + 48))
                        gate_up(pe, h, 0, 0).then_inc(gu, 1)
                        pe.wait_ge(hid, i + (E + 1))
                        carry(pe)
                        turn_hidden(pe, 0).then_inc(hturn, 1)
                        pe.wait_ge(hx, i + (E + 1))
                        down_product(pe, h, 0).then_inc(yprod, 1)
                    more(pe, body)

                @block.scalar
                def _(act):
                    def body(i, e, h, r):
                        act.wait_ge(turned, i + (E + 1))
                        act.activation(xt(0, 0), PS[2][:, 0:4 * sl], ACT.Copy).then_inc(xt_half, 1)
                        act.wait_ge(gu, i + (E + 1))
                        act.activation(SU[0][0:sl], PS[0][0:sl, 0:HID], ACT.Silu).then_inc(silud, 1)
                        act.wait_ge(yprod, i + (E + 1))
                        act.activation(YS[0][0:sl, 0:512], y_of(0), ACT.Copy).then_inc(y_half, 1)
                    more(act, body)

                @block.vector
                def _(dve):
                    slots = XT[1][:, 0:sl]
                    def body(i, e, h, r):
                        dve.tensor_scalar(slots, iota_s[:, 0:sl], LISTB[:, bass.ds(i, 1)], None, ALU.add).then_inc(placed, 1)
                        dve.wait_ge(placed, i + 1)
                        select(dve, 0, e, slots).then_inc(selected, 1)
                        dve.wait_ge(indexed, i + (ALL + 1))
                        dve.wait_ge(y_out[0], 16 * i + 8 * E)
                        index(dve, 0, index_half, i + (ALL + 1)).then_inc(index_made, 1)
                        dve.wait_ge(turned, i + (E + 1))
                        dve.tensor_copy(xt(0, 1), PS[3][:, 0:4 * sl]).then_inc(xt_made, 1)
                        dve.wait_ge(silud, i + (E + 1))
                        weigh(dve, 0, 0, e).then_inc(hid, 1)
                        dve.wait_ge(hturn, i + (E + 1))
                        dve.tensor_copy(HX[0][:, 0:2 * sl], PS[4][:, 0:2 * sl]).then_inc(hx, 1)
                        dve.wait_ge(yprod, i + (E + 1))
                        dve.tensor_copy(YS[0][0:sl, 512:D], y_of(1)).then_inc(y_made, 1)
                    more(dve, body)

                @block.gpsimd
                def _(pool):
                    def body(i, e, h, r):
                        pool.wait_ge(index_made, i + (ALL + 1))
                        carry(pool)
                        gather(pool, 0, 0).then_inc(x_in[0], 16)
                        pool.wait_ge(y_half, i + (E + 1))
                        pool.wait_ge(y_made, i + (E + 1))
                        carry(pool)
                        scatter(pool, 0, 0).then_inc(y_out[0], 16)
                        pool.wait_ge(y_out[0], 16 * i + (8 * E + 16))
                        carry(pool)
                    more(pool, body)

            y_in = s_("y_in")
            with nc.Block() as block:
                @block.sync
                def _(sp):
                    for i in range(nt):
                        sp.dma_start(Y[:, i, :], yd[P * i:P * i + P, :]).then_inc(y_in, 16)
                    sp.wait_ge(y_in, 16 * nt)

        KJ = D // P
        GY = cut(A, 0, KJ, HALF)
        BD = cut(A, 8192, 4 * KJ, P)
        M1 = cut(A, 12288, KJ, HALF)
        obuf = lambda n: cut(A, 2048 + 512 * n, T)
        RR, II, AA, TT = ([obuf(2 * q + n) for n in range(2)] for q in range(4))
        UC, HH = ([obuf(8 + 2 * q + n) for n in range(2)] for q in range(2))
        coef, ncoef = small[:, 225:241], small[:, 48:64]
        lw = [cut(gates, 16 * n, 16) for n in range(4)]
        od = {n: sem("od_" + n) for n in ("zero", "bd_in", "y", "gelu", "u", "conv", "ga", "gates", "decay", "iu", "ratio",
                                          "root", "scan", "lam")}

        def recurrent_unit():
            bias_load, products, sums = modulation_steps(1, range(4, 9))
            AT = {0: 0, 1: 1, 3: 2, 4: 3, 7: 4}
            with nc.Block() as block:
                @block.vector
                def _(dve):
                    for k in range(KD):
                        dve.tensor_copy(CR1[k], cT[:, 8 + k:9 + k].broadcast_to([P, P]))

            with nc.Block() as block:
                @block.sync
                def _(sp):
                    for kind, w in enumerate(("lru_w_a", "lru_w_x")):
                        for d in range(2):
                            for h in range(2):
                                r = slice(64 * h, 64 * h + 64)
                                at = 16 * kind + 8 * d
                                sp.dma_start(BD[r, at:at + KJ, r], a[w][0, d].rearrange("(j h) r c -> h r j c", h=2)[h]).then_inc(od["bd_in"], 16)
                    bias_load(sp)
                    send(sp, odi[3] + 1 + SLOTS)

                @block.tensor
                def _(pe):
                    for c in range(2):
                        arrived(pe, odi[c])
                        for q in range(4):
                            j = 4 * c + q
                            if j >= 2:
                                pe.wait_ge(od["gelu"], j - 1)
                            for k in range(KD):
                                mm = pe.matmul(PS[6 + j % 2][:, 0:HALF], view(odi[c])[:, k, P * q:P * q + P], HTt[:, k, HALF:T],
                                               start=(k == 0), stop=(k == KD - 1))
                            mm.then_inc(chunk_used if q == 3 else od["y"], 1)

                    def u_product(j):
                        c, q = 2 + j // 4, j % 4
                        if q == 0:
                            arrived(pe, odi[c])
                        if j >= 2:
                            pe.wait_ge(od["conv"], j - 1)
                        for k in range(KD):
                            mm = pe.matmul(PS[j % 2][:], view(odi[c])[:, k, P * q:P * q + P], HTt[:, k, :], start=(k == 0), stop=(k == KD - 1))
                        mm.then_inc(chunk_used if q == 3 else od["u"], 1)

                    u_product(0)
                    pe.wait_ge(od["bd_in"], 16 * 8)
                    for j in range(KJ):
                        if j + 1 < KJ:
                            u_product(j + 1)
                        pe.wait_ge(od["conv"], j + 1)
                        for d in range(2):
                            s = 2 * j + d
                            if s >= 2:
                                pe.wait_ge(od["gates"], s - 1)
                            for kind in range(2):
                                mm = pe.matmul(PS[2 + 2 * (s % 2) + kind][:], BD[:, 16 * kind + 8 * d + j, :], UC[j % 2], start=True, stop=True)
                            mm.then_inc(od["ga"], 1)
                        if j in AT:
                            if j < 2:
                                pe.wait_ge(od["gelu"], KJ - 1 + j)
                            products(pe, slice(AT[j], AT[j] + 1))

                @block.scalar
                def _(act):
                    act.activation(lw[0], lam, ACT.Abs).then_inc(od["lam"], 1)
                    act.wait_ge(od["lam"], 1)
                    act.activation(lw[0], lw[0], ACT.Exp, scale=-1.0).then_inc(od["lam"], 1)
                    for j in range(KJ):
                        if j % 4 == 3:
                            act.wait_ge(chunk_used, odi[j // 4] + 1)
                        else:
                            act.wait_ge(od["y"], 3 * (j // 4) + j % 4 + 1)
                        act.activation(GY[:, j, :], PS[6 + j % 2][:, 0:HALF], ACT.Gelu_apprx_tanh).then_inc(od["gelu"], 1)
                    act.wait_ge(od["lam"], 3)

                    def root(s):
                        act.wait_ge(od["ratio"], s + 1)
                        act.activation(RR[s % 2], TT[s % 2], ACT.Sqrt, scale=2.0).then_inc(od["root"], 1)

                    for s in range(2 * KJ):
                        j, d = s // 2, s % 2
                        act.wait_ge(od["ga"], s + 1)
                        if s >= 2:
                            act.wait_ge(od["scan"], s - 1)
                        n = 8 * d + j
                        AC.then(act.activation(RR[s % 2], PS[2 + 2 * (s % 2)][:], ACT.Sigmoid, bias=gbias[:, n:n + 1]))
                        act.activation(II[s % 2], PS[3 + 2 * (s % 2)][:], ACT.Sigmoid, bias=gbias[:, 16 + n:17 + n]).then_inc(od["gates"], 1)
                        AC.settle()
                        act.activation(AA[s % 2], RR[s % 2], ACT.Exp, scale=coef[:, n:n + 1])
                        act.activation(TT[s % 2], RR[s % 2], ACT.Tanh, scale=ncoef[:, n:n + 1]).then_inc(od["decay"], 1)
                        root(s)

                @block.gpsimd
                def _(pool):
                    for s in range(2 * KJ):
                        pool.wait_ge(od["gates"], s + 1)
                        pool.tensor_tensor(II[s % 2], II[s % 2], UC[(s // 2) % 2], ALU.mult).then_inc(od["iu"], 1)

                @block.vector
                def _(dve):
                    e, z, z2, q = lw
                    dve.wait_ge(od["lam"], 2)
                    DV.link(dve.tensor_scalar(z, e, 2.0, None, ALU.add))
                    DV.link(dve.reciprocal(z, z))
                    DV.link(dve.tensor_tensor(z, z, e, ALU.mult))
                    DV.link(dve.tensor_tensor(z2, z, z, ALU.mult))
                    DV.link(dve.tensor_scalar(q, z2, 1 / 15, None, ALU.mult))
                    for n in (13, 11, 9, 7, 5, 3):
                        DV.link(dve.scalar_tensor_tensor(q, q, 1 / n, z2, ALU.add, ALU.mult))
                    DV.link(dve.scalar_tensor_tensor(q, q, 1.0, z, ALU.add, ALU.mult))
                    DV.link(dve.tensor_scalar(z, lam, -1.0, 0.0, ALU.mult, ALU.max))
                    DV.link(dve.scalar_tensor_tensor(q, q, 2.0, z, ALU.mult, ALU.add))
                    DV.link(dve.tensor_scalar(coef, q, -LRU_C, None, ALU.mult))
                    dve.tensor_scalar(ncoef, q, LRU_C, None, ALU.mult).then_inc(od["lam"], 1)

                    def conv(j):
                        if j % 4 == 3:
                            dve.wait_ge(chunk_used, odi[2 + j // 4] + 1)
                        else:
                            dve.wait_ge(od["u"], 3 * (j // 4) + j % 4 + 1)
                        if j >= 2:
                            dve.wait_ge(od["iu"], 2 * (j - 1))
                        u = PS[j % 2][:].rearrange("p (s n) -> p s n", s=2)
                        o = UC[j % 2].rearrange("p (s n) -> p s n", s=2)
                        DV.link(dve.tensor_scalar(UC[j % 2], PS[j % 2][:], convw[:, 16 + j:17 + j], convb[:, j:j + 1], ALU.mult, ALU.add))
                        for tap, shift in ((0, -2), (1, -1), (3, 1)):
                            lo, hi = max(0, -shift), HALF - max(0, shift)
                            ins = dve.scalar_tensor_tensor(o[:, :, lo:hi], u[:, :, lo + shift:hi + shift], convw[:, 8 * tap + j:8 * tap + j + 1],
                                                           o[:, :, lo:hi], ALU.mult, ALU.add)
                            if tap == 3:
                                ins.then_inc(od["conv"], 1)
                            else:
                                DV.link(ins)

                    conv(0)
                    for s in range(2 * KJ):
                        j, d = s // 2, s % 2
                        x = s % 2
                        if d == 0 and j + 1 < KJ:
                            conv(j + 1)
                        dve.wait_ge(od["decay"], s + 1)
                        DV.link(dve.tensor_scalar(HH[d], TT[x], 1.0, None, ALU.add))
                        DV.link(dve.reciprocal(HH[d], HH[d]))
                        dve.tensor_tensor(TT[x], TT[x], HH[d], ALU.mult).then_inc(od["ratio"], 1)
                        dve.wait_ge(od["iu"], s + 1)
                        dve.wait_ge(od["root"], s + 1)
                        DV.link(dve.tensor_tensor(II[x], II[x], RR[x], ALU.mult))
                        if d == 0:
                            dve.tensor_tensor_scan(HH[0], AA[x], II[x], 0.0, ALU.mult, ALU.add).then_inc(od["scan"], 1)
                        else:
                            back = lambda v, q: v[:, HALF * q:HALF * q + HALF][:, ::-1]
                            DV.link(dve.tensor_tensor_scan(back(HH[1], 0), back(AA[x], 0), back(II[x], 0), 0.0, ALU.mult, ALU.add))
                            dve.tensor_tensor_scan(back(HH[1], 1), back(AA[x], 1), back(II[x], 1), HH[1][:, 0:1], ALU.mult, ALU.add).then_inc(od["scan"], 1)
                            dve.wait_ge(od["scan"], s + 1)
                            DV.link(dve.tensor_tensor(HH[0][:, HALF:T], HH[0][:, HALF:T], HH[1][:, HALF:T], ALU.add))
                            DV.link(dve.tensor_tensor(M1[:, j, :], HH[0][:, HALF:T], GY[:, j, :], ALU.mult))
                            if j in AT:
                                sums(dve, slice(AT[j], AT[j] + 1))

        def pack_latent():
            with nc.Block() as block:
                @block.vector
                def _(dve):
                    for i in range(2):
                        for s in range(2):
                            DV.link(dve.tensor_copy(Xt[64 * s:64 * s + 64, i, :], Xt[64:128, 2 * i + s, :]))

        def store():
            stored = sem("stored")
            with nc.Block() as block:
                @block.sync
                def _(sp):
                    for i in range(2):
                        sp.dma_start(out[P * i:P * i + P, :], Xt[:, i, :]).then_inc(stored, 16)
                    sp.wait_ge(stored, 32)


        replicate()
        modulation(0, range(12))
        modulate("a0", 0, 1, NT, True, na_w[0] + SLOTS)
        for p in range(PAIRS):
            attention(p)
            hgrn(p)
        project_out("e0", evo, A[:, 12032:16128], 2, NT, plain_cols, len(chunks))
        residual_norm("e0", 0, 0, NT, H, None, 0)
        modulate("b0", 3, 4, NT, False, 0)
        moe(0, NT, T, 128)
        limit[0] = moe1_at
        residual_norm("f0", 0, 1, NT, Y, 5, 0, modulation_steps(1, range(4)))

        modulate("a1", 0, 1, NT, True, odi[0] + SLOTS, A[:, 8192:12288])
        recurrent_unit()
        modulation(1, range(9, 12))
        pack_latent()
        project_out("o1", odo, A[:, 12288:14336], 2, 2, lambda t, k, i: t[:, HALF * k + P * i:HALF * k + P * i + P], len(chunks))
        residual_norm("e1", 1, 0, 2, H, None, 0)
        modulate("b1", 3, 4, 2, False, 0)
        clear_moe()
        moe(1, 2, HALF, 64)
        residual_norm("f1", 1, 1, 2, Y, 5, 0)
        store()


def _constants(np):
    f = np.float32
    head = np.arange(P) // HD
    lev = np.zeros((2, NL, HD, CH), f)
    s, t = np.meshgrid(np.arange(CH), np.arange(CH), indexing="ij")
    for l, b in enumerate(LEVELS):
        same = (s // b) == (t // b)
        lev[0, l] = same & (s % b < b // 2) & (t % b >= b // 2)
        lev[1, l] = same & (s % b >= b // 2) & (t % b < b // 2)
    lev[:, NL - 1] = s == t
    lev = np.concatenate([lev, lev], 2).transpose(2, 0, 1, 3).reshape(P, -1)
    restart = np.tile((np.arange(T) % CH != 0).astype(f), (P, 1))
    w = np.arange(CH)
    lo = np.clip(w - 8, 0, CH - 16)[:, None]
    inside = (w[None] >= lo) & (w[None] < lo + 16)
    window = np.where(inside, 0.0, -1e30).astype(f)
    return {
        "k_ident": np.eye(P, dtype=f),
        "k_ones64": (head[:, None] == head[None]).astype(f) / HD,
        "k_levmask": np.ascontiguousarray(lev),
        "k_restart": restart,
        "k_iota": np.tile(np.arange(P, dtype=f), (P, 1)),
        "k_columns": np.stack([-np.arange(P), 1024 + np.arange(P), np.arange(P)], 1).astype(f),
        "k_order": np.concatenate([np.triu(np.ones((P, P)), 1),
                                   np.stack([c for i in range(NT) for c in (P * i + np.arange(P) - 1024, np.ones(P))], 1)], 1).astype(f),
        "k_window": np.concatenate([window, window]),
    }


def _bias_layout(rpb, np):
    w = np.arange(CH)
    at = np.clip(w[None, :] - w[:, None] + 15, 0, 30)
    band = rpb[:, :, at]
    first, second = band[:, 5:11], band[:, 4:10]
    both = np.concatenate([first.transpose(2, 0, 1, 3), second.transpose(2, 0, 1, 3)])
    return np.ascontiguousarray(both)


def _vectors(given, np):
    turn = lambda v: v.reshape(-1, P).T
    norm = np.concatenate([given["hg_norm_g"][0]] * 2)
    return np.ascontiguousarray(np.concatenate([turn(v) for v in (
        given["hg_lb_raw"], norm, given["od_conv_w"], given["od_conv_b"], given["lru_b_a"], given["lru_b_x"],
        given["lru_lam"])], 1))


_INS = ["x", "c", "ctx", "c_ctx", "ada_w", "ada_b", "ln_g", "ln_b", "ev_w_in", "ev_w_out", "od_w_in", "lru_w_a", "lru_w_x", "od_w_out",
        "router_w", "router_bias", "exp_w_gate", "exp_w_up", "exp_w_down", "sh_w_gate", "sh_w_up", "sh_w_down"]


def kernel(**inputs):
    import numpy as _np
    import concourse.bacc as _bacc
    from concourse.bass_utils import run_bass_kernel_spmd as _run

    nc = _bacc.Bacc("TRN2", target_bir_lowering=False, num_devices=1)
    arrays, args = {}, {}
    given = {n: _np.ascontiguousarray(inputs[n]) for n in _INS}
    given["rpb_band"] = _bias_layout(_np.asarray(inputs["na_rpb"])[0], _np)
    given["vectors"] = _vectors({n: _np.asarray(inputs[n]) for n in inputs}, _np)
    given.update(_constants(_np))
    for name, v in given.items():
        arrays["in_" + name] = v
        args[name] = nc.dram_tensor("in_" + name, v.shape, F32, kind="ExternalInput").ap()
    out = nc.dram_tensor("out", (HALF, D), F32, kind="ExternalOutput").ap()
    trunk(nc, args, out)
    r = _run(nc, [arrays], core_ids=[0])
    return r.results[0]["out"].reshape(1, HALF, D)
```
